# Optimizing a Trainium2 kernel written in Bass

```python
import jax, jax.numpy as jnp
from jax import lax
import numpy as np
import math

D_MODEL = 1024
BATCH = 1
SEQ = 256
DEPTH = 2

CHUNK = 64
EXPAND = 2
D_INNER = EXPAND * D_MODEL
POOL_WINDOWS = (2, 4, 8, 16)
N_POOL_GROUPS = len(POOL_WINDOWS)
POOL_GROUP = D_INNER // N_POOL_GROUPS
HGRN_HEAD_DIM = 128
HGRN_HEADS = D_INNER // HGRN_HEAD_DIM
N_MIXERS = 2
N_POOL_LAYERS = (DEPTH + 1) // 2
N_HGRN_LAYERS = DEPTH // 2
EPS = 1e-6


def rms_norm(x, g):
    xf = x.astype(jnp.float32)
    y = xf * lax.rsqrt(jnp.mean(xf * xf, axis=-1, keepdims=True) + EPS)
    return (y * g.astype(jnp.float32)).astype(x.dtype)

def multiscale_pool(v):
    T = v.shape[1]
    vf = v.astype(jnp.float32)
    cs = jnp.cumsum(vf, axis=1)
    pos = jnp.arange(T, dtype=jnp.float32)
    outs = []
    for g, w in enumerate(POOL_WINDOWS):
        lo, hi = g * POOL_GROUP, (g + 1) * POOL_GROUP
        c = cs[..., lo:hi]
        prev = jnp.pad(c[:, :-w], ((0, 0), (w, 0), (0, 0)))
        cnt = jnp.minimum(pos + 1.0, float(w))[None, :, None]
        outs.append((c - prev) / cnt - vf[..., lo:hi])
    return jnp.stack(outs, axis=2).astype(v.dtype)

def pool_mixer(h, w_in, w_grp, scale, w_out):
    B, T, _ = h.shape
    u = h @ w_in
    v, gate = jnp.split(u, 2, axis=-1)
    p = multiscale_pool(v)
    m = jnp.einsum('btgc,gcd->btgd', p, w_grp).reshape(B, T, D_INNER) * scale
    return (m * jax.nn.silu(gate)) @ w_out

def hgrn2_chunk_scan(q, k, v, b):
    _, Bn, H, C, dk = q.shape
    dv = v.shape[-1]
    causal = jnp.tril(jnp.ones((C, C), dtype=bool))

    def step(S, xs):
        qc, kc, vc, bc = xs
        diff = bc[:, :, :, None, :] - bc[:, :, None, :, :]
        diff = jnp.where(causal[None, None, :, :, None], diff, -jnp.inf)
        A = jnp.einsum('bhtd,bhsd,bhtsd->bhts', qc, kc, jnp.exp(diff))
        o = (jnp.einsum('bhts,bhsv->bhtv', A, vc)
             + jnp.einsum('bhtd,bhdv->bhtv', qc * jnp.exp(bc), S))
        b_last = bc[:, :, -1:, :]
        S = (jnp.exp(b_last[:, :, 0, :])[..., None] * S
             + jnp.einsum('bhsd,bhsv->bhdv', kc * jnp.exp(b_last - bc), vc))
        return S, o

    S0 = jnp.zeros((Bn, H, dk, dv), jnp.float32)
    _, o = lax.scan(step, S0, (q, k, v, b))
    return o

def hgrn2_mixer(h, w_in, lb, norm_g, w_out):
    B, T, _ = h.shape
    N = T // CHUNK
    u = h @ w_in
    q, fz, i, gate = jnp.split(u, 4, axis=-1)
    fz = fz.astype(jnp.float32)
    lbf = lb.astype(jnp.float32)
    log_f = jnp.logaddexp(jnp.log(lbf), jnp.log1p(-lbf) + jax.nn.log_sigmoid(fz))
    k = (1.0 - lbf) * jax.nn.sigmoid(-fz)

    def to_chunks(a):
        return a.astype(jnp.float32).reshape(B, N, CHUNK, HGRN_HEADS, HGRN_HEAD_DIM).transpose(1, 0, 3, 2, 4)

    qc, kc, vc, lfc = to_chunks(q), to_chunks(k), to_chunks(i), to_chunks(log_f)
    bc = jnp.cumsum(lfc, axis=3)
    o = hgrn2_chunk_scan(qc, kc, vc, bc)
    o = o.transpose(1, 0, 3, 2, 4).reshape(B, T, HGRN_HEADS, HGRN_HEAD_DIM)
    o = o * lax.rsqrt(jnp.mean(o * o, axis=-1, keepdims=True) + EPS)
    o = (o * norm_g.astype(jnp.float32).reshape(HGRN_HEADS, HGRN_HEAD_DIM)).reshape(B, T, D_INNER)
    o = o.astype(h.dtype)
    return (o * jax.nn.silu(gate)) @ w_out

def first_inputs(seed: int = 0) -> dict:
    key = jax.random.key(seed)
    ks = jax.random.split(key, 12)
    f32 = jnp.float32
    x = jax.random.normal(ks[0], (BATCH, SEQ, D_MODEL), f32)
    norm_g = 1.0 + 0.05 * jax.random.normal(ks[1], (DEPTH, D_MODEL), f32)
    pool_w_in = jax.random.normal(ks[2], (N_POOL_LAYERS, D_MODEL, 2 * D_INNER), f32) * D_MODEL ** -0.5
    pool_w_grp = jax.random.normal(ks[3], (N_POOL_LAYERS, N_POOL_GROUPS, POOL_GROUP, POOL_GROUP), f32) * POOL_GROUP ** -0.5
    pool_scale = 1.0 + 0.1 * jax.random.normal(ks[4], (N_POOL_LAYERS, D_INNER), f32)
    pool_w_out = jax.random.normal(ks[5], (N_POOL_LAYERS, D_INNER, D_MODEL), f32) * D_INNER ** -0.5
    hgrn_w_in = jax.random.normal(ks[6], (N_HGRN_LAYERS, D_MODEL, 4 * D_INNER), f32) * D_MODEL ** -0.5
    hgrn_lower_bounds = 0.5 * jax.random.normal(ks[7], (DEPTH, D_INNER), f32)
    hgrn_norm_g = 1.0 + 0.05 * jax.random.normal(ks[8], (N_HGRN_LAYERS, D_INNER), f32)
    hgrn_w_out = jax.random.normal(ks[9], (N_HGRN_LAYERS, D_INNER, D_MODEL), f32) * D_INNER ** -0.5
    final_g = 1.0 + 0.05 * jax.random.normal(ks[10], (D_MODEL,), f32)
    return {"x": x, "norm_g": norm_g, "pool_w_in": pool_w_in, "pool_w_grp": pool_w_grp,
            "pool_scale": pool_scale, "pool_w_out": pool_w_out, "hgrn_w_in": hgrn_w_in,
            "hgrn_lower_bounds": hgrn_lower_bounds, "hgrn_norm_g": hgrn_norm_g,
            "hgrn_w_out": hgrn_w_out, "final_g": final_g}

def first_block(x, norm_g, pool_w_in, pool_w_grp, pool_scale, pool_w_out, hgrn_w_in,
              hgrn_lower_bounds, hgrn_norm_g, hgrn_w_out, final_g):
    p = jax.nn.softmax(hgrn_lower_bounds.astype(jnp.float32), axis=0)
    lbs = jnp.cumsum(p, axis=0) - p[0:1]
    h = x
    for layer in range(DEPTH):
        hn = rms_norm(h, norm_g[layer])
        j = layer // N_MIXERS
        if layer % N_MIXERS == 0:
            y = pool_mixer(hn, pool_w_in[j], pool_w_grp[j], pool_scale[j], pool_w_out[j])
        else:
            y = hgrn2_mixer(hn, hgrn_w_in[j], lbs[layer], hgrn_norm_g[j], hgrn_w_out[j])
        h = h + y.astype(h.dtype)
    return rms_norm(h, final_g)


DEPTH_2 = 1

GRID_W = 64
CTX_LEN = 256
HEAD_DIM = 64
ATT_W = D_MODEL // 2
NA_HEADS = ATT_W // HEAD_DIM
NA_ROWS_MAX = 8
NA_COLS = 16
NA_QCOLS = 16
SG_W = D_MODEL // 4
SG_GROUPS = 4
SG_CHUNK = 128
CV_W = D_MODEL // 4
CV_GROUPS = 4
CV_KERNEL = 31
MIX_W = ATT_W + SG_W + CV_W
N_IN = 3 * ATT_W + 2 * SG_W + 2 * CV_W
D_FF = 256 * ((8 * D_MODEL // 3 + 255) // 256)
FFN_KERNEL = 3
NEG_INF = -1e30


def _rmsnorm(x, g):
    x32 = x.astype(jnp.float32)
    y = x32 * lax.rsqrt(jnp.mean(x32 * x32, axis=-1, keepdims=True) + EPS)
    return y.astype(x.dtype) * g

def _layernorm(x, g, b):
    x32 = x.astype(jnp.float32)
    mu = jnp.mean(x32, axis=-1, keepdims=True)
    var = jnp.mean(jnp.square(x32 - mu), axis=-1, keepdims=True)
    return ((x32 - mu) * lax.rsqrt(var + EPS)).astype(x.dtype) * g + b

def _group_layernorm(x, g, b, groups):
    shp = x.shape
    x32 = x.astype(jnp.float32).reshape(shp[:-1] + (groups, shp[-1] // groups))
    mu = jnp.mean(x32, axis=-1, keepdims=True)
    var = jnp.mean(jnp.square(x32 - mu), axis=-1, keepdims=True)
    y = ((x32 - mu) * lax.rsqrt(var + EPS)).reshape(shp).astype(x.dtype)
    return y * g + b

def _modulate(h, shift, scale):
    return h * (1 + scale) + shift

def _dwconv(x, w, b):
    k = w.shape[0]
    ch = x.shape[-1]
    y = lax.conv_general_dilated(
        x, w[:, None, :].astype(x.dtype), window_strides=(1,),
        padding=[((k - 1) // 2, k // 2)],
        dimension_numbers=("NWC", "WIO", "NWC"), feature_group_count=ch)
    return y + b

def _heads(t):
    bn, ln, _ = t.shape
    return t.reshape(bn, ln, NA_HEADS, HEAD_DIM).transpose(0, 2, 1, 3)

def _axis_span(length, win, qblk):
    span = min(qblk + win, length)
    start = np.clip(np.arange(length) - win // 2, 0, length - win)
    a = np.clip(np.arange(0, length, qblk) - win // 2, 0, length - span)
    qpos = np.arange(length).reshape(-1, qblk)
    kpos = a[:, None] + np.arange(span)[None, :]
    s_q = start[qpos][:, :, None]
    inwin = (kpos[:, None, :] >= s_q) & (kpos[:, None, :] < s_q + win)
    off = kpos[:, None, :] - qpos[:, :, None]
    return kpos, inwin, off

def _na_index(rows):
    win_r = min(NA_ROWS_MAX, rows)
    qr = next(q for q in (8, 4, 2, 1) if rows % q == 0)
    kr, mr, dr = _axis_span(rows, win_r, qr)
    kc, mc, dc = _axis_span(GRID_W, NA_COLS, NA_QCOLS)
    nbr, nbc = kr.shape[0], kc.shape[0]
    nq = qr * NA_QCOLS
    key_idx = (kr[:, None, :, None] * GRID_W + kc[None, :, None, :]).reshape(nbr * nbc, -1)
    mask = (mr[:, None, :, None, :, None] & mc[None, :, None, :, None, :]).reshape(nbr * nbc, nq, -1)
    ridx = np.clip(dr + NA_ROWS_MAX - 1, 0, 2 * NA_ROWS_MAX - 2)
    cidx = np.clip(dc + NA_COLS - 1, 0, 2 * NA_COLS - 2)
    bias_idx = (ridx[:, None, :, None, :, None] * (2 * NA_COLS - 1)
                + cidx[None, :, None, :, None, :]).reshape(nbr * nbc, nq, -1)
    return qr, key_idx.astype(np.int32), mask, bias_idx.astype(np.int32)

def _neighbourhood_attention(q, k, v, k_ctx, v_ctx, rpb, rows):
    bn, nh, sl, dh = q.shape
    qr, key_idx, mask, bias_idx = _na_index(rows)
    nbr, nbc = rows // qr, GRID_W // NA_QCOLS
    span = key_idx.shape[-1]
    qb = q.reshape(bn, nh, nbr, qr, nbc, NA_QCOLS, dh).transpose(2, 4, 0, 1, 3, 5, 6)
    qb = qb.reshape(nbr * nbc, bn, nh, qr * NA_QCOLS, dh)
    rpb_flat = rpb.reshape(nh, -1)
    scale = dh ** -0.5

    def block(args):
        qblk, kidx, m, bidx = args
        kb = jnp.take(k, kidx, axis=2)
        vb = jnp.take(v, kidx, axis=2)
        s_loc = jnp.einsum("bhqd,bhkd->bhqk", qblk, kb).astype(jnp.float32) * scale
        s_loc = s_loc + jnp.take(rpb_flat, bidx, axis=1).astype(jnp.float32)[None]
        s_loc = jnp.where(m[None, None], s_loc, NEG_INF)
        s_ctx = jnp.einsum("bhqd,bhkd->bhqk", qblk, k_ctx).astype(jnp.float32) * scale
        p = jax.nn.softmax(jnp.concatenate([s_loc, s_ctx], axis=-1), axis=-1).astype(v.dtype)
        return (jnp.einsum("bhqk,bhkd->bhqd", p[..., :span], vb)
                + jnp.einsum("bhqk,bhkd->bhqd", p[..., span:], v_ctx))

    out = lax.map(block, (qb, jnp.asarray(key_idx), jnp.asarray(mask), jnp.asarray(bias_idx)))
    out = out.reshape(nbr, nbc, bn, nh, qr, NA_QCOLS, dh).transpose(2, 0, 4, 1, 5, 3, 6)
    return out.reshape(bn, sl, nh * dh)

def _context_attention(q, k, v):
    s = jnp.einsum("bhqd,bhkd->bhqk", q, k).astype(jnp.float32) * (q.shape[-1] ** -0.5)
    p = jax.nn.softmax(s, axis=-1).astype(v.dtype)
    o = jnp.einsum("bhqk,bhkd->bhqd", p, v)
    bn, nh, ln, dh = o.shape
    return o.transpose(0, 2, 1, 3).reshape(bn, ln, nh * dh)

def _spatial_gating(u, v, ln_g, ln_b, w_s, b_s):
    u = jax.nn.gelu(u)
    v = _layernorm(jax.nn.gelu(v), ln_g, ln_b)
    bn, ln, ch = v.shape
    vr = v.reshape(bn, ln // SG_CHUNK, SG_CHUNK, SG_GROUPS, ch // SG_GROUPS)
    mixed = jnp.einsum("gpq,bnqgc->bnpgc", w_s, vr) + b_s.T[None, None, :, :, None]
    return u * mixed.reshape(bn, ln, ch)

def _conformer_conv(a, gate, w, b, ng, nb):
    h = a * jax.nn.sigmoid(gate)
    h = _dwconv(h, w, b)
    h = _group_layernorm(h, ng, nb, CV_GROUPS)
    return jax.nn.silu(h)

def _mix_out(att, z, sg_ng, sg_nb, sg_w, sg_b, cv_w, cv_b, cv_ng, cv_nb, w_out):
    o1 = 3 * ATT_W
    o2 = o1 + 2 * SG_W
    sg = _spatial_gating(z[..., o1:o1 + SG_W], z[..., o1 + SG_W:o2], sg_ng, sg_nb, sg_w, sg_b)
    cv = _conformer_conv(z[..., o2:o2 + CV_W], z[..., o2 + CV_W:o2 + 2 * CV_W],
                         cv_w, cv_b, cv_ng, cv_nb)
    return jnp.concatenate([att, sg, cv], axis=-1) @ w_out

def _conv_ffn(h, w_up, conv_w, conv_b, w_down):
    gate, up = jnp.split(h @ w_up, 2, axis=-1)
    gate = _dwconv(gate, conv_w, conv_b)
    return (jax.nn.silu(gate) * up) @ w_down

def second_inputs(seed: int = 0) -> dict:
    key = jax.random.key(seed)
    ks = jax.random.split(key, 24)
    D = D_MODEL

    def n(k, shape, s):
        return jax.random.normal(k, shape, jnp.float32) * s

    return {
        "x": n(ks[0], (BATCH, SEQ, D), 1.0),
        "c": n(ks[1], (BATCH, D), 1.0),
        "ctx": n(ks[2], (BATCH, CTX_LEN, D), 1.0),
        "c_ctx": n(ks[3], (D,), 1.0),
        "ada_w": n(ks[4], (DEPTH_2, D, 6 * D), 0.5 * D ** -0.5),
        "ada_b": n(ks[5], (DEPTH_2, 6 * D), 0.02),
        "norm1_g": 1.0 + n(ks[6], (DEPTH_2, D), 0.05),
        "w_in": n(ks[7], (DEPTH_2, D, N_IN), D ** -0.5),
        "na_rpb": n(ks[8], (DEPTH_2, NA_HEADS, 2 * NA_ROWS_MAX - 1, 2 * NA_COLS - 1), 0.5),
        "sg_norm_g": 1.0 + n(ks[9], (DEPTH_2, SG_W), 0.05),
        "sg_norm_b": n(ks[10], (DEPTH_2, SG_W), 0.02),
        "sg_w": n(ks[11], (DEPTH_2, SG_GROUPS, SG_CHUNK, SG_CHUNK), SG_CHUNK ** -0.5),
        "sg_b": 1.0 + n(ks[12], (DEPTH_2, SG_GROUPS, SG_CHUNK), 0.1),
        "cv_w": n(ks[13], (DEPTH_2, CV_KERNEL, CV_W), CV_KERNEL ** -0.5),
        "cv_b": n(ks[14], (DEPTH_2, CV_W), 0.02),
        "cv_norm_g": 1.0 + n(ks[15], (DEPTH_2, CV_W), 0.05),
        "cv_norm_b": n(ks[16], (DEPTH_2, CV_W), 0.02),
        "w_out": n(ks[17], (DEPTH_2, MIX_W, D), MIX_W ** -0.5),
        "norm2_g": 1.0 + n(ks[18], (DEPTH_2, D), 0.05),
        "ffn_w_up": n(ks[19], (DEPTH_2, D, 2 * D_FF), D ** -0.5),
        "ffn_conv_w": n(ks[20], (DEPTH_2, FFN_KERNEL, D_FF), FFN_KERNEL ** -0.5),
        "ffn_conv_b": n(ks[21], (DEPTH_2, D_FF), 0.02),
        "ffn_w_down": n(ks[22], (DEPTH_2, D_FF, D), D_FF ** -0.5),
        "final_norm_g": 1.0 + n(ks[23], (D,), 0.05),
    }

def second_block(x, c, ctx, c_ctx, ada_w, ada_b, norm1_g, w_in, na_rpb, sg_norm_g, sg_norm_b,
              sg_w, sg_b, cv_w, cv_b, cv_norm_g, cv_norm_b, w_out, norm2_g, ffn_w_up,
              ffn_conv_w, ffn_conv_b, ffn_w_down, final_norm_g):
    rows = x.shape[1] // GRID_W
    xc = ctx
    for l in range(DEPTH_2):
        last = l == DEPTH_2 - 1
        mod_l = jnp.split((jax.nn.silu(c) @ ada_w[l] + ada_b[l])[:, None, :], 6, axis=-1)
        mod_c = jnp.split((jax.nn.silu(c_ctx) @ ada_w[l] + ada_b[l])[None, None, :], 6, axis=-1)

        h = _modulate(_rmsnorm(x, norm1_g[l]), mod_l[0], mod_l[1])
        hc = _modulate(_rmsnorm(xc, norm1_g[l]), mod_c[0], mod_c[1])
        z = h @ w_in[l]
        q = _heads(z[..., :ATT_W])
        k = _heads(z[..., ATT_W:2 * ATT_W])
        v = _heads(z[..., 2 * ATT_W:3 * ATT_W])
        if last:
            kvc = hc @ w_in[l][:, ATT_W:3 * ATT_W]
            kc = _heads(kvc[..., :ATT_W])
            vc = _heads(kvc[..., ATT_W:])
        else:
            zc = hc @ w_in[l]
            kc = _heads(zc[..., ATT_W:2 * ATT_W])
            vc = _heads(zc[..., 2 * ATT_W:3 * ATT_W])
        att = _neighbourhood_attention(q, k, v, kc, vc, na_rpb[l], rows)
        y = _mix_out(att, z, sg_norm_g[l], sg_norm_b[l], sg_w[l], sg_b[l], cv_w[l], cv_b[l],
                     cv_norm_g[l], cv_norm_b[l], w_out[l])
        x = x + mod_l[2] * y
        if not last:
            att_c = _context_attention(_heads(zc[..., :ATT_W]), kc, vc)
            yc = _mix_out(att_c, zc, sg_norm_g[l], sg_norm_b[l], sg_w[l], sg_b[l], cv_w[l],
                          cv_b[l], cv_norm_g[l], cv_norm_b[l], w_out[l])
            xc = xc + mod_c[2] * yc

        h2 = _modulate(_rmsnorm(x, norm2_g[l]), mod_l[3], mod_l[4])
        x = x + mod_l[5] * _conv_ffn(h2, ffn_w_up[l], ffn_conv_w[l], ffn_conv_b[l], ffn_w_down[l])
        if not last:
            h2c = _modulate(_rmsnorm(xc, norm2_g[l]), mod_c[3], mod_c[4])
            xc = xc + mod_c[5] * _conv_ffn(h2c, ffn_w_up[l], ffn_conv_w[l], ffn_conv_b[l],
                                           ffn_w_down[l])
    return _rmsnorm(x, final_norm_g)


def setup_inputs(seed=0):
    out = dict(first_inputs(seed))
    for name, value in second_inputs(seed + 1).items():
        if name != "x":
            out[name + "_2"] = value
    return out


def reference(
    x, norm_g, pool_w_in, pool_w_grp, pool_scale, pool_w_out, hgrn_w_in, hgrn_lower_bounds,
    hgrn_norm_g, hgrn_w_out, final_g, c_2, ctx_2, c_ctx_2, ada_w_2, ada_b_2, norm1_g_2, w_in_2,
    na_rpb_2, sg_norm_g_2, sg_norm_b_2, sg_w_2, sg_b_2, cv_w_2, cv_b_2, cv_norm_g_2,
    cv_norm_b_2, w_out_2, norm2_g_2, ffn_w_up_2, ffn_conv_w_2, ffn_conv_b_2, ffn_w_down_2,
    final_norm_g_2,
):
    x = first_block(
        x, norm_g, pool_w_in, pool_w_grp, pool_scale, pool_w_out, hgrn_w_in, hgrn_lower_bounds,
        hgrn_norm_g, hgrn_w_out, final_g,
    )
    return second_block(
        x, c_2, ctx_2, c_ctx_2, ada_w_2, ada_b_2, norm1_g_2, w_in_2, na_rpb_2, sg_norm_g_2,
        sg_norm_b_2, sg_w_2, sg_b_2, cv_w_2, cv_b_2, cv_norm_g_2, cv_norm_b_2, w_out_2,
        norm2_g_2, ffn_w_up_2, ffn_conv_w_2, ffn_conv_b_2, ffn_w_down_2, final_norm_g_2,
    )


_drawn_inputs = setup_inputs


def setup_inputs(seed=0):
    import zlib

    import numpy as np

    out = dict(_drawn_inputs(seed))
    spreads = {}
    factors = {'norm1_g_2': 5.311,
     'na_rpb_2': 8.0,
     'sg_norm_g_2': 8.0,
     'sg_norm_b_2': 24.314,
     'sg_b_2': 4.881,
     'cv_b_2': 64.0,
     'cv_norm_g_2': 57.764,
     'cv_norm_b_2': 180.524,
     'norm2_g_2': 3.556,
     'ffn_conv_b_2': 23.274}
    for name, (base, spread) in spreads.items():
        noise = np.random.default_rng([zlib.crc32(name.encode()), seed]).standard_normal(out[name].shape)
        drawn = base * np.exp(spread * noise) if base else spread * noise
        out[name] = __import__('jax').numpy.asarray(drawn.astype(out[name].dtype))
    for name, factor in factors.items():
        out[name] = (out[name] * factor).astype(out[name].dtype)
    return out
```

```python
from contextlib import ExitStack, contextmanager

import concourse.bass as bass
from concourse import mybir

P = 128
TOK = 256
D = 1024
KD = D // P
INNER = 2048
KI = INNER // P
HEADS = KI
ATT = 512
NA_HEADS = 8
DFF = 2816
KF = DFF // P
GRID = 64
TAPS = 31
SLAB = 4096
EPS = 1e-6
LEVELS = 8

F32 = mybir.dt.float32
F32R = mybir.dt.float32r
U8 = mybir.dt.uint8
I32 = mybir.dt.int32
ALU = mybir.AluOpType
ACT = mybir.ActivationFunctionType
AX_X = mybir.AxisListType.X
PE_, ACT_, DVE_, POOL_, SP_ = "PE", "ACT", "DVE", "POOL", "SP"


class Signal:

    def __init__(self, nc, stack, name):
        self.sem = stack.enter_context(nc.semaphore(name))
        self.count = 0
        self.offset = 0
        self.all = None

    def on(self, instruction, k=1):
        instruction.then_inc(self.sem, k)
        self.count += k
        return (self.sem, self.offset + self.count)


def build(nc, h, out):
    stack = ExitStack()
    with stack:
        _build(nc, h, out, stack)


def _build(nc, h, out, stack):
    pe, act, dve, pool, sp = nc.tensor, nc.scalar, nc.vector, nc.gpsimd, nc.sync
    stack.enter_context(nc.allow_non_contiguous_dma(reason="short rows of parameters"))

    base = (nc.sbuf_base + 63) // 64 * 64
    top = [base]

    def at(offset, name, shape, dt=F32):
        return nc.alloc_sbuf_tensor_at(name, [P] + shape, dt, offset=offset)

    def size(shape, dt):
        n = 1
        for x in shape:
            n *= x
        return (n * (1 if dt == U8 else 4) + 31) // 32 * 32

    def fixed(name, shape, dt=F32):
        t = at(top[0], name, shape, dt)
        top[0] += size(shape, dt)
        return t

    class Region:

        def __init__(self, nbytes):
            self.start, self.end = top[0], top[0] + nbytes
            top[0] = self.end
            assert self.end <= nc.sbuf_usable_end, (self.end, nc.sbuf_usable_end)
            self.next = self.start

        def restart(self, skip=0):
            self.next = self.start + skip

        def new(self, name, shape, dt=F32):
            t = at(self.next, name, shape, dt)
            self.next += size(shape, dt)
            assert self.next <= self.end, (name, self.next - self.end)
            return t

    raw = [fixed(f"raw{j}", [SLAB]) for j in range(2)]
    w_hi = [fixed(f"w_hi{j}", [SLAB], F32R) for j in range(2)]
    w_lo = [fixed(f"w_lo{j}", [SLAB], F32R) for j in range(2)]
    XT = fixed("XT", [KD, TOK])
    XH = fixed("XH", [KD, TOK], F32R)
    XL = fixed("XL", [KD, TOK], F32R)
    ident = fixed("ident", [P])
    ones = fixed("ones", [P])
    block64 = fixed("block64", [P])
    sel8 = fixed("sel8", [15])
    table = [fixed(f"table{n}", [w]) for n, w in enumerate((128, 116, 88))]
    mod = fixed("mod", [48])
    mod_ctx = fixed("mod_ctx", [16])
    silu_c = fixed("silu_c", [16])
    lb = fixed("lb", [4, KI])
    gain = fixed("gain", [4, KD])
    mask_diag = fixed("mask_diag", [P], U8)
    mask_level = fixed("mask_level", [7, 64], U8)
    rstd = fixed("rstd", [2, TOK])
    stats = fixed("stats", [2, 8])
    soft = fixed("soft", [2, 4])
    rM = Region(2 * KF * TOK * 4)
    rR = Region(nc.sbuf_usable_end - top[0])

    acc = [stack.enter_context(nc.psum_tensor(f"acc{b}", [P, 512], F32)) for b in range(4)]
    misc = [stack.enter_context(nc.psum_tensor(f"misc{b}", [P, 512], F32)) for b in range(4)]

    def sig(name):
        return Signal(nc, stack, name)

    raw_in = [sig(f"raw_in{j}") for j in range(2)]
    hi_done = sig("hi_done")
    lo_done = sig("lo_done")
    lo_pool = sig("lo_pool")
    tile_done = sig("tile_done")
    acc_free = [sig(f"acc_free{b}") for b in range(4)]
    V, A, G, T = (sig(n) for n in ("vector_step", "scalar_step", "pool_step", "tensor_step"))
    step_of = {V: dve, A: act, G: pool, T: pe}
    chains = (V, A, G, T)

    def wait(eng, *tokens):
        for t in tokens:
            if t is not None:
                eng.wait_ge(t[0], t[1])

    def v(f, *after, **k):
        wait(dve, *after)
        return V.on(f())

    def a(f, *after):
        wait(act, *after)
        return A.on(f())

    def g(f, *after):
        wait(pool, *after)
        return G.on(f())

    def latest(chain):
        return (chain.sem, chain.offset + chain.count)

    @contextmanager
    def loop(passes, **per):
        each = [per.get(n, 0) for n in "VAGT"]
        before = [c.count for c in chains]
        with nc.Fori(0, passes) as i:
            for c, n, k in zip(chains, each, before):
                c.offset, c.count = i * n + k, 0
            yield i
            got = [c.count for c in chains]
        for c, n, k in zip(chains, each, before):
            c.offset, c.count = 0, k + n * passes
        assert got == each, f"steps counted in a pass: {got}, stated: {each}"

    def earlier(token, steps):
        return (token[0], token[1] - steps)

    def view(t, offset, *dims):
        whole = t[:, :] if len(t.shape) == 2 else t[:, :, :]
        return bass.AP(whole.tensor, offset, [list(whole.ap[0])] + [list(d) for d in dims])

    def load(pair, j, src, first=False):
        if not first:
            for done in (lo_done, lo_pool):
                sp.wait_ge(done.sem, 2 * pair + j + 1)
        parts = src if isinstance(src, list) else [src]
        k, n = parts[0].shape[1:]
        dst = raw[j][:, 0:k * n * len(parts)].rearrange("p (k m n) -> p k m n", k=k, m=len(parts))
        for m, part in enumerate(parts):
            sp.dma_start(dst[:, :, m, :], part).then_inc(raw_in[j].sem, 64 // len(parts))

    def split(pair, j, tiles_before, width=SLAB):
        act.wait_ge(raw_in[j].sem, 64 * pair + 64)
        if tiles_before is not None:
            act.wait_ge(tile_done.sem, tiles_before)
        half, part = width // 2, width // 8 * 3
        for c in (slice(0, half), slice(half, width)):
            act.activation(w_hi[j][:, c], raw[j][:, c], ACT.Copy).then_inc(hi_done.sem, 1)
        for eng, halves_done, c, done in ((pool, 1, slice(0, part), lo_pool), (dve, 2, slice(part, width), lo_done)):
            eng.wait_ge(hi_done.sem, 4 * pair + 2 * j + halves_done)
            eng.tensor_tensor(w_lo[j][:, c], raw[j][:, c], w_hi[j][:, c].bitcast(F32),
                              ALU.subtract).then_inc(done.sem, 1)

    def weights(j, k, skip=0, n=None):
        n = SLAB // k if n is None else n
        return [w[j][:, 0:n * k].rearrange("p (k n) -> p k n", k=k) for w in (w_hi, w_lo)]

    def slab_ready(pair, j):
        for done in (lo_done, lo_pool):
            pe.wait_ge(done.sem, 2 * pair + j + 3)

    def project(q, b, w, cols, X, K):
        pe.wait_ge(acc_free[b].sem, q + 1)
        (wh, wl), (xh, xl) = w, X
        o = acc[b][:, 0:TOK]
        for k in range(K):
            pe.matmul(o, wh[:, k, cols:cols + P], xh[:, k, :], start=k == 0, stop=False)
            pe.matmul(o, wh[:, k, cols:cols + P], xl[:, k, :], start=False, stop=False)
            m = pe.matmul(o, wl[:, k, cols:cols + P], xh[:, k, :], start=False, stop=k == K - 1)
        m.then_inc(tile_done.sem, 1)

    def project_tokens(q, b, w, cols, width, X, K, half, at_col=0, first=True, last=True):
        if first:
            pe.wait_ge(acc_free[b].sem, q + 1)
        (wh, wl), (xh, xl) = w, X
        o = acc[b][:, at_col:at_col + width]
        ts = slice(half * P, half * P + P)
        for k in range(K):
            pe.matmul(o, xh[:, k, ts], wh[:, k, cols:cols + width], start=k == 0, stop=False)
            pe.matmul(o, xh[:, k, ts], wl[:, k, cols:cols + width], start=False, stop=False)
            m = pe.matmul(o, xl[:, k, ts], wh[:, k, cols:cols + width], start=False, stop=k == K - 1)
        if last:
            m.then_inc(tile_done.sem, 1)

    def complete(eng, q, b):
        eng.wait_ge(tile_done.sem, 4 * q + b + 1)

    def freed(q, b, instruction):
        instruction.then_inc(acc_free[b].sem, 1)
        return (acc_free[b].sem, q + 2)

    def rows(w, k):
        return w.rearrange("(k p) n -> p k n", k=k)

    w_pool_in = rows(h["pool_w_in"][0], KD)
    w_grp = h["pool_w_grp"][0]
    w_pool_out = rows(h["pool_w_out"][0], KI)
    w_hgrn_in = rows(h["hgrn_w_in"][0], KD)
    w_hgrn_out = rows(h["hgrn_w_out"][0], KI)
    w_in2 = rows(h["w_in_2"][0], KD)
    w_out2 = rows(h["w_out_2"][0], KD)
    w_up = rows(h["ffn_w_up_2"][0], KD)
    w_down = rows(h["ffn_w_down_2"][0], KF)
    w_ada = rows(h["ada_w_2"][0], KD)

    def pool_in(grp, gate):
        return w_pool_in[:, :, bass.ds(grp * 512 + gate * INNER, 512)]

    def pool_grp(grp):
        return w_grp[bass.ds(grp, 1)].rearrange("a (k p) n -> p (a k) n", k=4)

    def out_slab(w, n):
        return w[:, :, bass.ds(n * 256, 256)]

    def head_slab(n):
        return [w_hgrn_in[:, :, bass.ds(n * P + m * INNER, P)] for m in range(4)]

    def up_slab(n):
        return [w_up[:, :, bass.ds(n * 256 + m * DFF, 256)] for m in range(2)]

    def down_slab(n):
        return w_down[:, :, bass.ds(n * P, P)]

    s_x, s_par, s_ctx, s_row, s_pad, s_bias, s_scr = (sig(n) for n in (
        "x_in", "parameters_in", "context_in", "rows_in", "padded_in", "bias_in", "scratch_out"))
    s_ada = [sig(f"ada_in{n}") for n in range(2)]

    rM.restart()
    x_tok = rM.new("x_tok", [2, D])
    par = [rM.new(f"par{n}", [P]) for n in range(3)]
    rR.restart()
    band = rR.new("band", [4, 384])
    iota_i = rM.new("iota_i", [TOK], I32)
    iota_f = rM.new("iota_f", [TOK])
    inverse = rM.new("inverse", [TOK])
    mask_f = rM.new("mask_f", [7, 64])
    SQ = rM.new("SQ", [KD, TOK])
    XN = rM.new("XN", [KD, TOK])

    sp.dma_start(x_tok[:, :, :], h["x"][0].rearrange("(a p) n -> p a n", a=2)).then_inc(s_x.sem, 16)
    place = {}
    n_par = 0
    for n, names in enumerate((
            ("norm_g", "pool_scale", "hgrn_lower_bounds", "hgrn_norm_g", "final_g", "c_2", "c_ctx_2",
             "norm1_g_2", "norm2_g_2", "final_norm_g_2"),
            ("ada_b_2", "cv_w_2", "cv_b_2", "cv_norm_g_2", "cv_norm_b_2"),
            ("ffn_conv_w_2", "ffn_conv_b_2"))):
        r = 0
        for name in names:
            src = h[name]
            s = src.shape
            flat = {1: "(r c) -> r c", 2: "a (r c) -> (a r) c", 3: "a b (r c) -> (a b r) c"}[len(s)]
            src = src.rearrange(flat, c=P)
            k = src.shape[0]
            if n_par >= 0:
                sp.dma_start(par[n][r:r + k, :], src).then_inc(s_par.sem, 16)
            n_par += 1
            place[name] = (n, r, k)
            r += k

    def param(name, i=0, n=1):
        t, r, k = place[name]
        if isinstance(i, int):
            return table[t][:, r + i:r + i + n]
        return table[t][:, bass.ds(i + r, n)]

    one = g(lambda: pool.memset(ident[:, :], 0.0))
    ident_ok = g(lambda: pool.affine_select(out=ident[:, :], in_=ident[:, :], compare_op=ALU.not_equal, fill=1.0,
                                            base=0, pattern=[[-1, P]], channel_multiplier=1), one)
    ones_ok = v(lambda: dve.memset(ones[:, :], 1.0))
    v(lambda: dve.memset(block64[:, :], 0.0))
    z = v(lambda: dve.memset(sel8[:, :], 0.0))
    v(lambda: dve.memset(block64[0:64, 0:64], 1.0), z)
    v(lambda: dve.memset(block64[64:P, 64:P], 1.0))
    sel_ok = v(lambda: dve.memset(sel8[:, 7:8], 1.0))
    for b in range(4):
        dve.sem_inc(acc_free[b].sem, 1)
    dve.sem_inc(lo_done.sem, 2)
    pool.sem_inc(lo_pool.sem, 2)

    m1 = g(lambda: pool.memset(mask_f[:, :, :], 1.0))
    for l in range(7):
        B = 1 << l
        mk = mask_f[:, l, :].rearrange("p (n b) -> p n b", b=B)
        t1 = g(lambda: pool.affine_select(out=mk, in_=mk, compare_op=ALU.is_ge, fill=0.0, base=0,
                                          pattern=[[-2 * B, 64 // B], [0, B]], channel_multiplier=1), m1)
        mask_ok = g(lambda: pool.affine_select(out=mk, in_=mk, compare_op=ALU.is_ge, fill=0.0, base=B - 1,
                                               pattern=[[2 * B, 64 // B], [0, B]], channel_multiplier=-1), t1)
    i1 = g(lambda: pool.iota(iota_i[:, :], pattern=[[1, TOK]], base=1, channel_multiplier=0))
    b1 = g(lambda: pool.memset(band[:, :, :], 1.0))
    for n in range(4):
        w = 2 << n
        for half, (c0, c1) in enumerate(((0, 256), (256, 384))):
            bb = band[:, n, c0:c1]
            b2 = g(lambda: pool.affine_select(out=bb, in_=bb, compare_op=ALU.is_ge, fill=0.0, base=0,
                                              pattern=[[1, c1 - c0]], channel_multiplier=-1), b1)
            b3 = g(lambda: pool.affine_select(out=bb, in_=bb, compare_op=ALU.is_ge, fill=0.0, base=w - 1,
                                              pattern=[[-1, c1 - c0]], channel_multiplier=1), b2)
    f1 = v(lambda: dve.tensor_copy(iota_f[:, :], iota_i[:, :]), i1, b3, mask_ok)
    v(lambda: dve.tensor_copy(mask_level[:, :, :], mask_f[:, :, :]))
    mask2_ok = v(lambda: dve.tensor_copy(mask_diag[:, :], ident[:, :]), ident_ok)
    for n in range(4):
        w = 2 << n
        f2 = v(lambda: dve.tensor_scalar(inverse[:, :], iota_f[:, :], float(w), None, ALU.min), f1)
        f3 = v(lambda: dve.reciprocal(inverse[:, :], inverse[:, :]), f2)
        v(lambda: dve.tensor_tensor(band[:, n, 0:256], band[:, n, 0:256], inverse[:, :], ALU.mult), f3)
        f1 = v(lambda: dve.tensor_tensor(band[:, n, 256:384], band[:, n, 256:384], inverse[:, P:TOK], ALU.mult))
        for c in (0, 256):
            f1 = v(lambda: dve.tensor_tensor(band[:, n, c:c + P], band[:, n, c:c + P], ident[:, :], ALU.subtract), f1)
    band_ok = f1

    pe.wait_ge(s_par.sem, 16 * n_par)
    wait(pe, ident_ok)
    for n, wdt in enumerate((128, 116, 88)):
        m = pe.transpose(misc[3][:, n * P:n * P + wdt], par[n][0:wdt, :], ident[0:wdt, 0:wdt])
    par_t = T.on(m)
    for n, wdt in enumerate((128, 116, 88)):
        par_ok = v(lambda: dve.tensor_copy(table[n][:, :], misc[3][:, n * P:n * P + wdt]), par_t)

    def turn_in(src, dst, arrived, frees):
        wait(pe, arrived, *frees)
        done = []
        for n, (half, kq) in enumerate(((0, 0), (0, 4), (1, 0), (1, 4))):
            for k in range(4):
                m = pe.transpose(misc[n][:, k * P:k * P + P],
                                 src[:, half, (kq + k) * P:(kq + k + 1) * P], ident[:, :])
            t = T.on(m)
            done.append(v(lambda: dve.tensor_copy(
                dst[:, kq:kq + 4, half * P:half * P + P],
                misc[n][:, :].rearrange("p (k t) -> p k t", k=4)), t))
        return done[-1]

    x_ok = turn_in(x_tok, XT, (s_x.sem, 16), (par_ok,))

    r0 = param("hgrn_lower_bounds", 0, KI)
    r1 = param("hgrn_lower_bounds", KI, KI)
    t = v(lambda: dve.tensor_tensor(lb[:, 2, :], r0, r1, ALU.max), par_ok)
    v(lambda: dve.tensor_tensor(lb[:, 0, :], r0, lb[:, 2, :], ALU.subtract), t)
    t = v(lambda: dve.tensor_tensor(lb[:, 1, :], r1, lb[:, 2, :], ALU.subtract))
    t = a(lambda: act.activation(lb[:, 0:2, :], lb[:, 0:2, :], ACT.Exp, bias=0.0), t)
    t = v(lambda: dve.tensor_tensor(lb[:, 2, :], lb[:, 0, :], lb[:, 1, :], ALU.add), t)
    t = v(lambda: dve.reciprocal(lb[:, 2, :], lb[:, 2, :]), t)
    v(lambda: dve.tensor_tensor(lb[:, 3, :], lb[:, 0, :], lb[:, 2, :], ALU.mult), t)
    t = v(lambda: dve.tensor_tensor(lb[:, 1, :], lb[:, 1, :], lb[:, 2, :], ALU.mult), t)
    t = v(lambda: dve.tensor_tensor(lb[:, 0, :], lb[:, 3, :], lb[:, 1, :], ALU.add), t)
    t = v(lambda: dve.tensor_tensor(lb[:, 0, :], lb[:, 0, :], lb[:, 3, :], ALU.subtract), t)
    lb_ok = v(lambda: dve.tensor_scalar(lb[:, 1, :], lb[:, 0, :], -1.0, 1.0, ALU.mult, ALU.add), t)
    silu_ok = a(lambda: act.activation(silu_c[:, :], param("c_2", 0, 16), ACT.Silu, bias=0.0), par_ok)

    def rms(X, sq, xn, ready, bank, free):
        t = a(lambda: act.activation(sq[:, :, :], X[:, :, :], ACT.Square, bias=0.0), ready)
        wait(pe, t, free, ones_ok)
        for k in range(KD):
            m = pe.matmul(misc[bank][:, 0:TOK], ones[:, :], sq[:, k, :], start=k == 0, stop=k == KD - 1)
        t = T.on(m)
        t = v(lambda: dve.tensor_scalar(rstd[:, 0, :], misc[bank][:, 0:TOK], 1.0 / D, EPS, ALU.mult, ALU.add), t)
        t = a(lambda: act.activation(rstd[:, 1, :], rstd[:, 0, :], ACT.Sqrt, bias=0.0), t)
        t = v(lambda: dve.reciprocal(rstd[:, 0, :], rstd[:, 1, :]), t)
        r = view(rstd, 0, (0, KD), (1, TOK))
        return v(lambda: dve.tensor_tensor(xn[:, :, :], X[:, :, :], r, ALU.mult), t)

    def halves(src, hi, lo, k, ready, scale=None, shift=None):
        if scale is not None:
            if shift is None:
                ready = v(lambda: dve.tensor_scalar(src[:, k, :], src[:, k, :], scale, None, ALU.mult), ready)
            else:
                ready = v(lambda: dve.tensor_scalar(src[:, k, :], src[:, k, :], scale, shift, ALU.mult, ALU.add), ready)
        t = a(lambda: act.activation(hi[:, k, :], src[:, k, :], ACT.Copy), ready)
        return v(lambda: dve.tensor_tensor(lo[:, k, :], src[:, k, :], hi[:, k, :].bitcast(F32), ALU.subtract), t)

    t = rms(XT, SQ, XN, x_ok, 0, x_ok)
    for k in range(KD):
        xn_ok = halves(XN, XH, XL, k, t, param("norm_g", k))
    ada_raw = [rR.new(f"ada_raw{n}", [4, 512]) for n in range(2)]
    ada_acc = rR.new("ada_acc", [2, 512])
    p_hi = rR.new("p_hi", [4, TOK], F32R)
    p_lo = rR.new("p_lo", [4, TOK], F32R)
    v_tok = at(rM.start + (KF + KI) * TOK * 4, "v_tok", [2, 512])
    sg = at(rM.start + KI * TOK * 4, "sg", [4, TOK])
    rM.restart()
    MH = rM.new("MH", [KF, TOK], F32R)
    ML = rM.new("ML", [KF, TOK], F32R)

    def ada_load(chunk, n, *after):
        wait(act, *after)
        act.dma_start(ada_raw[n][:, :, :], w_ada[:, 4 * n:4 * n + 4, bass.ds(chunk * 512, 512)])\
            .then_inc(s_ada[n].sem, 16)

    def ada(chunk, turn, context):
        read = []
        for n in range(2):
            dve.wait_ge(s_ada[n].sem, 16 * turn + 16)
            for kk in range(4):
                k = 4 * n + kk
                for who in range(1 + context):
                    w, o = ada_raw[n][:, kk, :], ada_acc[:, who, :]
                    s = silu_c[:, 8 * who + k:8 * who + k + 1]
                    if k == 0:
                        t = v(lambda: dve.tensor_scalar(o, w, s, None, ALU.mult), latest(T))
                        summed = [t, t]
                    else:
                        t = v(lambda: dve.scalar_tensor_tensor(out=o, in0=w, scalar=s, in1=o, op0=ALU.mult,
                                                               op1=ALU.add), summed[who])
                    summed[who] = t
            read.append(t)
        return read

    def ada_sum(context, *after):
        wait(pe, *after)
        for who in range(1 + context):
            for n in range(4):
                m = pe.matmul(misc[1][:, 4 * who + n:4 * who + n + 1], ada_acc[:, who, n * P:n * P + P],
                              ones[:, 0:1], start=True, stop=True)
        return T.on(m)

    def ada_store(chunk, context, summed):
        t = summed
        tb, r, _ = place["ada_b_2"]
        for who in range(1 + context):
            dst = (mod, mod_ctx)[who]
            d, bias = dst[:, bass.ds(chunk * 4, 4)], table[tb][:, bass.ds(chunk * 4 + r, 4)]
            t = v(lambda: dve.tensor_tensor(d, misc[1][:, 4 * who:4 * who + 4], bias, ALU.add), t)

    W8 = [weights(j, 8) for j in range(2)]
    W4 = [weights(j, 4, n=512) for j in range(2)]
    W16 = [weights(j, 16) for j in range(2)]
    W22 = [weights(j, KF, n=P) for j in range(2)]
    X = (XH, XL)

    split(0, 0, None)
    split(0, 1, None)
    wait(pe, xn_ok, band_ok)
    wait(dve, silu_ok)

    def pool_group(i, e):
        grp, q, turn = 2 * i + e, 6 * i + 3 * e, 4 * i + 2 * e
        for n, src in enumerate((pool_in(grp, 0), pool_in(grp, 1), pool_grp(grp))):
            u = 3 * e + n
            load(3 * i + u // 2, u % 2, src)
        step = [(3 * i + (3 * e + n) // 2, (e + n) % 2) for n in range(3)]
        ahead = [(3 * i + (3 * e + n + 2) // 2, (e + n) % 2) for n in range(3)]

        for b in range(2):
            ada_load(grp, b, latest(V))
        slab_ready(*step[0])
        for b in range(4):
            project_tokens(q, b, W8[step[0][1]], (b // 2) * 256, 256, X, KD, b % 2)
        read = ada(grp, turn, True)
        wait(act, latest(T))
        for b in range(4):
            complete(act, q, b)
            f = (b // 2) * 256
            freed(q, b, act.activation(v_tok[:, b % 2, f:f + 256], acc[b][:, 0:256], ACT.Copy))
        split(*ahead[0], 4 * q + 4, 4 * 512)

        slab_ready(*step[1])
        pools = []
        for b in range(4):
            project(q + 1, b, W8[step[1][1]], b * P, X, KD)
            for f in ((0, 1), (2, 3), (), ())[b]:
                wait(pe, *((acc_free[n].sem, q + 2) for n in (2 * (f // 2), 2 * (f // 2) + 1)))
                o = misc[2 + f // 2][:, (f % 2) * TOK:(f % 2) * TOK + TOK]
                pe.matmul(o, v_tok[:, 0, f * P:f * P + P], band[:, bass.ds(grp, 1), 0:TOK],
                          start=True, stop=False)
                m = pe.matmul(o[:, P:TOK], v_tok[:, 1, f * P:f * P + P], band[:, bass.ds(grp, 1), TOK:384],
                              start=False, stop=True)
                if f % 2:
                    pools.append(T.on(m))
            if b == 2:
                summed = ada_sum(True, read[1])
        for n in range(2):
            pt = misc[2 + n][:, :].rearrange("p (k t) -> p k t", k=2)
            t = a(lambda: act.activation(p_hi[:, 2 * n:2 * n + 2, :], pt, ACT.Copy), pools[n])
            p_ok = v(lambda: dve.tensor_tensor(p_lo[:, 2 * n:2 * n + 2, :], pt,
                                               p_hi[:, 2 * n:2 * n + 2, :].bitcast(F32), ALU.subtract), t)
        wait(act, p_ok)
        for b in range(4):
            if b < 2:
                ada_load(8 + grp, b, read[b])
            complete(act, q + 1, b)
            freed(q + 1, b, act.activation(sg[:, b, :], acc[b][:, 0:TOK], ACT.Silu, bias=0.0))
        ada_store(grp, True, summed)
        read = ada(8 + grp, turn + 1, False)
        split(*ahead[1], 4 * q + 8)

        slab_ready(*step[2])
        wait(pe, p_ok)
        for b in range(4):
            project(q + 2, b, W4[step[2][1]], b * P, (p_hi, p_lo), 4)
        summed = ada_sum(False, read[1])
        rounded = []
        for b in range(5):
            if b < 4:
                wait(dve, (acc_free[b].sem, q + 3))
                complete(dve, q + 2, b)
                t = freed(q + 2, b, dve.scalar_tensor_tensor(
                    out=sg[:, b, :], in0=acc[b][:, 0:TOK], scalar=param("pool_scale", 4 * grp + b, 1),
                    in1=sg[:, b, :], op0=ALU.mult, op1=ALU.mult))
                rounded.append(a(lambda: act.activation(MH[:, bass.ds(4 * grp + b, 1), :], sg[:, b, :], ACT.Copy), t))
            if b > 0:
                n = bass.ds(4 * grp + b - 1, 1)
                m_ok = v(lambda: dve.tensor_tensor(ML[:, n, :], sg[:, b - 1, :], MH[:, n, :].bitcast(F32),
                                                   ALU.subtract), rounded[b - 1])
        split(*ahead[2], 4 * q + 12)
        ada_store(8 + grp, False, summed)

    with loop(2, V=66, A=12, T=8) as i:
        pool_group(i, 0)
        pool_group(i, 1)
    m_ok = latest(V)
    pair, q = 6, 12

    def out_projection(pair, q, w, gate=None, between=None, **per):
        with loop(2, **per) as i:
            for j in range(2):
                load(pair + i, j, out_slab(w, 2 * i + j))
                finish = between(2 * i + j) if between else None
                slab_ready(pair + i, j)
                for n in range(2):
                    b = 2 * j + n
                    project(q + i, b, W16[j], n * P, (MH, ML), KI)
                    complete(dve, q + i, b)
                    x = XT[:, bass.ds(4 * i + b, 1), :]
                    freed(q + i, b, dve.tensor_tensor(x, acc[b][:, 0:TOK], x, ALU.add))
                if finish:
                    finish()
                split(pair + i + 1, j, 4 * (q + i) + 2 * j + 2)
        return (acc_free[3].sem, q + 3)

    wait(pe, m_ok)

    def late_ada(n):
        for b in range(2):
            ada_load(4 + n, b, latest(V))
        read = ada(4 + n, 8 + n, False)
        return lambda: ada_store(4 + n, False, ada_sum(False, read[1]))

    x_ok = out_projection(pair, q, w_pool_out, between=late_ada, V=18, T=2)
    for b in range(3):
        wait(act, (acc_free[b].sem, q + 3))
    pair, q = pair + 2, q + 2

    rM.restart()
    SQ2 = rM.new("SQ2", [KD, TOK])
    XN2 = rM.new("XN2", [KD, TOK])
    t = rms(XT, SQ2, XN2, x_ok, 0, latest(V))
    for k in range(KD):
        xn_ok = halves(XN2, XH, XL, k, t, param("norm_g", KD + k))
    wait(pe, xn_ok)

    rM.restart()
    KQ = rM.new("KQ", [LEVELS * 2, TOK])
    QK = [rM.new(f"QK{j}", [2, TOK]) for j in range(2)]
    DD = [rM.new(f"DD{j}", [2, TOK]) for j in range(2)]
    AT = [rM.new(f"AT{j}", [3, P]) for j in range(2)]
    VT = [rM.new(f"VT{j}", [2, P]) for j in range(2)]
    sigma = rM.new("sigma", [2, TOK])
    gsig = [rM.new(f"gsig{j}", [TOK]) for j in range(2)]
    rR.restart()
    O = rR.new("O", [HEADS + 2, TOK])
    SG = rR.new("SG", [HEADS, TOK])

    zs = xn_ok
    for t0 in (KQ, *QK, *AT, *VT):
        zs = g(lambda: pool.memset(t0[:, :, :], 0.0), zs)
    wait(pe, zs)
    wait(act, zs, x_ok)
    wait(dve, zs)

    def score_matmuls(j):
        kk, qq = QK[j][:, 0, :], QK[j][:, 1, :]
        for n in range(2):
            pe.matmul(misc[0][:, n * P:n * P + P], kk[:, n * P:n * P + P], qq[:, n * P:n * P + P],
                      start=True, stop=True)
        col = 2 * P
        for l in range(7):
            B = 1 << l
            for n in range(2):
                bank, c = divmod(col, 512)
                lhs = kk[:, n * P:n * P + P] if l == 0 else KQ[:, 2 * l, n * P:n * P + P]
                rhs = view(KQ, (2 * l + 1) * TOK + n * P + B, (2 * B, 64 // B), (1, B))
                o = misc[bank][:, c:c + 64].rearrange("p (n b) -> p n b", b=B)
                pe.matmul(o, lhs, rhs, start=True, stop=True)
                col += 64
        bank, c = divmod(col, 512)
        return T.on(pe.matmul(misc[bank][:, c:c + P], KQ[:, 14, 0:P], KQ[:, 15, P:TOK], start=True, stop=True))

    def score_copies(j):
        md = view(mask_diag, 0, (0, 2), (1, P))
        t = v(lambda: dve.copy_predicated(AT[j][:, 0:3:2, :], md, misc[0][:, 0:2 * P].rearrange("p (n t) -> p n t", n=2)))
        col = 2 * P
        for l in range(7):
            B = 1 << l
            bank, c = divmod(col, 512)
            dims = [(2 * B, 64 // B), (1, B)]
            o = view(AT[j], B, (2 * P, 2), *dims)
            m = view(mask_level, l * 64, (0, 2), (B, 64 // B), (1, B))
            d = misc[bank][:, c:c + P].rearrange("p (n m b) -> p n m b", n=2, b=B)
            dve.drain()
            t = v(lambda: dve.copy_predicated(o, m, d))
            col += P
        bank, c = divmod(col, 512)
        return v(lambda: dve.tensor_copy(AT[j][:, 1, :], misc[bank][:, c:c + P]), t)

    def value_matmuls(j):
        o = misc[3][:, 0:TOK]
        pe.matmul(o, VT[j][:, 0, :], AT[j][:, 0:2, :], start=True, stop=False)
        return T.on(pe.matmul(o[:, P:TOK], VT[j][:, 1, :], AT[j][:, 2, :], start=False, stop=True))

    def levels(j, ready):
        for l in range(LEVELS):
            B = 1 << l
            dims = [(2 * B, P // B), (TOK + B, 2), (1, B)]
            src, dec, o = view(QK[j], 0, *dims), view(DD[j], 0, *dims), view(KQ, l * 2 * TOK, *dims)
            made = v(lambda: dve.tensor_tensor(o, src, dec, ALU.mult), ready)
            if l < LEVELS - 1:
                other = view(DD[j], TOK + 2 * B - 1, (2 * B, P // B), (-B, 2), (0, B))
                ready = v(lambda: dve.tensor_tensor(dec, dec, other, ALU.mult))
        return made

    def head(i, j, q0, pair0):
        n, q, pair = 2 * i + j, q0 + 2 * i + j, pair0 + i
        load(pair, j, head_slab(n))
        before_v, before_a = latest(V), latest(A)
        o = view(ones, 0, (0, 2), (1, P))
        suffix = g(lambda: pool.tensor_tensor(DD[j][:, 0, :].rearrange("p (a t) -> p a t", a=2), o, o, ALU.mult),
                   before_v)

        slab_ready(pair, j)
        project(q, 0, W8[j], 0, X, KD)
        project(q, 1, W8[j], P, X, KD)
        wait(pe, before_v, before_a)
        scored = score_matmuls(1 - j)
        o_done = value_matmuls(j)
        project(q, 2, W8[j], 3 * P, X, KD)
        for half in range(2):
            project_tokens(q, 3, W8[j], 2 * P, P, X, KD, half, at_col=half * P, first=half == 0,
                           last=half == 1)

        complete(act, q, 0)
        freed(q, 0, act.activation(QK[j][:, 1, :], acc[0][:, 0:TOK], ACT.Copy))
        complete(act, q, 1)
        wait(act, before_a)
        act.activation(sigma[:, 0, :], acc[1][:, 0:TOK], ACT.Sigmoid, bias=0.0, scale=-1.0)
        sig_ok = freed(q, 1, act.activation(sigma[:, 1, :], acc[1][:, 0:TOK], ACT.Sigmoid, bias=0.0))
        l0, l1 = lb[:, 0, bass.ds(n, 1)], lb[:, 1, bass.ds(n, 1)]
        wait(act, sig_ok)
        a(lambda: act.activation(QK[j][:, 0, :], sigma[:, 0, :], ACT.Copy, scale=l1))
        factors = a(lambda: act.activation(DD[j][:, 1, :], sigma[:, 1, :], ACT.Identity, bias=l0, scale=l1))
        a(lambda: act.activation(O[:, bass.ds(n, 1), :], misc[3][:, 0:TOK], ACT.Copy), o_done)
        complete(act, q, 2)
        g_ok = a(lambda: act.activation(gsig[j][:, :], acc[2][:, 0:TOK], ACT.Sigmoid, bias=0.0))
        complete(act, q, 3)
        freed(q, 3, act.activation(VT[j][:, :, :], acc[3][:, 0:TOK].rearrange("p (a d) -> p a d", a=2), ACT.Copy))

        wait(dve, factors, suffix, scored)
        levels(j, None)
        dve.drain()
        score_copies(1 - j)
        wait(dve, g_ok)
        freed(q, 2, dve.scalar_tensor_tensor(out=SG[:, bass.ds(n, 1), :], in0=acc[2][:, 0:TOK],
                                             scalar=param("hgrn_norm_g", n, 1), in1=gsig[j][:, :],
                                             op0=ALU.mult, op1=ALU.mult))
        split(pair + 1, j, 4 * q + 4)

    VH = 2 * LEVELS - 1 + 9
    with loop(HEADS // 2, V=2 * VH, A=8, G=2, T=4) as i:
        head(i, 0, q, pair)
        head(i, 1, q, pair)
    pair, q = pair + HEADS // 2, q + HEADS
    wait(pe, latest(V), latest(A))
    t = value_matmuls(0)
    scored = score_matmuls(1)
    a(lambda: act.activation(O[:, HEADS, :], misc[3][:, 0:TOK], ACT.Copy), t)
    wait(dve, scored)
    t = score_copies(1)
    wait(pe, t, latest(A))
    t = value_matmuls(1)
    o_ok = a(lambda: act.activation(O[:, HEADS + 1, :], misc[3][:, 0:TOK], ACT.Copy), t)

    rM.restart()
    OSQ = rM.new("OSQ", [HEADS, TOK])
    L8 = at(rM.start + KI * TOK * 4, "L8", [8, P])
    R8 = at(rM.start + (KF + KI) * TOK * 4, "R8", [2, 512])
    t = g(lambda: pool.memset(L8[0:8, :, :], 0.0), o_ok)
    sel_rows = g(lambda: pool.affine_select(out=L8[0:8, :, :], in_=L8[0:8, :, :], compare_op=ALU.not_equal,
                                            fill=1.0, base=0, pattern=[[-1, 8], [0, P]], channel_multiplier=1), t)
    wait(act, o_ok)
    for c in range(2):
        t = a(lambda: act.activation(OSQ[:, 8 * c:8 * c + 8, :], O[:, 2 + 8 * c:10 + 8 * c, :], ACT.Square, bias=0.0))
        wait(pe, t, sel_ok)
        for n in range(8):
            m = pe.matmul(misc[0][0:8, c * TOK:c * TOK + TOK], sel8[:, 7 - n:15 - n], OSQ[:, 8 * c + n, :],
                          start=n == 0, stop=n == 7)
        t = T.on(m)
    t = v(lambda: dve.tensor_scalar(R8[0:8, 0, :], misc[0][0:8, :], 1.0 / P, EPS, ALU.mult, ALU.add), t)
    t = a(lambda: act.activation(R8[0:8, 1, :], R8[0:8, 0, :], ACT.Sqrt, bias=0.0), t)
    root = v(lambda: dve.reciprocal(R8[0:8, 0, :], R8[0:8, 1, :]), t)
    rM.restart()
    MH = rM.new("MH_b", [KF, TOK], F32R)
    ML = rM.new("ML_b", [KF, TOK], F32R)
    wait(pe, root, sel_rows)
    wait(act, root)
    read = {0: root, 1: root}
    for n in range(0, HEADS, 2):
        b = (n // 2) % 2
        bank = misc[1 + b]
        wait(pe, read[b])
        for k in range(2):
            m = pe.matmul(bank[:, k * TOK:k * TOK + TOK], L8[0:8, (n + k) % 8, :],
                          R8[0:8, 0, (n // 8) * TOK:(n // 8) * TOK + TOK], start=True, stop=True)
        t = T.on(m)
        both = slice(n + 2, n + 4)
        pv = bank[:, :].rearrange("p (k t) -> p k t", k=2)
        read[b] = t = v(lambda: dve.tensor_tensor(O[:, both, :], O[:, both, :], pv, ALU.mult), t)
        t = v(lambda: dve.tensor_tensor(O[:, both, :], O[:, both, :], SG[:, n:n + 2, :], ALU.mult), t)
        t = a(lambda: act.activation(MH[:, n:n + 2, :], O[:, both, :], ACT.Copy), t)
        m_ok = v(lambda: dve.tensor_tensor(ML[:, n:n + 2, :], O[:, both, :], MH[:, n:n + 2, :].bitcast(F32),
                                           ALU.subtract), t)
    wait(pe, m_ok)
    x_ok = out_projection(pair, q, w_hgrn_out)
    pair, q = pair + 2, q + 2

    rM.restart()
    MIXH = rM.new("MIXH", [8, TOK], F32R)
    MIXL = rM.new("MIXL", [8, TOK], F32R)
    HCH = rM.new("HCH", [KD, TOK], F32R)
    HCL = rM.new("HCL", [KD, TOK], F32R)
    QT = rM.new("QT", [4, TOK])
    CP = rM.new("CP", [2, TOK + TAPS - 1])
    CA = rM.new("CA", [2, TOK])
    U = rM.new("U", [2, TOK])
    rR.restart()
    BIAS = rR.new("BIAS", [2, NA_HEADS, TOK])
    KT = rR.new("KT", [4, 2 * TOK])
    VV = rR.new("VV", [4, ATT])
    VG = rR.new("VG", [2, TOK])
    SR = rR.new("SR", [2, TOK])
    BS = rM.new("BS", [2, P])
    WS = rstd[:, :, :].rearrange("p a (b q) -> p (a b) q", b=2)
    c_tok = at(rM.start, "c_tok", [2, D])
    XC = at(rM.start + 8192, "XC", [KD, TOK])
    ws_in = at(rM.start + 32768, "ws_in", [4, P])
    SQ3 = at(rR.start + 16384, "SQ3", [KD, TOK])
    XN3 = at(rR.start + 24576, "XN3", [KD, TOK])
    pad = at(rM.start + 36864, "pad", [P])
    REL = 31
    rpb = at(rM.start + 36864 + 512, "rpb", [REL])
    scratch = nc.dram_tensor("rpb_padded", (NA_HEADS * 15, P), F32, kind="Internal").ap()

    def cols2(n, width=512):
        return w_in2[:, :, n:n + width]

    load(pair, 0, cols2(2048))
    load(pair, 1, cols2(1536))
    for b in range(4):
        for eng in (sp, pool, act, dve, pe):
            eng.wait_ge(acc_free[b].sem, q + 1)
    sp.dma_start(c_tok[:, :, :], h["ctx_2"][0].rearrange("(a p) n -> p a n", a=2)).then_inc(s_ctx.sem, 16)

    def whole(name):
        return h[name].ap if False else h[name]

    def spread(name, offset, n, parts):
        return bass.AP(h[name].tensor, offset, [[0, parts], [1, n]])

    n_rows = 0
    for k, name in enumerate(("sg_norm_g_2", "sg_norm_b_2")):
        sp.dma_start(SR[:, k, :], spread(name, 0, 256, P)).then_inc(s_row.sem, 16)
        n_rows += 16
    for n in range(4):
        sp.dma_start(BS[64 * (n % 2):64 * (n % 2) + 64, n // 2, :], spread("sg_b_2", n * P, P, 64))\
          .then_inc(s_row.sem, 16)
        n_rows += 16
    sp.dma_start(ws_in[:, :, :], h["sg_w_2"][0].rearrange("g p q -> p g q")).then_inc(s_row.sem, 16)
    n_rows += 16
    sp.dma_start(rpb[0:120, :], h["na_rpb_2"].rearrange("a h r c -> (a h r) c")).then_inc(s_pad.sem, 16)
    t = g(lambda: pool.memset(pad[:, :], 0.0))
    back = view(rpb, REL - 1, (-1, REL))
    t = g(lambda: pool.tensor_copy(pad[0:120, 48:48 + REL], bass.AP(back.tensor, REL - 1, [[back.ap[0][0], 120], [-1, REL]])),
          t, (s_pad.sem, 16))
    wait(sp, t)
    sp.dma_start(scratch, pad[0:120, :]).then_inc(s_scr.sem, 16)
    sp.wait_ge(s_scr.sem, 16)
    n_bias = 0
    for r in range(4):
        for r2 in range(4):
            dst = BIAS[64 * (r % 2):64 * (r % 2) + 64, r // 2, :, (3 - r2) * GRID:(4 - r2) * GRID]
            src = bass.AP(scratch.tensor, (r2 - r + 7) * P, [[1, 64], [15 * P, NA_HEADS], [1, GRID]])
            sp.dma_start(dst, src).then_inc(s_bias.sem, 16)
            n_bias += 16
    pool.wait_ge(s_bias.sem, n_bias)
    for a0 in range(2):
        for r in range(2):
            part = BIAS[64 * r:64 * r + 64, a0, :, :].rearrange("p h (r c) -> p (h r) c", c=GRID)
            left, right = part[:, :, 16:64], part[:, :, 0:48]
            t = g(lambda: pool.affine_select(out=left, in_=left, compare_op=ALU.is_ge, fill=-1e30, base=55,
                                             pattern=[[0, 32], [-1, 48]], channel_multiplier=-1))
            bias_ok = g(lambda: pool.affine_select(out=right, in_=right, compare_op=ALU.is_ge, fill=-1e30,
                                                   base=-56, pattern=[[0, 32], [1, 48]],
                                                   channel_multiplier=1), t)

    wait(pool, bias_ok)

    t = rms(XT, SQ3, XN3, x_ok, 0, latest(V))
    for k in range(KD):
        x_ok = v(lambda: dve.tensor_scalar(XT[:, k, :], XN3[:, k, :], param("final_g", k), None, ALU.mult), t)

    for n, (gname, m0, s0) in enumerate((("norm1_g_2", mod, 8), ("norm1_g_2", mod_ctx, 8), ("norm2_g_2", mod, 32))):
        gain_ok = v(lambda: dve.scalar_tensor_tensor(out=gain[:, n, :], in0=m0[:, s0:s0 + 8], scalar=1.0,
                                                     in1=param(gname, 0, 8), op0=ALU.add, op1=ALU.mult))
    t = rms(XT, SQ3, XN3, x_ok, 0, gain_ok)
    for k in range(KD):
        xn_ok = halves(XN3, XH, XL, k, t, gain[:, 0, k:k + 1], mod[:, k:k + 1])
    xc_ok = turn_in(c_tok, XC, (s_ctx.sem, 16), (xn_ok,))
    t = rms(XC, SQ3, XN3, xc_ok, 0, xc_ok)
    for k in range(KD):
        hc_ok = halves(XN3, HCH, HCL, k, t, gain[:, 1, k:k + 1], mod_ctx[:, k:k + 1])
    HC = (HCH, HCL)

    for n, (c, j) in enumerate(((512, 0), (1024, 1), (0, 0))):
        load(pair + 1 + n // 2, j, cols2(c))
    load(pair + 2, 1, w_out2[:, :, 0:512])
    load(pair + 3, 0, w_out2[:, :, 512:1024])
    load(pair + 3, 1, up_slab(0))

    wait(pe, xn_ok, hc_ok)
    slab_ready(pair, 0)
    for b in range(4):
        project(q, b, W8[0], b * P, X, KD)
    cz = v(lambda: dve.memset(CP[:, :, :], 0.0), (s_scr.sem, 16))
    for f in range(2):
        complete(act, q, 2 + f)
        t = freed(q, 2 + f, act.activation(CA[:, f, :], acc[2 + f][:, 0:TOK], ACT.Sigmoid, bias=0.0))
        wait(dve, t, cz)
        complete(dve, q, f)
        gated = freed(q, f, dve.tensor_tensor(CP[:, f, 15:15 + TOK], acc[f][:, 0:TOK], CA[:, f, :], ALU.mult))
    split(pair + 1, 0, 4 * q + 4)
    q += 1
    chain = [gated, gated]

    def conv(k0, k1):
        for k in range(k0, k1):
            for f in range(2):
                w, x = param("cv_w_2", 2 * k + f), CP[:, f, k:k + TOK]
                if k == 0:
                    chain[f] = v(lambda: dve.tensor_scalar(CA[:, f, :], x, w, param("cv_b_2", f), ALU.mult,
                                                           ALU.add), (acc_free[f].sem, q + 1), chain[f])
                else:
                    chain[f] = v(lambda: dve.scalar_tensor_tensor(out=CA[:, f, :], in0=x, scalar=w, in1=CA[:, f, :],
                                                                  op0=ALU.mult, op1=ALU.add), chain[f])

    pe.wait_ge(s_row.sem, n_rows)
    dve.wait_ge(s_row.sem, n_rows)
    for n in range(4):
        m = pe.transpose(misc[3][:, n * P:n * P + P], ws_in[:, n, :], ident[:, :])
    t = T.on(m)
    ws_ok = v(lambda: dve.tensor_copy(WS, misc[3][:, :].rearrange("p (g q) -> p g q", g=4)), t)

    slab_ready(pair, 1)
    for b in range(2):
        project(q, b, W8[1], b * P, X, KD)
    for b in range(2):
        project_tokens(q, 2 + b, W8[1], 256, 256, X, KD, b)
    for b in range(2):
        complete(act, q, b)
        u_ok = freed(q, b, act.activation(U[:, b, :], acc[b][:, 0:TOK], ACT.Gelu_apprx_tanh, bias=0.0))
    split(pair + 1, 1, 4 * q + 4)
    conv(0, 8)
    for b in range(2):
        complete(act, q, 2 + b)
        t = freed(q, 2 + b, act.activation(VG[:, b, :], acc[2 + b][:, 0:TOK], ACT.Gelu_apprx_tanh, bias=0.0))
        t = v(lambda: dve.bn_stats(stats[:, b, 0:6], VG[:, b, :]), t)
        t = v(lambda: dve.bn_aggr(stats[:, b, 6:8], stats[:, b, 0:6]), t)
        t = v(lambda: dve.tensor_scalar(stats[:, b, 0:1], stats[:, b, 7:8], EPS, None, ALU.add), t)
        t = a(lambda: act.activation(stats[:, b, 1:2], stats[:, b, 0:1], ACT.Sqrt, bias=0.0), t)
        t = v(lambda: dve.reciprocal(stats[:, b, 2:3], stats[:, b, 1:2]), t)
        t = v(lambda: dve.tensor_scalar(VG[:, b, :], VG[:, b, :], stats[:, b, 6:7], stats[:, b, 2:3], ALU.subtract,
                                        ALU.mult), t)
        t = v(lambda: dve.tensor_tensor(VG[:, b, :], VG[:, b, :], SR[:, 0, :], ALU.mult), t)
        vg_ok = v(lambda: dve.tensor_tensor(VG[:, b, :], VG[:, b, :], SR[:, 1, :], ALU.add), t)
    q += 1

    slab_ready(pair + 1, 0)
    for who, xx in enumerate((X, HC)):
        for b in range(4):
            project(q + who, b, W8[0], b * P, xx, KD)
            complete(act, q + who, b)
            k_ok = freed(q + who, b, act.activation(KT[:, b, who * TOK:who * TOK + TOK], acc[b][:, 0:TOK], ACT.Copy))
        if who == 0:
            wait(pe, vg_ok, ws_ok)
            for n in range(4):
                for half in range(2):
                    c = (n // 2) * TOK + half * P
                    m = pe.matmul(misc[0][64 * (n % 2):64 * (n % 2) + 64, c:c + P],
                                  VG[:, half, n * 64:n * 64 + 64], WS[:, n, :], start=True, stop=True)
            mixed = T.on(m)
    split(pair + 2, 0, 4 * q + 8)
    q += 2
    conv(8, 20)
    wait(dve, mixed, u_ok)
    mv = misc[0][:, :].rearrange("p (f a t) -> p f a t", f=2, a=2)
    uv = U[:, :, :].rearrange("p f (a t) -> p f a t", a=2)
    bsv = view(BS, 0, (P, 2), (0, 2), (1, P))
    t = v(lambda: dve.tensor_tensor(mv, mv, bsv, ALU.add))
    t = v(lambda: dve.tensor_tensor(uv, uv, mv, ALU.mult), t)
    t = a(lambda: act.activation(MIXH[:, 4:6, :], U[:, :, :], ACT.Copy), t)
    v(lambda: dve.tensor_tensor(MIXL[:, 4:6, :], U[:, :, :], MIXH[:, 4:6, :].bitcast(F32), ALU.subtract), t)

    slab_ready(pair + 1, 1)
    for b in range(4):
        project_tokens(q, b, W8[1], 0, 512, (X, HC)[b // 2], KD, b % 2)
        complete(act, q, b)
        v_ok = freed(q, b, act.activation(VV[:, b, :], acc[b][:, :], ACT.Copy))
    split(pair + 2, 1, 4 * q + 4)
    q += 1
    conv(20, TAPS)

    slab_ready(pair + 2, 0)
    for b in range(4):
        project(q, b, W8[0], b * P, X, KD)
        complete(act, q, b)
        q_ok = freed(q, b, act.activation(QT[:, b, :], acc[b][:, 0:TOK], ACT.Copy))
    split(pair + 3, 0, 4 * q + 4)
    q += 1

    caf = CA[:, :, :].rearrange("p f t -> p (f t)")
    rsf = rstd[:, :, :].rearrange("p f t -> p (f t)")
    wait(pe, chain[0], chain[1], latest(V))
    t = T.on(pe.matmul(misc[1][:, :], block64[:, :], caf, start=True, stop=True))
    t = v(lambda: dve.scalar_tensor_tensor(out=caf, in0=misc[1][:, :], scalar=-1.0 / 64, in1=caf, op0=ALU.mult,
                                           op1=ALU.add), t)
    t = a(lambda: act.activation(rsf, caf, ACT.Square, bias=0.0), t)
    wait(pe, t)
    t = T.on(pe.matmul(misc[1][:, :], block64[:, :], rsf, start=True, stop=True))
    t = v(lambda: dve.tensor_scalar(rsf, misc[1][:, :], 1.0 / 64, EPS, ALU.mult, ALU.add), t)
    t = a(lambda: act.activation(rsf, rsf, ACT.Sqrt, bias=0.0), t)
    t = v(lambda: dve.reciprocal(rsf, rsf), t)
    t = v(lambda: dve.tensor_tensor(caf, caf, rsf, ALU.mult), t)
    for f in range(2):
        t2 = v(lambda: dve.tensor_scalar(CA[:, f, :], CA[:, f, :], param("cv_norm_g_2", f), param("cv_norm_b_2", f),
                                         ALU.mult, ALU.add), t)
    t = a(lambda: act.activation(CA[:, :, :], CA[:, :, :], ACT.Silu, bias=0.0), t2)
    t = a(lambda: act.activation(MIXH[:, 6:8, :], CA[:, :, :], ACT.Copy), t)
    cv_ok = v(lambda: dve.tensor_tensor(MIXL[:, 6:8, :], CA[:, :, :], MIXH[:, 6:8, :].bitcast(F32),
                                        ALU.subtract), t)

    SS = [at(rM.start + 16384 + 2048 * n, f"SS{n}", [512]) for n in range(2)]
    EE = [at(rM.start + 20480 + 2048 * n, f"EE{n}", [512]) for n in range(2)]
    PT = at(rM.start + 24576, "PT", [4, TOK])
    wait(pe, q_ok, k_ok, v_ok, cv_ok)
    wait(dve, bias_ok, v_ok)
    scale = 0.125
    s_read = [cv_ok, cv_ok]
    e_read = [cv_ok, cv_ok]
    pv_done = cv_ok
    mix_ok = None
    units = [(n, half) for n in range(NA_HEADS) for half in range(2)]
    s_tok, p_tok = {}, {}

    def scores(n, half):
        r0 = 64 * (n % 2)
        wait(pe, s_read[half])
        s_tok[n, half] = T.on(pe.matmul(misc[half][:, :], QT[r0:r0 + 64, n // 2, half * P:half * P + P],
                                        KT[r0:r0 + 64, n // 2, :], start=True, stop=True))

    def view4(t, offset):
        whole = t[:, :, :, :]
        return bass.AP(whole.tensor, offset, [list(whole.ap[0]), [-1, TOK]])

    def softmax(n, half):
        S, E = SS[half], EE[half]
        t = v(lambda: dve.scalar_tensor_tensor(out=S[:, 0:TOK], in0=misc[half][:, 0:TOK], scalar=scale,
                                               in1=view4(BIAS, (half * NA_HEADS + n) * TOK + TOK - 1), op0=ALU.mult, op1=ALU.add), s_tok[n, half])
        t = s_read[half] = v(lambda: dve.tensor_scalar(S[:, TOK:512], misc[half][:, TOK:512], scale, None, ALU.mult))
        t = v(lambda: dve.tensor_reduce(soft[:, half, 0:1], S[:, :], AX_X, ALU.max, negate=True), t)
        wait(act, e_read[half])
        t = a(lambda: act.activation(E[:, :], S[:, :], ACT.Exp, bias=soft[:, half, 0:1],
                                     accum_out=soft[:, half, 1:2]), t)
        t = v(lambda: dve.reciprocal(soft[:, half, 2:3], soft[:, half, 1:2]), t)
        p_tok[n, half] = v(lambda: dve.tensor_scalar(E[:, :], E[:, :], soft[:, half, 2:3], None, ALU.mult), t)

    turned = {}

    def turn(n, half):
        wait(pe, p_tok[n, half])
        if n > 0:
            wait(pe, turned[n - 1, half])
        for k in range(4):
            m = pe.transpose(misc[2 + half][:, k * P:k * P + P], EE[half][:, k * P:k * P + P], ident[:, :])
        e_read[half] = t = T.on(m)
        turned[n, half] = a(lambda: act.activation(
            PT[:, :, half * P:half * P + P], misc[2 + half][:, :].rearrange("p (k t) -> p k t", k=4), ACT.Copy),
            t, pv_done)

    def values(n):
        r0, b = 64 * (n % 2), n // 2
        wait(pe, turned[n, 0], turned[n, 1])
        if n % 2 == 0:
            pe.wait_ge(acc_free[b].sem, q + 1)
        for k in range(4):
            m = pe.matmul(acc[b][r0:r0 + 64, 0:TOK], VV[:, k, n * 64:n * 64 + 64], PT[:, k, :],
                          start=k == 0, stop=k == 3)
        if n % 2 == 0:
            return T.on(m)
        m.then_inc(tile_done.sem, 1)
        return (tile_done.sem, 4 * q + b + 1)

    scores(0, 0)
    scores(0, 1)
    for n in range(NA_HEADS):
        for half in range(2):
            softmax(n, half)
            if n + 1 < NA_HEADS:
                scores(n + 1, half)
        for half in range(2):
            turn(n, half)
        pv_done = values(n)
        if n % 2:
            b = n // 2
            complete(act, q, b)
            t = a(lambda: act.activation(MIXH[:, b, :], acc[b][:, 0:TOK], ACT.Copy))
            wait(dve, t)
            mix_ok = freed(q, b, dve.tensor_tensor(MIXL[:, b, :], acc[b][:, 0:TOK],
                                                   MIXH[:, b, :].bitcast(F32), ALU.subtract))
    q += 1

    wait(pe, mix_ok)
    for n in range(2):
        pr, j = pair + 2 + (n + 1) // 2, (n + 1) % 2
        slab_ready(pr, j)
        for b in range(4):
            project(q, b, W8[j], b * P, (MIXH, MIXL), KD)
            complete(dve, q, b)
            k = 4 * n + b
            x_ok = freed(q, b, dve.scalar_tensor_tensor(out=XT[:, k, :], in0=acc[b][:, 0:TOK],
                                                        scalar=mod[:, 16 + k:17 + k], in1=XT[:, k, :],
                                                        op0=ALU.mult, op1=ALU.add))
        if n == 0:
            split(pair + 3, 1, 4 * q + 4)
            load(pair + 4, 0, up_slab(1))
        else:
            split(pair + 4, 0, 4 * q + 4)
            load(pair + 4, 1, up_slab(2))
        q += 1

    SQ4 = at(rR.start, "SQ4", [KD, TOK])
    XN4 = at(rR.start + 8192, "XN4", [KD, TOK])
    GP = at(rR.start + 16384, "GP", [2, TOK + 2])
    GC = at(rR.start + 20480, "GC", [2, TOK])
    rM.restart()
    MH = rM.new("MH_c", [KF, TOK], F32R)
    ML = rM.new("ML_c", [KF, TOK], F32R)
    gz = v(lambda: dve.memset(GP[:, :, :], 0.0))
    t = rms(XT, SQ4, XN4, x_ok, 0, latest(V))
    for k in range(KD):
        xn_ok = halves(XN4, XH, XL, k, t, gain[:, 2, k:k + 1], mod[:, 24 + k:25 + k])
    wait(pe, xn_ok)
    wait(act, gz)

    def up(pr, j, n, q, after=None):
        slab_ready(pr, j)
        before = latest(V)
        for b in range(4):
            project(q, b, W8[j], b * P, X, KD)
        for f in range(2):
            complete(act, q, f)
            wait(act, before)
            t = freed(q, f, act.activation(GP[:, f, 1:1 + TOK], acc[f][:, 0:TOK], ACT.Copy))
            k = 2 * n + f
            w = [param("ffn_conv_w_2", KF * tap + k, 1) for tap in range(3)]
            t = v(lambda: dve.tensor_scalar(GC[:, f, :], GP[:, f, 0:TOK], w[0], param("ffn_conv_b_2", k, 1),
                                            ALU.mult, ALU.add), t)
            for tap in (1, 2):
                t = v(lambda: dve.scalar_tensor_tensor(out=GC[:, f, :], in0=GP[:, f, tap:tap + TOK], scalar=w[tap],
                                                       in1=GC[:, f, :], op0=ALU.mult, op1=ALU.add), t)
            tt = a(lambda: act.activation(GC[:, f, :], GC[:, f, :], ACT.Silu, bias=0.0), t)
            wait(dve, tt)
            complete(dve, q, 2 + f)
            t = freed(q, 2 + f, dve.tensor_tensor(GC[:, f, :], GC[:, f, :], acc[2 + f][:, 0:TOK], ALU.mult))
        both = bass.ds(2 * n, 2)
        t = a(lambda: act.activation(MH[:, both, :], GC[:, :, :], ACT.Copy), t)
        t = v(lambda: dve.tensor_tensor(ML[:, both, :], GC[:, :, :], MH[:, both, :].bitcast(F32), ALU.subtract), t)
        split(pr + 1, j, 4 * q + 4)
        return t

    up(pair + 3, 1, 0, q)
    pair, q = pair + 4, q + 1
    with loop(5, V=14, A=6) as i:
        for j in range(2):
            up(pair + i, j, 1 + 2 * i + j, q + 2 * i + j)
    for i in range(3, 11):
        pr, j = pair + (i - 1) // 2, (i - 1) % 2
        load(pr, j, up_slab(i))
    wait(pe, latest(V))
    pair, q = pair + 5, q + 10
    tiles = 4 * q

    def down(i, j, ahead):
        n = 2 * i + j
        load(pair + i, j, down_slab(n))
        slab_ready(pair + i, j)
        pe.wait_ge(acc_free[j].sem, q + i + 1)
        (wh, wl) = W22[j]
        o = acc[j][:, 0:TOK]
        for k in range(KF):
            pe.matmul(o, wh[:, k, :], MH[:, k, :], start=k == 0, stop=False)
            pe.matmul(o, wh[:, k, :], ML[:, k, :], start=False, stop=False)
            m = pe.matmul(o, wl[:, k, :], MH[:, k, :], start=False, stop=k == KF - 1)
        m.then_inc(tile_done.sem, 1)
        dve.wait_ge(tile_done.sem, tiles + n + 1)
        x = XT[:, bass.ds(n, 1), :]
        freed(q, j, dve.scalar_tensor_tensor(out=x, in0=acc[j][:, 0:TOK], scalar=mod[:, bass.ds(40 + n, 1)],
                                             in1=x, op0=ALU.mult, op1=ALU.add))
        if ahead:
            split(pair + i + 1, j, tiles + n + 1, KF * P)

    with loop(3) as i:
        down(i, 0, True)
        down(i, 1, True)
    down(3, 0, False)
    down(3, 1, False)

    x_ok = (acc_free[1].sem, q + 5)
    wait(act, (acc_free[0].sem, q + 5))
    OT = at(rR.start + 24576, "OT", [2, D])
    t = rms(XT, SQ4, XN4, x_ok, 0, latest(V))
    for k in range(KD):
        t2 = v(lambda: dve.tensor_scalar(XN4[:, k, :], XN4[:, k, :], param("final_norm_g_2", k), None, ALU.mult), t)
    wait(pe, t2)
    s_out = sig("out_stored")
    for half in range(2):
        for kq in range(2):
            n = 2 * half + kq
            for k in range(4):
                m = pe.transpose(misc[n][:, k * P:k * P + P], XN4[:, 4 * kq + k, half * P:half * P + P], ident[:, :])
            t = T.on(m)
            t = v(lambda: dve.tensor_copy(OT[:, half, kq * 512:kq * 512 + 512], misc[n][:, :]), t)
        wait(sp, t)
        sp.dma_start(out[0, half * P:half * P + P, :], OT[:, half, :]).then_inc(s_out.sem, 16)
    sp.wait_ge(s_out.sem, 32)


_INS = ["x", "norm_g", "pool_w_in", "pool_w_grp", "pool_scale", "pool_w_out", "hgrn_w_in",
        "hgrn_lower_bounds", "hgrn_norm_g", "hgrn_w_out", "final_g", "c_2", "ctx_2", "c_ctx_2",
        "ada_w_2", "ada_b_2", "norm1_g_2", "w_in_2", "na_rpb_2", "sg_norm_g_2", "sg_norm_b_2",
        "sg_w_2", "sg_b_2", "cv_w_2", "cv_b_2", "cv_norm_g_2", "cv_norm_b_2", "w_out_2",
        "norm2_g_2", "ffn_w_up_2", "ffn_conv_w_2", "ffn_conv_b_2", "ffn_w_down_2",
        "final_norm_g_2"]


def kernel(**inputs):
    import numpy as _np
    import concourse.bacc as _bacc
    from concourse.bass_utils import run_bass_kernel_spmd as _run

    nc = _bacc.Bacc("TRN2", target_bir_lowering=False, num_devices=1)
    arrays, args = {}, {}
    for name in _INS:
        a = _np.ascontiguousarray(inputs[name])
        arrays[f"in_{name}_dram"] = a
        args[name] = nc.dram_tensor(f"in_{name}_dram", a.shape, mybir.dt.from_np(a.dtype),
                                    kind="ExternalInput").ap()
    out = nc.dram_tensor("out_0_dram", (1, TOK, D), F32, kind="ExternalOutput").ap()
    build(nc, args, out)
    r = _run(nc, [arrays], core_ids=[0])
    return r.results[0]["out_0_dram"]
```

```python
from contextlib import ExitStack, contextmanager

import concourse.bass as bass
from concourse import mybir

P = 128
TOK = 256
D = 1024
KD = D // P
INNER = 2048
KI = INNER // P
HEADS = KI
ATT = 512
NA_HEADS = 8
DFF = 2816
KF = DFF // P
GRID = 64
TAPS = 31
SLAB = 4096
EPS = 1e-6
LEVELS = 8

F32 = mybir.dt.float32
F32R = mybir.dt.float32r
U8 = mybir.dt.uint8
I32 = mybir.dt.int32
ALU = mybir.AluOpType
ACT = mybir.ActivationFunctionType
AX_X = mybir.AxisListType.X
PE_, ACT_, DVE_, POOL_, SP_ = "PE", "ACT", "DVE", "POOL", "SP"


class Signal:

    def __init__(self, nc, stack, name):
        self.sem = stack.enter_context(nc.semaphore(name))
        self.count = 0
        self.offset = 0
        self.all = None

    def on(self, instruction, k=1):
        instruction.then_inc(self.sem, k)
        self.count += k
        return (self.sem, self.offset + self.count)


def build(nc, h, out):
    stack = ExitStack()
    with stack:
        _build(nc, h, out, stack)


def _build(nc, h, out, stack):
    pe, act, dve, pool, sp = nc.tensor, nc.scalar, nc.vector, nc.gpsimd, nc.sync
    stack.enter_context(nc.allow_non_contiguous_dma(reason="short rows of parameters"))

    base = (nc.sbuf_base + 63) // 64 * 64
    top = [base]

    def at(offset, name, shape, dt=F32):
        return nc.alloc_sbuf_tensor_at(name, [P] + shape, dt, offset=offset)

    def size(shape, dt):
        n = 1
        for x in shape:
            n *= x
        return (n * (1 if dt == U8 else 4) + 31) // 32 * 32

    def fixed(name, shape, dt=F32):
        t = at(top[0], name, shape, dt)
        top[0] += size(shape, dt)
        return t

    class Region:

        def __init__(self, nbytes):
            self.start, self.end = top[0], top[0] + nbytes
            top[0] = self.end
            assert self.end <= nc.sbuf_usable_end, (self.end, nc.sbuf_usable_end)
            self.next = self.start

        def restart(self, skip=0):
            self.next = self.start + skip

        def new(self, name, shape, dt=F32):
            t = at(self.next, name, shape, dt)
            self.next += size(shape, dt)
            assert self.next <= self.end, (name, self.next - self.end)
            return t

    raw = [fixed(f"raw{j}", [SLAB]) for j in range(2)]
    w_hi = [fixed(f"w_hi{j}", [SLAB], F32R) for j in range(2)]
    w_lo = [fixed(f"w_lo{j}", [SLAB], F32R) for j in range(2)]
    XT = fixed("XT", [KD, TOK])
    XH = fixed("XH", [KD, TOK], F32R)
    XL = fixed("XL", [KD, TOK], F32R)
    ident = fixed("ident", [P])
    ones = fixed("ones", [P])
    block64 = fixed("block64", [P])
    sel8 = fixed("sel8", [15])
    table = [fixed(f"table{n}", [w]) for n, w in enumerate((128, 116, 88))]
    mod = fixed("mod", [48])
    mod_ctx = fixed("mod_ctx", [16])
    silu_c = fixed("silu_c", [16])
    lb = fixed("lb", [4, KI])
    gain = fixed("gain", [4, KD])
    mask_diag = fixed("mask_diag", [P], U8)
    mask_level = fixed("mask_level", [7, 64], U8)
    rstd = fixed("rstd", [2, TOK])
    eps = fixed("eps", [2])
    stats = fixed("stats", [2, 8])
    soft = fixed("soft", [2, 4])
    rM = Region(2 * KF * TOK * 4)
    rR = Region(nc.sbuf_usable_end - top[0])

    acc = [stack.enter_context(nc.psum_tensor(f"acc{b}", [P, 512], F32)) for b in range(4)]
    misc = [stack.enter_context(nc.psum_tensor(f"misc{b}", [P, 512], F32)) for b in range(4)]

    def sig(name):
        return Signal(nc, stack, name)

    raw_in = [sig(f"raw_in{j}") for j in range(2)]
    hi_done = sig("hi_done")
    lo_done = sig("lo_done")
    lo_pool = sig("lo_pool")
    tile_done = sig("tile_done")
    acc_free = [sig(f"acc_free{b}") for b in range(4)]
    V, A, G, T = (sig(n) for n in ("vector_step", "scalar_step", "pool_step", "tensor_step"))
    step_of = {V: dve, A: act, G: pool, T: pe}
    chains = (V, A, G, T)

    def wait(eng, *tokens):
        for t in tokens:
            if t is not None:
                eng.wait_ge(t[0], t[1])

    def v(f, *after, **k):
        wait(dve, *after)
        return V.on(f())

    def a(f, *after):
        wait(act, *after)
        return A.on(f())

    def g(f, *after):
        wait(pool, *after)
        return G.on(f())

    def latest(chain):
        return (chain.sem, chain.offset + chain.count)

    @contextmanager
    def loop(passes, **per):
        each = [per.get(n, 0) for n in "VAGT"]
        before = [c.count for c in chains]
        with nc.Fori(0, passes) as i:
            for c, n, k in zip(chains, each, before):
                c.offset, c.count = i * n + k, 0
            yield i
            got = [c.count for c in chains]
        for c, n, k in zip(chains, each, before):
            c.offset, c.count = 0, k + n * passes
        assert got == each, f"steps counted in a pass: {got}, stated: {each}"

    def earlier(token, steps):
        return (token[0], token[1] - steps)

    def view(t, offset, *dims):
        whole = t[:, :] if len(t.shape) == 2 else t[:, :, :]
        return bass.AP(whole.tensor, offset, [list(whole.ap[0])] + [list(d) for d in dims])

    def load(pair, j, src, first=False):
        if not first:
            for done in (lo_done, lo_pool):
                sp.wait_ge(done.sem, 2 * pair + j + 1)
        parts = src if isinstance(src, list) else [src]
        k, n = parts[0].shape[1], sum(part.shape[2] for part in parts)
        dst, c = raw[j][:, 0:k * n].rearrange("p (k n) -> p k n", k=k), 0
        for part in parts:
            wide = part.shape[2]
            sp.dma_start(dst[:, :, c:c + wide], part).then_inc(raw_in[j].sem, 64 * wide // n)
            c += wide

    def split(pair, j, tiles_before, width=SLAB):
        act.wait_ge(raw_in[j].sem, 64 * pair + 64)
        if tiles_before is not None:
            act.wait_ge(tile_done.sem, tiles_before)
        half, part = width // 2, width // 8 * 3
        for c in (slice(0, half), slice(half, width)):
            act.activation(w_hi[j][:, c], raw[j][:, c], ACT.Copy).then_inc(hi_done.sem, 1)
        for eng, halves_done, c, done in ((pool, 1, slice(0, part), lo_pool), (dve, 2, slice(part, width), lo_done)):
            eng.wait_ge(hi_done.sem, 4 * pair + 2 * j + halves_done)
            eng.tensor_tensor(w_lo[j][:, c], raw[j][:, c], w_hi[j][:, c].bitcast(F32),
                              ALU.subtract).then_inc(done.sem, 1)

    def weights(j, k, skip=0, n=None):
        n = SLAB // k if n is None else n
        return [w[j][:, 0:n * k].rearrange("p (k n) -> p k n", k=k) for w in (w_hi, w_lo)]

    def slab_ready(pair, j):
        for done in (lo_done, lo_pool):
            pe.wait_ge(done.sem, 2 * pair + j + 3)

    def project(q, b, w, cols, X, K):
        pe.wait_ge(acc_free[b].sem, q + 1)
        (wh, wl), (xh, xl) = w, X
        o = acc[b][:, 0:TOK]
        for k in range(K):
            pe.matmul(o, wh[:, k, cols:cols + P], xh[:, k, :], start=k == 0, stop=False)
            pe.matmul(o, wh[:, k, cols:cols + P], xl[:, k, :], start=False, stop=False)
            m = pe.matmul(o, wl[:, k, cols:cols + P], xh[:, k, :], start=False, stop=k == K - 1)
        m.then_inc(tile_done.sem, 1)

    def project_tokens(q, b, w, cols, width, X, K, half, at_col=0, first=True, last=True):
        if first:
            pe.wait_ge(acc_free[b].sem, q + 1)
        (wh, wl), (xh, xl) = w, X
        o = acc[b][:, at_col:at_col + width]
        ts = slice(half * P, half * P + P)
        for k in range(K):
            pe.matmul(o, xh[:, k, ts], wh[:, k, cols:cols + width], start=k == 0, stop=False)
            pe.matmul(o, xh[:, k, ts], wl[:, k, cols:cols + width], start=False, stop=False)
            m = pe.matmul(o, xl[:, k, ts], wh[:, k, cols:cols + width], start=False, stop=k == K - 1)
        if last:
            m.then_inc(tile_done.sem, 1)

    def complete(eng, q, b):
        eng.wait_ge(tile_done.sem, 4 * q + b + 1)

    def freed(q, b, instruction):
        instruction.then_inc(acc_free[b].sem, 1)
        return (acc_free[b].sem, q + 2)

    def rows(w, k):
        return w.rearrange("(k p) n -> p k n", k=k)

    w_pool_in = rows(h["pool_w_in"][0], KD)
    w_grp = h["pool_w_grp"][0]
    w_pool_out = rows(h["pool_w_out"][0], KI)
    w_hgrn_in = rows(h["hgrn_w_in"][0], KD)
    w_hgrn_out = rows(h["hgrn_w_out"][0], KI)
    w_in2 = rows(h["w_in_2"][0], KD)
    w_out2 = rows(h["w_out_2"][0], KD)
    w_up = rows(h["ffn_w_up_2"][0], KD)
    w_down = rows(h["ffn_w_down_2"][0], KF)
    w_ada = rows(h["ada_w_2"][0], KD)

    def pool_in(grp, gate):
        return w_pool_in[:, :, bass.ds(grp * 512 + gate * INNER, 512)]

    def pool_grp(grp):
        return w_grp[bass.ds(grp, 1)].rearrange("a (k p) n -> p (a k) n", k=4)

    def out_slab(w, n):
        return w[:, :, bass.ds(n * 256, 256)]

    def head_slab(i, j):
        n = 2 * i + j
        both = (3 - j) * INNER + i * 2 * P
        return [w_hgrn_in[:, :, bass.ds(c, wide)] for c, wide in
                ((n * P, P), (n * P + INNER, P), (both, 2 * P))]

    def up_slab(n):
        return [w_up[:, :, bass.ds(n * 256 + m * DFF, 256)] for m in range(2)]

    def down_slab(n):
        return w_down[:, :, bass.ds(n * P, P)]

    s_x, s_par, s_ctx, s_row, s_pad, s_bias, s_scr = (sig(n) for n in (
        "x_in", "parameters_in", "context_in", "rows_in", "padded_in", "bias_in", "scratch_out"))
    s_ada = [sig(f"ada_in{n}") for n in range(2)]

    rM.restart()
    x_tok = rM.new("x_tok", [2, D])
    par = [rM.new(f"par{n}", [P]) for n in range(3)]
    rR.restart()
    band = rR.new("band", [4, 384])
    iota_i = rM.new("iota_i", [16], I32)
    first = rM.new("first", [4, 16])
    mask_f = rM.new("mask_f", [7, 64])
    SQ = rM.new("SQ", [KD, TOK])

    sp.dma_start(x_tok[:, :, :], h["x"][0].rearrange("(a p) n -> p a n", a=2)).then_inc(s_x.sem, 16)
    place = {}
    n_par = 0
    for n, names in enumerate((
            ("norm_g", "pool_scale", "hgrn_lower_bounds", "hgrn_norm_g", "final_g", "c_2", "c_ctx_2",
             "norm1_g_2", "norm2_g_2", "final_norm_g_2"),
            ("ada_b_2", "cv_w_2", "cv_b_2", "cv_norm_g_2", "cv_norm_b_2"),
            ("ffn_conv_w_2", "ffn_conv_b_2"))):
        r = 0
        for name in names:
            src = h[name]
            s = src.shape
            flat = {1: "(r c) -> r c", 2: "a (r c) -> (a r) c", 3: "a b (r c) -> (a b r) c"}[len(s)]
            src = src.rearrange(flat, c=P)
            k = src.shape[0]
            sp.dma_start(par[n][r:r + k, :], src).then_inc(s_par.sem, 16)
            n_par += 1
            place[name] = (n, r, k)
            r += k

    def param(name, i=0, n=1):
        t, r, k = place[name]
        if isinstance(i, int):
            return table[t][:, r + i:r + i + n]
        return table[t][:, bass.ds(i + r, n)]

    one = g(lambda: pool.memset(ident[:, :], 0.0))
    ident_ok = g(lambda: pool.affine_select(out=ident[:, :], in_=ident[:, :], compare_op=ALU.not_equal, fill=1.0,
                                            base=0, pattern=[[-1, P]], channel_multiplier=1), one)
    ones_ok = v(lambda: dve.memset(ones[:, :], 1.0))
    v(lambda: dve.memset(block64[:, :], 0.0))
    z = v(lambda: dve.memset(sel8[:, :], 0.0))
    v(lambda: dve.memset(block64[0:64, 0:64], 1.0), z)
    v(lambda: dve.memset(block64[64:P, 64:P], 1.0))
    sel_ok = v(lambda: dve.memset(sel8[:, 7:8], 1.0))
    eps_ok = v(lambda: dve.memset(eps[:, :], EPS))
    for b in range(4):
        dve.sem_inc(acc_free[b].sem, 1)
    dve.sem_inc(lo_done.sem, 2)
    pool.sem_inc(lo_pool.sem, 2)

    m1 = g(lambda: pool.memset(mask_f[:, :, :], 1.0))
    for l in range(7):
        B = 1 << l
        mk = mask_f[:, l, :].rearrange("p (n b) -> p n b", b=B)
        t1 = g(lambda: pool.affine_select(out=mk, in_=mk, compare_op=ALU.is_ge, fill=0.0, base=0,
                                          pattern=[[-2 * B, 64 // B], [0, B]], channel_multiplier=1), m1)
        mask_ok = g(lambda: pool.affine_select(out=mk, in_=mk, compare_op=ALU.is_ge, fill=0.0, base=B - 1,
                                               pattern=[[2 * B, 64 // B], [0, B]], channel_multiplier=-1), t1)
    i1 = g(lambda: pool.iota(iota_i[:, :], pattern=[[1, 16]], base=1, channel_multiplier=0))
    for n in range(4):
        b1 = g(lambda: pool.memset(band[:, n, :], 1.0 / (2 << n)))
    for n in range(4):
        w = 2 << n
        for half, (c0, c1) in enumerate(((0, 256), (256, 384))):
            bb = band[:, n, c0:c1]
            b2 = g(lambda: pool.affine_select(out=bb, in_=bb, compare_op=ALU.is_ge, fill=0.0, base=0,
                                              pattern=[[1, c1 - c0]], channel_multiplier=-1), b1)
            b3 = g(lambda: pool.affine_select(out=bb, in_=bb, compare_op=ALU.is_ge, fill=0.0, base=w - 1,
                                              pattern=[[-1, c1 - c0]], channel_multiplier=1), b2)
    def roots(X, sq, ready, bank, *free):
        for k in range(KD):
            t = a(lambda: act.activation(sq[:, k, :], X[:, k, :], ACT.Square, bias=0.0), ready[k])
            wait(pe, t, *(free if k == 0 else ()))
            m = pe.matmul(misc[bank][:, 0:TOK], ones[:, :], sq[:, k, :], start=k == 0, stop=k == KD - 1)
        t = T.on(m)
        a(lambda: act.activation(eps[:, 1:2], eps[:, 0:1], ACT.Sqrt, bias=0.0), eps_ok)
        t = a(lambda: act.activation(rstd[:, 1, :], misc[bank][:, 0:TOK], ACT.Sqrt, bias=eps[:, 0:1], scale=1.0 / D), t)
        return v(lambda: dve.reciprocal(rstd[:, 0, :], rstd[:, 1, :]), t)

    def normed(X, xn, gain_of, ready):
        return [v(lambda: dve.scalar_tensor_tensor(out=xn[:, k, :], in0=X[:, k, :], scalar=gain_of(k),
                                                   in1=rstd[:, 0, :], op0=ALU.mult, op1=ALU.mult), ready)
                for k in range(KD)]

    def norm_in(X, xn, hi, lo, gain_of, shift_of, ready):
        rounded, done = [], []
        for k in range(KD + 2):
            if k < KD:
                t = v(lambda: dve.scalar_tensor_tensor(out=xn[:, k, :], in0=X[:, k, :], scalar=gain_of(k),
                                                       in1=rstd[:, 0, :], op0=ALU.mult, op1=ALU.mult), ready)
                shift = shift_of(k) if shift_of else 0.0
                rounded.append(a(lambda: act.activation(hi[:, k, :], xn[:, k, :], ACT.Identity, bias=shift), t))
            if k > 1:
                n = k - 2
                shift = shift_of(n) if shift_of else 0.0
                done.append(v(lambda: dve.scalar_tensor_tensor(out=lo[:, n, :], in0=xn[:, n, :], scalar=shift,
                                                               in1=hi[:, n, :].bitcast(F32), op0=ALU.add,
                                                               op1=ALU.subtract), rounded[n]))
        return done

    def turn_in(src, dst, arrived, frees):
        wait(pe, arrived, *frees)
        done = []
        for n, (half, kq) in enumerate(((0, 0), (1, 0), (0, 4), (1, 4))):
            for k in range(4):
                m = pe.transpose(misc[n][:, k * P:k * P + P],
                                 src[:, half, (kq + k) * P:(kq + k + 1) * P], ident[:, :])
            t = T.on(m)
            done.append(v(lambda: dve.tensor_copy(
                dst[:, kq:kq + 4, half * P:half * P + P],
                misc[n][:, :].rearrange("p (k t) -> p k t", k=4)), t))
        return [done[1 + 2 * (k // 4)] for k in range(KD)]

    x_ok = turn_in(x_tok, XT, (s_x.sem, 16), (ident_ok,))

    t = roots(XT, SQ, x_ok, 0, x_ok[-1])
    pe.wait_ge(s_par.sem, 16 * n_par)
    for n, wdt in enumerate((128, 116, 88)):
        m = pe.transpose(misc[3][:, n * P:n * P + wdt], par[n][0:wdt, :], ident[0:wdt, 0:wdt])
    par_t = T.on(m)
    for n, wdt in enumerate((128, 116, 88)):
        par_ok = v(lambda: dve.tensor_copy(table[n][:, :], misc[3][:, n * P:n * P + wdt]), par_t)

    wait(dve, par_ok)
    wait(act, par_ok)
    xn_ok = norm_in(XT, SQ, XH, XL, lambda k: param("norm_g", k), None, t)
    for n in range(4):
        f1 = v(lambda: dve.tensor_scalar(first[:, n, :], iota_i[:, :], float(2 << n), 0.5 ** (n + 1), ALU.min, ALU.mult),
               i1)
    f1 = v(lambda: dve.reciprocal(first[:, :, :], first[:, :, :]), f1)
    f1 = v(lambda: dve.tensor_tensor(band[:, :, 0:16], band[:, :, 0:16], first[:, :, :], ALU.mult), f1, b3)
    for c in (0, TOK):
        band_ok = v(lambda: dve.tensor_tensor(band[:, :, c:c + P], band[:, :, c:c + P],
                                              view(ident, 0, (0, 4), (1, P)), ALU.subtract), f1, ident_ok)
    v(lambda: dve.tensor_copy(mask_level[:, :, :], mask_f[:, :, :]), mask_ok)
    mask2_ok = v(lambda: dve.tensor_copy(mask_diag[:, :], ident[:, :]))

    ada_raw = [rR.new(f"ada_raw{n}", [4, 512]) for n in range(2)]
    ada_acc = rR.new("ada_acc", [3, 512])
    p_hi_at = rR.next
    p_hi = rR.new("p_hi", [4, TOK], F32R)
    p_lo = rR.new("p_lo", [4, TOK], F32R)
    v_tok = at(rM.start + (KF + KI) * TOK * 4, "v_tok", [2, 512])
    sg = at(rM.start + KI * TOK * 4, "sg", [4, TOK])
    rM.restart()
    MH = rM.new("MH", [KF, TOK], F32R)
    ML = rM.new("ML", [KF, TOK], F32R)

    def ada_load(eng, chunk, n, *after):
        wait(eng, *after)
        eng.dma_start(ada_raw[n][:, :, :], w_ada[:, 4 * n:4 * n + 4, bass.ds(chunk * 512, 512)])\
            .then_inc(s_ada[n].sem, 16)

    def ada(turn, accs, free):
        read, summed = [], {}
        for n in range(2):
            dve.wait_ge(s_ada[n].sem, 16 * turn + 16)
            for k in range(4 * n, 4 * n + 4):
                for m in accs:
                    w, o = ada_raw[n][:, k % 4, :], ada_acc[:, m, :]
                    s = silu_c[:, 8 * (m % 2) + k:8 * (m % 2) + k + 1]
                    if k == 0:
                        t = v(lambda: dve.tensor_scalar(o, w, s, None, ALU.mult), free)
                    else:
                        t = v(lambda: dve.scalar_tensor_tensor(out=o, in0=w, scalar=s, in1=o, op0=ALU.mult,
                                                               op1=ALU.add), summed[m])
                    summed[m] = t
            read.append(t)
        return read

    def ada_sum(accs, *after):
        wait(pe, *after)
        for m in accs:
            for n in range(4):
                ins = pe.matmul(misc[1][:, 4 * m + n:4 * m + n + 1], ada_acc[:, m, n * P:n * P + P],
                                ones[:, 0:1], start=True, stop=True)
        return T.on(ins)

    def ada_store(m, chunk, summed):
        tb, r, _ = place["ada_b_2"]
        d, bias = (mod, mod_ctx, mod)[m][:, bass.ds(chunk * 4, 4)], table[tb][:, bass.ds(chunk * 4 + r, 4)]
        return v(lambda: dve.tensor_tensor(d, misc[1][:, 4 * m:4 * m + 4], bias, ALU.add), summed)

    W8 = [weights(j, 8) for j in range(2)]
    W4 = [weights(j, 4, n=512) for j in range(2)]
    W16 = [weights(j, 16) for j in range(2)]
    W22 = [weights(j, KF, n=P) for j in range(2)]
    X = (XH, XL)

    split(0, 0, None)
    split(0, 1, None)

    r0 = param("hgrn_lower_bounds", 0, KI)
    r1 = param("hgrn_lower_bounds", KI, KI)
    t = v(lambda: dve.tensor_tensor(lb[:, 2, :], r0, r1, ALU.max), par_ok)
    v(lambda: dve.tensor_tensor(lb[:, 0, :], r0, lb[:, 2, :], ALU.subtract), t)
    t = v(lambda: dve.tensor_tensor(lb[:, 1, :], r1, lb[:, 2, :], ALU.subtract))
    t = a(lambda: act.activation(lb[:, 0:2, :], lb[:, 0:2, :], ACT.Exp, bias=0.0), t)
    t = v(lambda: dve.tensor_tensor(lb[:, 2, :], lb[:, 0, :], lb[:, 1, :], ALU.add), t)
    t = v(lambda: dve.reciprocal(lb[:, 2, :], lb[:, 2, :]), t)
    v(lambda: dve.tensor_tensor(lb[:, 3, :], lb[:, 0, :], lb[:, 2, :], ALU.mult), t)
    t = v(lambda: dve.tensor_tensor(lb[:, 1, :], lb[:, 1, :], lb[:, 2, :], ALU.mult), t)
    t = v(lambda: dve.tensor_tensor(lb[:, 0, :], lb[:, 3, :], lb[:, 1, :], ALU.add), t)
    t = v(lambda: dve.tensor_tensor(lb[:, 0, :], lb[:, 0, :], lb[:, 3, :], ALU.subtract), t)
    lb_ok = v(lambda: dve.tensor_scalar(lb[:, 1, :], lb[:, 0, :], -1.0, 1.0, ALU.mult, ALU.add), t)
    silu_ok = a(lambda: act.activation(silu_c[:, :], param("c_2", 0, 16), ACT.Silu, bias=0.0), par_ok)

    wait(pe, xn_ok[-1], band_ok)
    wait(dve, silu_ok)
    v(lambda: dve.memset(ada_acc[:, 2, :], 0.0))

    def pool_group(i, e):
        grp, q, turn = 2 * i + e, 6 * i + 3 * e, 4 * i + 2 * e
        for n, src in enumerate((pool_in(grp, 0), pool_in(grp, 1), pool_grp(grp))):
            u = 3 * e + n
            if n == 2:
                for b in range(2):
                    ada_load(sp, grp, b, (V.sem, latest(V)[1] - 4 * (1 - b)))
            load(3 * i + u // 2, u % 2, src)
        step = [(3 * i + (3 * e + n) // 2, (e + n) % 2) for n in range(3)]
        ahead = [(3 * i + (3 * e + n + 2) // 2, (e + n) % 2) for n in range(3)]

        slab_ready(*step[0])
        for b in range(4):
            project_tokens(q, b, W8[step[0][1]], (b // 2) * 256, 256, X, KD, b % 2)
        read = ada(turn, (0, 1), latest(T))
        wait(act, latest(T))
        for b in range(4):
            complete(act, q, b)
            f = (b // 2) * 256
            freed(q, b, act.activation(v_tok[:, b % 2, f:f + 256], acc[b][:, 0:256], ACT.Copy))
        split(*ahead[0], 4 * q + 4, 4 * 512)

        slab_ready(*step[1])
        pools = []
        for b in range(4):
            project(q + 1, b, W8[step[1][1]], b * P, X, KD)
            for f in ((0, 1), (2, 3), (), ())[b]:
                wait(pe, *((acc_free[n].sem, q + 2) for n in (2 * (f // 2), 2 * (f // 2) + 1)))
                o = misc[2 + f // 2][:, (f % 2) * TOK:(f % 2) * TOK + TOK]
                pe.matmul(o, v_tok[:, 0, f * P:f * P + P], band[:, bass.ds(grp, 1), 0:TOK],
                          start=True, stop=False)
                m = pe.matmul(o[:, P:TOK], v_tok[:, 1, f * P:f * P + P], band[:, bass.ds(grp, 1), TOK:384],
                              start=False, stop=True)
                if f % 2:
                    pools.append(T.on(m))
        summed = ada_sum((0, 1, 2), read[1])
        for n in range(2):
            pt = misc[2 + n][:, :].rearrange("p (k t) -> p k t", k=2)
            t = a(lambda: act.activation(p_hi[:, 2 * n:2 * n + 2, :], pt, ACT.Copy), pools[n])
            ada_load(act, 4 + grp, n, read[n])
            p_ok = v(lambda: dve.tensor_tensor(p_lo[:, 2 * n:2 * n + 2, :], pt,
                                               p_hi[:, 2 * n:2 * n + 2, :].bitcast(F32), ALU.subtract), t)
        wait(act, p_ok)
        for b in range(4):
            complete(act, q + 1, b)
            freed(q + 1, b, act.activation(sg[:, b, :], acc[b][:, 0:TOK], ACT.Silu, bias=0.0))
        ada_store(2, 3 + grp, summed)
        ada_store(0, grp, summed)
        ada_store(1, grp, summed)
        split(*ahead[1], 4 * q + 8)

        slab_ready(*step[2])
        wait(pe, p_ok)
        for b in range(4):
            project(q + 2, b, W4[step[2][1]], b * P, (p_hi, p_lo), 4)
        rounded = []
        for b in range(5):
            if b < 4:
                wait(dve, (acc_free[b].sem, q + 3))
                complete(dve, q + 2, b)
                t = freed(q + 2, b, dve.scalar_tensor_tensor(
                    out=sg[:, b, :], in0=acc[b][:, 0:TOK], scalar=param("pool_scale", 4 * grp + b, 1),
                    in1=sg[:, b, :], op0=ALU.mult, op1=ALU.mult))
                rounded.append(a(lambda: act.activation(MH[:, bass.ds(4 * grp + b, 1), :], sg[:, b, :], ACT.Copy), t))
            if b > 0:
                n = bass.ds(4 * grp + b - 1, 1)
                m_ok = v(lambda: dve.tensor_tensor(ML[:, n, :], sg[:, b - 1, :], MH[:, n, :].bitcast(F32),
                                                   ALU.subtract), rounded[b - 1])
        split(*ahead[2], 4 * q + 12)
        ada(turn + 1, (2,), summed)

    with loop(2, V=66, A=12, T=6) as i:
        pool_group(i, 0)
        pool_group(i, 1)
    m_ok = (V.sem, latest(V)[1] - 8)
    pair, q = 6, 12

    def out_projection(pair, q, w, gate=None, between=None, **per):
        with loop(2, **per) as i:
            for j in range(2):
                load(pair + i, j, out_slab(w, 2 * i + j))
                if between:
                    between.first(2 * i + j)
                slab_ready(pair + i, j)
                for n in range(2):
                    b = 2 * j + n
                    project(q + i, b, W16[j], n * P, (MH, ML), KI)
                    complete(dve, q + i, b)
                    x = XT[:, bass.ds(4 * i + b, 1), :]
                    freed(q + i, b, dve.tensor_tensor(x, acc[b][:, 0:TOK], x, ALU.add))
                split(pair + i + 1, j, 4 * (q + i) + 2 * j + 2)
                if between:
                    between.last(2 * i + j)
        return [(acc_free[k % 4].sem, q + 2 + k // 4) for k in range(KD)]

    wait(pe, m_ok)

    class LateAda:

        def first(n):
            for b in range(2):
                ada_load(act, 8 + n, b, (V.sem, latest(V)[1] - 4 * (1 - b)))

        def last(n):
            t = ada_store(2, 7 + n, ada_sum((2,), latest(V)))
            ada(8 + n, (2,), t)

    x_ok = out_projection(pair, q, w_pool_out, between=LateAda, V=18, T=2)
    last_chunk = latest(V)
    pair, q = pair + 2, q + 2

    SQ2 = at(p_hi_at, "SQ2", [KD, TOK])
    t = roots(XT, SQ2, x_ok, 0, latest(V))
    xn_ok = norm_in(XT, SQ2, XH, XL, lambda k: param("norm_g", KD + k), None, t)[-1]
    ada_store(2, 11, ada_sum((2,), last_chunk))
    wait(pe, xn_ok)

    rM.restart()
    KQ = rM.new("KQ", [LEVELS * 2, TOK])
    QK = [rM.new(f"QK{j}", [2, TOK]) for j in range(2)]
    DD = [rM.new(f"DD{j}", [2, TOK]) for j in range(2)]
    AT = [rM.new(f"AT{j}", [3, P]) for j in range(2)]
    VT = rM.new("VT", [2, 2 * P])
    sigma = rM.new("sigma", [2, TOK])
    gsig = rM.new("gsig", [2, TOK])
    rR.restart()
    O = rR.new("O", [HEADS + 2, TOK])
    SG = rR.new("SG", [HEADS, TOK])

    zs = x_ok[-1]
    for t0 in (KQ, *QK, *AT, VT):
        zs = g(lambda: pool.memset(t0[:, :, :], 0.0), zs)
    wait(pe, zs)
    wait(act, zs)
    wait(dve, zs)

    def score_matmuls(j):
        kk, qq = QK[j][:, 0, :], QK[j][:, 1, :]
        for n in range(2):
            pe.matmul(misc[0][:, n * P:n * P + P], kk[:, n * P:n * P + P], qq[:, n * P:n * P + P],
                      start=True, stop=True)
        col = 2 * P
        for l in range(7):
            B = 1 << l
            for n in range(2):
                bank, c = divmod(col, 512)
                lhs = kk[:, n * P:n * P + P] if l == 0 else KQ[:, 2 * l, n * P:n * P + P]
                rhs = view(KQ, (2 * l + 1) * TOK + n * P + B, (2 * B, 64 // B), (1, B))
                o = misc[bank][:, c:c + 64].rearrange("p (n b) -> p n b", b=B)
                pe.matmul(o, lhs, rhs, start=True, stop=True)
                col += 64
        bank, c = divmod(col, 512)
        return T.on(pe.matmul(misc[bank][:, c:c + P], KQ[:, 14, 0:P], KQ[:, 15, P:TOK], start=True, stop=True))

    def score_copies(j):
        md = view(mask_diag, 0, (0, 2), (1, P))
        t = v(lambda: dve.copy_predicated(AT[j][:, 0:3:2, :], md, misc[0][:, 0:2 * P].rearrange("p (n t) -> p n t", n=2)))
        col = 2 * P
        for l in range(7):
            B = 1 << l
            bank, c = divmod(col, 512)
            dims = [(2 * B, 64 // B), (1, B)]
            o = view(AT[j], B, (2 * P, 2), *dims)
            m = view(mask_level, l * 64, (0, 2), (B, 64 // B), (1, B))
            d = misc[bank][:, c:c + P].rearrange("p (n m b) -> p n m b", n=2, b=B)
            dve.drain()
            t = v(lambda: dve.copy_predicated(o, m, d))
            col += P
        bank, c = divmod(col, 512)
        return v(lambda: dve.tensor_copy(AT[j][:, 1, :], misc[bank][:, c:c + P]), t)

    def value_matmuls(j):
        o = misc[3][:, 0:TOK]
        c = slice(j * P, j * P + P)
        pe.matmul(o, VT[:, 0, c], AT[j][:, 0:2, :], start=True, stop=False)
        return T.on(pe.matmul(o[:, P:TOK], VT[:, 1, c], AT[j][:, 2, :], start=False, stop=True))

    def levels(j, ready):
        for l in range(LEVELS):
            B = 1 << l
            dims = [(2 * B, P // B), (TOK + B, 2), (1, B)]
            src, dec, o = view(QK[j], 0, *dims), view(DD[j], 0, *dims), view(KQ, l * 2 * TOK, *dims)
            made = v(lambda: dve.tensor_tensor(o, src, dec, ALU.mult), ready)
            if l < LEVELS - 1:
                other = view(DD[j], TOK + 2 * B - 1, (2 * B, P // B), (-B, 2), (0, B))
                ready = v(lambda: dve.tensor_tensor(dec, dec, other, ALU.mult))
        return made

    def head(i, j, q0, pair0):
        n, q, pair = 2 * i + j, q0 + 2 * i + j, pair0 + i
        load(pair, j, head_slab(i, j))
        before_v, before_a = latest(V), latest(A)
        o = view(ones, 0, (0, 2), (1, P))
        suffix = g(lambda: pool.tensor_tensor(DD[j][:, 0, :].rearrange("p (a t) -> p a t", a=2), o, o, ALU.mult),
                   before_v)

        slab_ready(pair, j)
        project(q, 0, W8[j], 0, X, KD)
        project(q, 1, W8[j], P, X, KD)
        wait(pe, before_v, before_a)
        if j == 0:
            wait(pe, *((acc_free[b].sem, q + 1) for b in (2, 3)))
        scored = score_matmuls(1 - j)
        o_done = value_matmuls(j)
        for b in (2, 3):
            if j == 0:
                project(q, b, W8[0], b * P, X, KD)
            else:
                project_tokens(q, b, W8[1], 2 * P, 2 * P, X, KD, b - 2)

        complete(act, q, 0)
        freed(q, 0, act.activation(QK[j][:, 1, :], acc[0][:, 0:TOK], ACT.Copy))
        complete(act, q, 1)
        wait(act, before_a)
        act.activation(sigma[:, 0, :], acc[1][:, 0:TOK], ACT.Sigmoid, bias=0.0, scale=-1.0)
        sig_ok = freed(q, 1, act.activation(sigma[:, 1, :], acc[1][:, 0:TOK], ACT.Sigmoid, bias=0.0))
        l0, l1 = lb[:, 0, bass.ds(n, 1)], lb[:, 1, bass.ds(n, 1)]
        wait(act, sig_ok)
        a(lambda: act.activation(QK[j][:, 0, :], sigma[:, 0, :], ACT.Copy, scale=l1))
        factors = a(lambda: act.activation(DD[j][:, 1, :], sigma[:, 1, :], ACT.Identity, bias=l0, scale=l1))
        a(lambda: act.activation(O[:, bass.ds(n, 1), :], misc[3][:, 0:TOK], ACT.Copy), o_done)
        g_ok = []
        for b in (2, 3):
            complete(act, q, b)
            if j == 0:
                g_ok.append(a(lambda: act.activation(gsig[:, b - 2, :], acc[b][:, 0:TOK], ACT.Sigmoid, bias=0.0)))
            else:
                freed(q, b, act.activation(VT[:, b - 2, :], acc[b][:, 0:TOK], ACT.Copy))

        wait(dve, factors, suffix, scored)
        levels(j, None)
        dve.drain()
        score_copies(1 - j)
        for b, ready in zip((2, 3), g_ok):
            wait(dve, ready)
            freed(q, b, dve.scalar_tensor_tensor(out=SG[:, bass.ds(n + b - 2, 1), :], in0=acc[b][:, 0:TOK],
                                                 scalar=param("hgrn_norm_g", n + b - 2, 1),
                                                 in1=gsig[:, b - 2, :], op0=ALU.mult, op1=ALU.mult))
        split(pair + 1, j, 4 * q + 4)

    VH = 2 * LEVELS - 1 + 9
    with loop(HEADS // 2, V=2 * VH, A=8, G=2, T=4) as i:
        head(i, 0, q, pair)
        head(i, 1, q, pair)
    pair, q = pair + HEADS // 2, q + HEADS
    wait(pe, latest(V), latest(A), *((acc_free[b].sem, q + 1) for b in (2, 3)))
    t = value_matmuls(0)
    scored = score_matmuls(1)
    a(lambda: act.activation(O[:, HEADS, :], misc[3][:, 0:TOK], ACT.Copy), t)
    wait(dve, scored)
    t = score_copies(1)
    wait(pe, t, latest(A))
    t = value_matmuls(1)
    o_ok = a(lambda: act.activation(O[:, HEADS + 1, :], misc[3][:, 0:TOK], ACT.Copy), t)

    rM.restart()
    OSQ = rM.new("OSQ", [HEADS, TOK])
    L8 = at(rM.start + KI * TOK * 4, "L8", [8, P])
    R8 = at(rM.start + (KF + KI) * TOK * 4, "R8", [2, 512])
    t = g(lambda: pool.memset(L8[0:8, :, :], 0.0), o_ok)
    sel_rows = g(lambda: pool.affine_select(out=L8[0:8, :, :], in_=L8[0:8, :, :], compare_op=ALU.not_equal,
                                            fill=1.0, base=0, pattern=[[-1, 8], [0, P]], channel_multiplier=1), t)
    wait(act, o_ok)
    for c in range(2):
        t = a(lambda: act.activation(OSQ[:, 8 * c:8 * c + 8, :], O[:, 2 + 8 * c:10 + 8 * c, :], ACT.Square, bias=0.0))
        wait(pe, t, sel_ok)
        for n in range(8):
            m = pe.matmul(misc[0][0:8, c * TOK:c * TOK + TOK], sel8[:, 7 - n:15 - n], OSQ[:, 8 * c + n, :],
                          start=n == 0, stop=n == 7)
        t = T.on(m)
    t = v(lambda: dve.tensor_scalar(R8[0:8, 0, :], misc[0][0:8, :], 1.0 / P, EPS, ALU.mult, ALU.add), t)
    t = a(lambda: act.activation(R8[0:8, 1, :], R8[0:8, 0, :], ACT.Sqrt, bias=0.0), t)
    root = v(lambda: dve.reciprocal(R8[0:8, 0, :], R8[0:8, 1, :]), t)
    rM.restart()
    MH = rM.new("MH_b", [KF, TOK], F32R)
    ML = rM.new("ML_b", [KF, TOK], F32R)
    wait(pe, root, sel_rows)
    wait(act, root)
    read = {0: root, 1: root}
    for n in range(0, HEADS, 2):
        b = (n // 2) % 2
        bank = misc[1 + b]
        wait(pe, read[b])
        for k in range(2):
            m = pe.matmul(bank[:, k * TOK:k * TOK + TOK], L8[0:8, (n + k) % 8, :],
                          R8[0:8, 0, (n // 8) * TOK:(n // 8) * TOK + TOK], start=True, stop=True)
        t = T.on(m)
        both = slice(n + 2, n + 4)
        pv = bank[:, :].rearrange("p (k t) -> p k t", k=2)
        read[b] = t = v(lambda: dve.tensor_tensor(O[:, both, :], O[:, both, :], pv, ALU.mult), t)
        t = v(lambda: dve.tensor_tensor(O[:, both, :], O[:, both, :], SG[:, n:n + 2, :], ALU.mult), t)
        t = a(lambda: act.activation(MH[:, n:n + 2, :], O[:, both, :], ACT.Copy), t)
        m_ok = v(lambda: dve.tensor_tensor(ML[:, n:n + 2, :], O[:, both, :], MH[:, n:n + 2, :].bitcast(F32),
                                           ALU.subtract), t)
    wait(pe, m_ok)
    x_ok = out_projection(pair, q, w_hgrn_out)
    pair, q = pair + 2, q + 2

    rM.restart()
    MIXH = rM.new("MIXH", [8, TOK], F32R)
    MIXL = rM.new("MIXL", [8, TOK], F32R)
    HCH = rM.new("HCH", [KD, TOK], F32R)
    HCL = rM.new("HCL", [KD, TOK], F32R)
    QT = rM.new("QT", [4, TOK])
    CP = rM.new("CP", [2, TOK + TAPS - 1])
    CA = rM.new("CA", [2, TOK])
    U = rM.new("U", [2, TOK])
    rR.restart()
    BIAS = rR.new("BIAS", [2, NA_HEADS, TOK])
    KT = rR.new("KT", [4, 2 * TOK])
    VV = rR.new("VV", [4, ATT])
    VG = rR.new("VG", [2, TOK])
    SR = rR.new("SR", [2, TOK])
    BS = rM.new("BS", [2, P])
    WS = rstd[:, :, :].rearrange("p a (b q) -> p (a b) q", b=2)
    c_tok = at(rM.start, "c_tok", [2, D])
    XC = at(rM.start + 8192, "XC", [KD, TOK])
    ws_in = at(rM.start + 32768, "ws_in", [4, P])
    SQ3 = at(rR.start + 16384, "SQ3", [KD, TOK])
    pad = at(rM.start + 36864, "pad", [P])
    REL = 31
    rpb = at(rM.start + 36864 + 512, "rpb", [REL])
    scratch = nc.dram_tensor("rpb_padded", (NA_HEADS * 15, P), F32, kind="Internal").ap()

    def cols2(n, width=512):
        return w_in2[:, :, n:n + width]

    load(pair, 0, cols2(2048))
    load(pair, 1, cols2(1536))
    for b in range(4):
        for eng in (sp, pool, act, dve, pe):
            eng.wait_ge(acc_free[b].sem, q + 1)
    sp.dma_start(c_tok[:, :, :], h["ctx_2"][0].rearrange("(a p) n -> p a n", a=2)).then_inc(s_ctx.sem, 16)

    def whole(name):
        return h[name].ap if False else h[name]

    def spread(name, offset, n, parts):
        return bass.AP(h[name].tensor, offset, [[0, parts], [1, n]])

    n_rows = 0
    for k, name in enumerate(("sg_norm_g_2", "sg_norm_b_2")):
        sp.dma_start(SR[:, k, :], spread(name, 0, 256, P)).then_inc(s_row.sem, 16)
        n_rows += 16
    for n in range(4):
        sp.dma_start(BS[64 * (n % 2):64 * (n % 2) + 64, n // 2, :], spread("sg_b_2", n * P, P, 64))\
          .then_inc(s_row.sem, 16)
        n_rows += 16
    sp.dma_start(ws_in[:, :, :], h["sg_w_2"][0].rearrange("g p q -> p g q")).then_inc(s_row.sem, 16)
    n_rows += 16
    sp.dma_start(rpb[0:120, :], h["na_rpb_2"].rearrange("a h r c -> (a h r) c")).then_inc(s_pad.sem, 16)
    t = g(lambda: pool.memset(pad[:, :], 0.0))
    back = view(rpb, REL - 1, (-1, REL))
    t = g(lambda: pool.tensor_copy(pad[0:120, 48:48 + REL], bass.AP(back.tensor, REL - 1, [[back.ap[0][0], 120], [-1, REL]])),
          t, (s_pad.sem, 16))
    wait(sp, t)
    sp.dma_start(scratch, pad[0:120, :]).then_inc(s_scr.sem, 16)
    sp.wait_ge(s_scr.sem, 16)
    n_bias = 0
    for r in range(4):
        for r2 in range(4):
            dst = BIAS[64 * (r % 2):64 * (r % 2) + 64, r // 2, :, (3 - r2) * GRID:(4 - r2) * GRID]
            src = bass.AP(scratch.tensor, (r2 - r + 7) * P, [[1, 64], [15 * P, NA_HEADS], [1, GRID]])
            sp.dma_start(dst, src).then_inc(s_bias.sem, 16)
            n_bias += 16
    pool.wait_ge(s_bias.sem, n_bias)
    for a0 in range(2):
        for r in range(2):
            part = BIAS[64 * r:64 * r + 64, a0, :, :].rearrange("p h (r c) -> p (h r) c", c=GRID)
            left, right = part[:, :, 16:64], part[:, :, 0:48]
            t = g(lambda: pool.affine_select(out=left, in_=left, compare_op=ALU.is_ge, fill=-1e30, base=55,
                                             pattern=[[0, 32], [-1, 48]], channel_multiplier=-1))
            bias_ok = g(lambda: pool.affine_select(out=right, in_=right, compare_op=ALU.is_ge, fill=-1e30,
                                                   base=-56, pattern=[[0, 32], [1, 48]],
                                                   channel_multiplier=1), t)

    wait(pool, bias_ok)

    for n, (gname, m0, s0) in enumerate((("norm1_g_2", mod, 8), ("norm1_g_2", mod_ctx, 8), ("norm2_g_2", mod, 32))):
        gain_ok = v(lambda: dve.scalar_tensor_tensor(out=gain[:, n, :], in0=m0[:, s0:s0 + 8], scalar=1.0,
                                                     in1=param(gname, 0, 8), op0=ALU.add, op1=ALU.mult))
    t = roots(XT, SQ3, x_ok, 0, latest(V))
    x_ok = normed(XT, XT, lambda k: param("final_g", k), t)
    t = roots(XT, SQ3, x_ok, 0, x_ok[0])
    wait(dve, gain_ok)
    xn_ok = norm_in(XT, SQ3, XH, XL, lambda k: gain[:, 0, k:k + 1], lambda k: mod[:, k:k + 1], t)
    HC = (HCH, HCL)

    for n, (c, j) in enumerate(((512, 0), (1024, 1), (0, 0))):
        load(pair + 1 + n // 2, j, cols2(c))
    load(pair + 2, 1, w_out2[:, :, 0:512])
    load(pair + 3, 0, w_out2[:, :, 512:1024])
    load(pair + 3, 1, up_slab(0))

    wait(pe, xn_ok[-1])
    slab_ready(pair, 0)
    for b in range(4):
        project(q, b, W8[0], b * P, X, KD)
    cz = v(lambda: dve.memset(CP[:, :, :], 0.0), (s_scr.sem, 16))
    for f in range(2):
        complete(act, q, 2 + f)
        t = freed(q, 2 + f, act.activation(CA[:, f, :], acc[2 + f][:, 0:TOK], ACT.Sigmoid, bias=0.0))
        wait(dve, t, cz)
        complete(dve, q, f)
        gated = freed(q, f, dve.tensor_tensor(CP[:, f, 15:15 + TOK], acc[f][:, 0:TOK], CA[:, f, :], ALU.mult))
    split(pair + 1, 0, 4 * q + 4)
    q += 1
    chain = [gated, gated]

    xc_ok = turn_in(c_tok, XC, (s_ctx.sem, 16), ())

    def conv(k0, k1):
        for k in range(k0, k1):
            for f in range(2):
                w, x = param("cv_w_2", 2 * k + f), CP[:, f, k:k + TOK]
                if k == 0:
                    chain[f] = v(lambda: dve.tensor_scalar(CA[:, f, :], x, w, param("cv_b_2", f), ALU.mult,
                                                           ALU.add), (acc_free[f].sem, q + 1), chain[f])
                else:
                    chain[f] = v(lambda: dve.scalar_tensor_tensor(out=CA[:, f, :], in0=x, scalar=w, in1=CA[:, f, :],
                                                                  op0=ALU.mult, op1=ALU.add), chain[f])

    def context():
        t = roots(XC, SQ3, xc_ok, 0, xc_ok[-1])
        return norm_in(XC, SQ3, HCH, HCL, lambda k: gain[:, 1, k:k + 1], lambda k: mod_ctx[:, k:k + 1], t)[-1]

    slab_ready(pair, 1)
    for b in range(2):
        project(q, b, W8[1], b * P, X, KD)
    for b in range(2):
        project_tokens(q, 2 + b, W8[1], 256, 256, X, KD, b)
    for b in range(2):
        complete(act, q, b)
        u_ok = freed(q, b, act.activation(U[:, b, :], acc[b][:, 0:TOK], ACT.Gelu_apprx_tanh, bias=0.0))
    split(pair + 1, 1, 4 * q + 4)
    hc_ok = context()
    pe.wait_ge(s_row.sem, n_rows)
    dve.wait_ge(s_row.sem, n_rows)
    wait(pe, hc_ok)
    for n in range(4):
        m = pe.transpose(misc[3][:, n * P:n * P + P], ws_in[:, n, :], ident[:, :])
    t = T.on(m)
    ws_ok = v(lambda: dve.tensor_copy(WS, misc[3][:, :].rearrange("p (g q) -> p g q", g=4)), t)
    conv(0, 8)
    for b in range(2):
        complete(act, q, 2 + b)
        t = freed(q, 2 + b, act.activation(VG[:, b, :], acc[2 + b][:, 0:TOK], ACT.Gelu_apprx_tanh, bias=0.0))
        t = v(lambda: dve.bn_stats(stats[:, b, 0:6], VG[:, b, :]), t)
        t = v(lambda: dve.bn_aggr(stats[:, b, 6:8], stats[:, b, 0:6]), t)
        t = v(lambda: dve.tensor_scalar(stats[:, b, 0:1], stats[:, b, 7:8], EPS, None, ALU.add), t)
        t = a(lambda: act.activation(stats[:, b, 1:2], stats[:, b, 0:1], ACT.Sqrt, bias=0.0), t)
        t = v(lambda: dve.reciprocal(stats[:, b, 2:3], stats[:, b, 1:2]), t)
        t = v(lambda: dve.tensor_scalar(VG[:, b, :], VG[:, b, :], stats[:, b, 6:7], stats[:, b, 2:3], ALU.subtract,
                                        ALU.mult), t)
        t = v(lambda: dve.tensor_tensor(VG[:, b, :], VG[:, b, :], SR[:, 0, :], ALU.mult), t)
        vg_ok = v(lambda: dve.tensor_tensor(VG[:, b, :], VG[:, b, :], SR[:, 1, :], ALU.add), t)
    q += 1

    slab_ready(pair + 1, 0)
    for who, xx in enumerate((X, HC)):
        if who:
            wait(pe, hc_ok)
        for b in range(4):
            project(q + who, b, W8[0], b * P, xx, KD)
            complete(act, q + who, b)
            k_ok = freed(q + who, b, act.activation(KT[:, b, who * TOK:who * TOK + TOK], acc[b][:, 0:TOK], ACT.Copy))
        if who == 0:
            wait(pe, vg_ok, ws_ok)
            for n in range(4):
                for half in range(2):
                    c = (n // 2) * TOK + half * P
                    m = pe.matmul(misc[0][64 * (n % 2):64 * (n % 2) + 64, c:c + P],
                                  VG[:, half, n * 64:n * 64 + 64], WS[:, n, :], start=True, stop=True)
            mixed = T.on(m)
    split(pair + 2, 0, 4 * q + 8)
    q += 2
    conv(8, 20)
    wait(dve, mixed, u_ok)
    mv = misc[0][:, :].rearrange("p (f a t) -> p f a t", f=2, a=2)
    uv = U[:, :, :].rearrange("p f (a t) -> p f a t", a=2)
    bsv = view(BS, 0, (P, 2), (0, 2), (1, P))
    t = v(lambda: dve.tensor_tensor(mv, mv, bsv, ALU.add))
    t = v(lambda: dve.tensor_tensor(uv, uv, mv, ALU.mult), t)
    t = a(lambda: act.activation(MIXH[:, 4:6, :], U[:, :, :], ACT.Copy), t)
    v(lambda: dve.tensor_tensor(MIXL[:, 4:6, :], U[:, :, :], MIXH[:, 4:6, :].bitcast(F32), ALU.subtract), t)

    slab_ready(pair + 1, 1)
    for b in range(4):
        project_tokens(q, b, W8[1], 0, 512, (X, HC)[b // 2], KD, b % 2)
        complete(act, q, b)
        v_ok = freed(q, b, act.activation(VV[:, b, :], acc[b][:, :], ACT.Copy))
    split(pair + 2, 1, 4 * q + 4)
    q += 1
    conv(20, TAPS)

    slab_ready(pair + 2, 0)
    for b in range(4):
        project(q, b, W8[0], b * P, X, KD)
        complete(act, q, b)
        q_ok = freed(q, b, act.activation(QT[:, b, :], acc[b][:, 0:TOK], ACT.Copy))
    split(pair + 3, 0, 4 * q + 4)
    q += 1

    caf = CA[:, :, :].rearrange("p f t -> p (f t)")
    rsf = rstd[:, :, :].rearrange("p f t -> p (f t)")

    def group_sum(src, *after):
        wait(pe, *after)
        return T.on(pe.matmul(acc[3][:, :], block64[:, :], src, start=True, stop=True))

    def group_norm():
        t = group_sum(caf, chain[0], chain[1], (acc_free[3].sem, q + 1))
        yield
        t = v(lambda: dve.scalar_tensor_tensor(out=caf, in0=acc[3][:, :], scalar=-1.0 / 64, in1=caf, op0=ALU.mult,
                                               op1=ALU.add), t)
        t = a(lambda: act.activation(rsf, caf, ACT.Square, bias=0.0), t)
        yield
        t = group_sum(rsf, t)
        yield
        t = a(lambda: act.activation(rsf, acc[3][:, :], ACT.Sqrt, bias=eps[:, 0:1], scale=1.0 / 64), t)
        t = v(lambda: dve.reciprocal(rsf, rsf), t)
        t = v(lambda: dve.tensor_tensor(caf, caf, rsf, ALU.mult), t)
        yield
        for f in range(2):
            t2 = v(lambda: dve.tensor_scalar(CA[:, f, :], CA[:, f, :], param("cv_norm_g_2", f),
                                             param("cv_norm_b_2", f), ALU.mult, ALU.add), t)
        t = a(lambda: act.activation(CA[:, :, :], CA[:, :, :], ACT.Silu, bias=0.0), t2)
        t = a(lambda: act.activation(MIXH[:, 6:8, :], CA[:, :, :], ACT.Copy), t)
        yield
        v(lambda: dve.tensor_tensor(MIXL[:, 6:8, :], CA[:, :, :], MIXH[:, 6:8, :].bitcast(F32), ALU.subtract), t)

    SS = [at(rM.start + 16384 + 2048 * n, f"SS{n}", [512]) for n in range(2)]
    EE = [at(rM.start + 20480 + 2048 * n, f"EE{n}", [512]) for n in range(2)]
    PT = [at(rM.start + 24576 + 4096 * n, f"PT{n}", [4, TOK]) for n in range(2)]
    wait(pe, q_ok, k_ok, v_ok)
    wait(dve, bias_ok, v_ok)
    scale = 0.125
    s_read, e_read = [None, None], [None, None]
    s_tok, p_tok, turned, pv_done = {}, {}, {}, {}

    def scores(n, half):
        r0 = 64 * (n % 2)
        wait(pe, s_read[half])
        s_tok[n, half] = T.on(pe.matmul(misc[half][:, :], QT[r0:r0 + 64, n // 2, half * P:half * P + P],
                                        KT[r0:r0 + 64, n // 2, :], start=True, stop=True))

    def view4(t, offset):
        whole = t[:, :, :, :]
        return bass.AP(whole.tensor, offset, [list(whole.ap[0]), [-1, TOK]])

    def softmax(n, half):
        S, E = SS[half], EE[half]
        t = v(lambda: dve.scalar_tensor_tensor(out=S[:, 0:TOK], in0=misc[half][:, 0:TOK], scalar=scale,
                                               in1=view4(BIAS, (half * NA_HEADS + n) * TOK + TOK - 1), op0=ALU.mult, op1=ALU.add), s_tok[n, half])
        t = s_read[half] = v(lambda: dve.tensor_scalar(S[:, TOK:512], misc[half][:, TOK:512], scale, None, ALU.mult))
        t = v(lambda: dve.tensor_reduce(soft[:, half, 0:1], S[:, :], AX_X, ALU.max, negate=True), t)
        wait(act, e_read[half])
        t = a(lambda: act.activation(E[:, :], S[:, :], ACT.Exp, bias=soft[:, half, 0:1],
                                     accum_out=soft[:, half, 1:2]), t)
        t = v(lambda: dve.reciprocal(soft[:, half, 2:3], soft[:, half, 1:2]), t)
        p_tok[n, half] = v(lambda: dve.tensor_scalar(E[:, :], E[:, :], soft[:, half, 2:3], None, ALU.mult), t)

    def turn(n, half):
        wait(pe, p_tok[n, half])
        if n > 0:
            wait(pe, turned[n - 1, half])
        for k in range(4):
            m = pe.transpose(misc[2 + half][:, k * P:k * P + P], EE[half][:, k * P:k * P + P], ident[:, :])
        e_read[half] = t = T.on(m)
        turned[n, half] = a(lambda: act.activation(
            PT[n % 2][:, :, half * P:half * P + P], misc[2 + half][:, :].rearrange("p (k t) -> p k t", k=4), ACT.Copy),
            t, pv_done.get(n - 2))

    def values(n):
        r0, b = 64 * (n % 2), n // 2
        wait(pe, turned[n, 0], turned[n, 1])
        if n % 2 == 0:
            pe.wait_ge(acc_free[b].sem, q + 1)
        for k in range(4):
            m = pe.matmul(acc[b][r0:r0 + 64, 0:TOK], VV[:, k, n * 64:n * 64 + 64], PT[n % 2][:, k, :],
                          start=k == 0, stop=k == 3)
        if n % 2 == 0:
            return T.on(m)
        m.then_inc(tile_done.sem, 1)
        return (tile_done.sem, 4 * q + b + 1)

    def finish(n):
        pv_done[n] = values(n)
        if n % 2:
            b = n // 2
            complete(act, q, b)
            t = a(lambda: act.activation(MIXH[:, b, :], acc[b][:, 0:TOK], ACT.Copy))
            wait(dve, t)
            return freed(q, b, dve.tensor_tensor(MIXL[:, b, :], acc[b][:, 0:TOK],
                                                 MIXH[:, b, :].bitcast(F32), ALU.subtract))

    steps = group_norm()
    scores(0, 0)
    scores(0, 1)
    for n in range(NA_HEADS):
        next(steps, None)
        for half in range(2):
            softmax(n, half)
            if n + 1 < NA_HEADS:
                scores(n + 1, half)
        for half in range(2):
            turn(n, half)
        if n > 0:
            finish(n - 1)
    mix_ok = finish(NA_HEADS - 1)
    q += 1

    x_ok = []
    wait(pe, mix_ok)
    for n in range(2):
        pr, j = pair + 2 + (n + 1) // 2, (n + 1) % 2
        slab_ready(pr, j)
        for b in range(4):
            project(q, b, W8[j], b * P, (MIXH, MIXL), KD)
            complete(dve, q, b)
            k = 4 * n + b
            x_ok.append(freed(q, b, dve.scalar_tensor_tensor(out=XT[:, k, :], in0=acc[b][:, 0:TOK],
                                                        scalar=mod[:, 16 + k:17 + k], in1=XT[:, k, :],
                                                        op0=ALU.mult, op1=ALU.add)))
        if n == 0:
            split(pair + 3, 1, 4 * q + 4)
            load(pair + 4, 0, up_slab(1))
        else:
            split(pair + 4, 0, 4 * q + 4)
            load(pair + 4, 1, up_slab(2))
        q += 1

    SQ4 = at(rR.start, "SQ4", [KD, TOK])
    GP = at(rR.start + 16384, "GP", [2, TOK + 2])
    GC = at(rR.start + 20480, "GC", [2, TOK])
    rM.restart()
    MH = rM.new("MH_c", [KF, TOK], F32R)
    ML = rM.new("ML_c", [KF, TOK], F32R)
    gz = v(lambda: dve.memset(GP[:, :, :], 0.0))
    t = roots(XT, SQ4, x_ok, 0, latest(V))
    xn_ok = norm_in(XT, SQ4, XH, XL, lambda k: gain[:, 2, k:k + 1], lambda k: mod[:, 24 + k:25 + k], t)
    wait(pe, xn_ok[-1])
    wait(act, gz)

    def up(pr, j, n, q, after=None):
        slab_ready(pr, j)
        before = latest(V)
        for b in range(4):
            project(q, b, W8[j], b * P, X, KD)
        for f in range(2):
            complete(act, q, f)
            wait(act, before)
            t = freed(q, f, act.activation(GP[:, f, 1:1 + TOK], acc[f][:, 0:TOK], ACT.Copy))
            k = 2 * n + f
            w = [param("ffn_conv_w_2", KF * tap + k, 1) for tap in range(3)]
            t = v(lambda: dve.tensor_scalar(GC[:, f, :], GP[:, f, 0:TOK], w[0], param("ffn_conv_b_2", k, 1),
                                            ALU.mult, ALU.add), t)
            for tap in (1, 2):
                t = v(lambda: dve.scalar_tensor_tensor(out=GC[:, f, :], in0=GP[:, f, tap:tap + TOK], scalar=w[tap],
                                                       in1=GC[:, f, :], op0=ALU.mult, op1=ALU.add), t)
            tt = a(lambda: act.activation(GC[:, f, :], GC[:, f, :], ACT.Silu, bias=0.0), t)
            wait(dve, tt)
            complete(dve, q, 2 + f)
            t = freed(q, 2 + f, dve.tensor_tensor(GC[:, f, :], GC[:, f, :], acc[2 + f][:, 0:TOK], ALU.mult))
        both = bass.ds(2 * n, 2)
        t = a(lambda: act.activation(MH[:, both, :], GC[:, :, :], ACT.Copy), t)
        t = v(lambda: dve.tensor_tensor(ML[:, both, :], GC[:, :, :], MH[:, both, :].bitcast(F32), ALU.subtract), t)
        split(pr + 1, j, 4 * q + 4)
        return t

    up(pair + 3, 1, 0, q)
    pair, q = pair + 4, q + 1
    with loop(5, V=14, A=6) as i:
        for j in range(2):
            up(pair + i, j, 1 + 2 * i + j, q + 2 * i + j)
    for i in range(3, 11):
        pr, j = pair + (i - 1) // 2, (i - 1) % 2
        load(pr, j, up_slab(i))
    wait(pe, latest(V))
    pair, q = pair + 5, q + 10
    tiles = 4 * q

    def down(i, j, ahead):
        n = 2 * i + j
        load(pair + i, j, down_slab(n))
        slab_ready(pair + i, j)
        pe.wait_ge(acc_free[j].sem, q + i + 1)
        (wh, wl) = W22[j]
        o = acc[j][:, 0:TOK]
        for k in range(KF):
            pe.matmul(o, wh[:, k, :], MH[:, k, :], start=k == 0, stop=False)
            pe.matmul(o, wh[:, k, :], ML[:, k, :], start=False, stop=False)
            m = pe.matmul(o, wl[:, k, :], MH[:, k, :], start=False, stop=k == KF - 1)
        m.then_inc(tile_done.sem, 1)
        dve.wait_ge(tile_done.sem, tiles + n + 1)
        x = XT[:, bass.ds(n, 1), :]
        freed(q, j, dve.scalar_tensor_tensor(out=x, in0=acc[j][:, 0:TOK], scalar=mod[:, bass.ds(40 + n, 1)],
                                             in1=x, op0=ALU.mult, op1=ALU.add))
        if ahead:
            split(pair + i + 1, j, tiles + n + 1, KF * P)

    with loop(3) as i:
        down(i, 0, True)
        down(i, 1, True)
    down(3, 0, False)
    down(3, 1, False)

    x_ok = [(acc_free[k % 2].sem, q + 2 + k // 2) for k in range(KD)]
    OT = at(rR.start + 24576, "OT", [2, D])
    t = roots(XT, SQ4, x_ok, 0, latest(V))
    xn_ok = normed(XT, SQ4, lambda k: param("final_norm_g_2", k), t)
    s_out = sig("out_stored")
    wait(pe, xn_ok[-1])
    for half in range(2):
        for kq in range(2):
            n = 2 * half + kq
            for k in range(4):
                m = pe.transpose(misc[n][:, k * P:k * P + P], SQ4[:, 4 * kq + k, half * P:half * P + P], ident[:, :])
            t = T.on(m)
            t = v(lambda: dve.tensor_copy(OT[:, half, kq * 512:kq * 512 + 512], misc[n][:, :]), t)
        wait(sp, t)
        sp.dma_start(out[0, half * P:half * P + P, :], OT[:, half, :]).then_inc(s_out.sem, 16)
    sp.wait_ge(s_out.sem, 32)


_INS = ["x", "norm_g", "pool_w_in", "pool_w_grp", "pool_scale", "pool_w_out", "hgrn_w_in",
        "hgrn_lower_bounds", "hgrn_norm_g", "hgrn_w_out", "final_g", "c_2", "ctx_2", "c_ctx_2",
        "ada_w_2", "ada_b_2", "norm1_g_2", "w_in_2", "na_rpb_2", "sg_norm_g_2", "sg_norm_b_2",
        "sg_w_2", "sg_b_2", "cv_w_2", "cv_b_2", "cv_norm_g_2", "cv_norm_b_2", "w_out_2",
        "norm2_g_2", "ffn_w_up_2", "ffn_conv_w_2", "ffn_conv_b_2", "ffn_w_down_2",
        "final_norm_g_2"]


def kernel(**inputs):
    import numpy as _np
    import concourse.bacc as _bacc
    from concourse.bass_utils import run_bass_kernel_spmd as _run

    nc = _bacc.Bacc("TRN2", target_bir_lowering=False, num_devices=1)
    arrays, args = {}, {}
    for name in _INS:
        a = _np.ascontiguousarray(inputs[name])
        arrays[f"in_{name}_dram"] = a
        args[name] = nc.dram_tensor(f"in_{name}_dram", a.shape, mybir.dt.from_np(a.dtype),
                                    kind="ExternalInput").ap()
    out = nc.dram_tensor("out_0_dram", (1, TOK, D), F32, kind="ExternalOutput").ap()
    build(nc, args, out)
    r = _run(nc, [arrays], core_ids=[0])
    return r.results[0]["out_0_dram"]
```

```python
from contextlib import ExitStack, contextmanager

import concourse.bass as bass
from concourse import mybir

P = 128
TOK = 256
D = 1024
KD = D // P
INNER = 2048
KI = INNER // P
HEADS = KI
ATT = 512
NA_HEADS = 8
DFF = 2816
KF = DFF // P
GRID = 64
TAPS = 31
SLAB = 4096
EPS = 1e-6
LEVELS = 8

F32 = mybir.dt.float32
F32R = mybir.dt.float32r
U8 = mybir.dt.uint8
I32 = mybir.dt.int32
ALU = mybir.AluOpType
ACT = mybir.ActivationFunctionType
AX_X = mybir.AxisListType.X


class Signal:

    def __init__(self, nc, stack, name):
        self.sem = stack.enter_context(nc.semaphore(name))
        self.count = 0
        self.offset = 0

    def on(self, instruction, k=1):
        instruction.then_inc(self.sem, k)
        self.count += k
        return (self.sem, self.offset + self.count)


def build(nc, h, out):
    stack = ExitStack()
    with stack:
        _build(nc, h, out, stack)


def _build(nc, h, out, stack):
    pe, act, dve, pool, sp = nc.tensor, nc.scalar, nc.vector, nc.gpsimd, nc.sync
    stack.enter_context(nc.allow_non_contiguous_dma(reason="short rows of parameters"))

    base = (nc.sbuf_base + 63) // 64 * 64
    top = [base]

    def at(offset, name, shape, dt=F32):
        return nc.alloc_sbuf_tensor_at(name, [P] + shape, dt, offset=offset)

    def size(shape, dt):
        n = 1
        for x in shape:
            n *= x
        return (n * (1 if dt == U8 else 4) + 31) // 32 * 32

    def fixed(name, shape, dt=F32):
        t = at(top[0], name, shape, dt)
        top[0] += size(shape, dt)
        return t

    class Region:

        def __init__(self, nbytes):
            self.start, self.end = top[0], top[0] + nbytes
            top[0] = self.end
            assert self.end <= nc.sbuf_usable_end, (self.end, nc.sbuf_usable_end)
            self.next = self.start

        def restart(self):
            self.next = self.start

        def new(self, name, shape, dt=F32):
            t = at(self.next, name, shape, dt)
            self.next += size(shape, dt)
            assert self.next <= self.end, (name, self.next - self.end)
            return t

    raw = [fixed(f"raw{j}", [SLAB]) for j in range(2)]
    w_hi = [fixed(f"w_hi{j}", [SLAB], F32R) for j in range(2)]
    w_lo = [fixed(f"w_lo{j}", [SLAB], F32R) for j in range(2)]
    XT = fixed("XT", [KD, TOK])
    XH = fixed("XH", [KD, TOK], F32R)
    XL = fixed("XL", [KD, TOK], F32R)
    ident = fixed("ident", [P])
    ones = fixed("ones", [P])
    block64 = fixed("block64", [P])
    sel8 = fixed("sel8", [15])
    table = [fixed(f"table{n}", [w]) for n, w in enumerate((128, 116, 88))]
    mod = fixed("mod", [48])
    mod_ctx = fixed("mod_ctx", [16])
    silu_c = fixed("silu_c", [16])
    lb = fixed("lb", [4, KI])
    gain = fixed("gain", [4, KD])
    mask_diag = fixed("mask_diag", [P], U8)
    mask_level = fixed("mask_level", [7, 64], U8)
    rstd = fixed("rstd", [2, TOK])
    eps = fixed("eps", [2])
    stats = fixed("stats", [2, 8])
    soft = fixed("soft", [2, 4])
    rM = Region(2 * KF * TOK * 4)
    rR = Region(nc.sbuf_usable_end - top[0])

    acc = [stack.enter_context(nc.psum_tensor(f"acc{b}", [P, 512], F32)) for b in range(4)]
    misc = [stack.enter_context(nc.psum_tensor(f"misc{b}", [P, 512], F32)) for b in range(4)]

    def sig(name):
        return Signal(nc, stack, name)

    raw_in = [sig(f"raw_in{j}") for j in range(2)]
    hi_done = sig("hi_done")
    lo_done = sig("lo_done")
    lo_pool = sig("lo_pool")
    tile_done = sig("tile_done")
    acc_free = [sig(f"acc_free{b}") for b in range(4)]
    V, A, G, T = (sig(n) for n in ("vector_step", "scalar_step", "pool_step", "tensor_step"))
    step_of = {V: dve, A: act, G: pool, T: pe}
    chains = (V, A, G, T)

    def wait(eng, *tokens):
        for t in tokens:
            if t is not None:
                eng.wait_ge(t[0], t[1])

    def v(f, *after, **k):
        wait(dve, *after)
        return V.on(f())

    def a(f, *after):
        wait(act, *after)
        return A.on(f())

    def g(f, *after):
        wait(pool, *after)
        return G.on(f())

    def latest(chain):
        return (chain.sem, chain.offset + chain.count)

    @contextmanager
    def loop(passes, **per):
        each = [per.get(n, 0) for n in "VAGT"]
        before = [c.count for c in chains]
        with nc.Fori(0, passes) as i:
            for c, n, k in zip(chains, each, before):
                c.offset, c.count = i * n + k, 0
            yield i
            got = [c.count for c in chains]
        for c, n, k in zip(chains, each, before):
            c.offset, c.count = 0, k + n * passes
        assert got == each, f"steps counted in a pass: {got}, stated: {each}"

    def view(t, offset, *dims):
        whole = t[(slice(None),) * len(t.shape)]
        return bass.AP(whole.tensor, offset, [list(whole.ap[0])] + [list(d) for d in dims])

    def load(pair, j, src):
        for done in (lo_done, lo_pool):
            sp.wait_ge(done.sem, 2 * pair + j + 1)
        parts = src if isinstance(src, list) else [src]
        k, n = parts[0].shape[1], sum(part.shape[2] for part in parts)
        dst, c = raw[j][:, 0:k * n].rearrange("p (k n) -> p k n", k=k), 0
        for part in parts:
            wide = part.shape[2]
            sp.dma_start(dst[:, :, c:c + wide], part).then_inc(raw_in[j].sem, 64 * wide // n)
            c += wide

    def split(pair, j, tiles_before, width=SLAB):
        act.wait_ge(raw_in[j].sem, 64 * pair + 64)
        if tiles_before is not None:
            act.wait_ge(tile_done.sem, tiles_before)
        halves = slice(0, width // 2), slice(width // 2, width)
        for c in halves:
            act.activation(w_hi[j][:, c], raw[j][:, c], ACT.Copy).then_inc(hi_done.sem, 1)
        for n, (eng, done) in enumerate(((pool, lo_pool), (dve, lo_done))):
            eng.wait_ge(hi_done.sem, 4 * pair + 2 * j + n + 1)
            eng.tensor_tensor(w_lo[j][:, halves[n]], raw[j][:, halves[n]], w_hi[j][:, halves[n]].bitcast(F32),
                              ALU.subtract).then_inc(done.sem, 1)

    def weights(j, k, n=None):
        n = SLAB // k if n is None else n
        return [w[j][:, 0:n * k].rearrange("p (k n) -> p k n", k=k) for w in (w_hi, w_lo)]

    def slab_ready(pair, j):
        for done in (lo_done, lo_pool):
            pe.wait_ge(done.sem, 2 * pair + j + 3)

    def project(q, b, w, cols, X, K, ready=None):
        pe.wait_ge(acc_free[b].sem, q + 1)
        (wh, wl), (xh, xl) = w, X
        o = acc[b][:, 0:TOK]
        for k in range(K):
            if ready:
                wait(pe, ready[k])
            pe.matmul(o, wh[:, k, cols:cols + P], xh[:, k, :], start=k == 0, stop=False)
            pe.matmul(o, wh[:, k, cols:cols + P], xl[:, k, :], start=False, stop=False)
            m = pe.matmul(o, wl[:, k, cols:cols + P], xh[:, k, :], start=False, stop=k == K - 1)
        m.then_inc(tile_done.sem, 1)

    def project_tokens(q, b, w, cols, width, X, K, half, at_col=0, first=True, last=True):
        if first:
            pe.wait_ge(acc_free[b].sem, q + 1)
        (wh, wl), (xh, xl) = w, X
        o = acc[b][:, at_col:at_col + width]
        ts = slice(half * P, half * P + P)
        for k in range(K):
            pe.matmul(o, xh[:, k, ts], wh[:, k, cols:cols + width], start=k == 0, stop=False)
            pe.matmul(o, xh[:, k, ts], wl[:, k, cols:cols + width], start=False, stop=False)
            m = pe.matmul(o, xl[:, k, ts], wh[:, k, cols:cols + width], start=False, stop=k == K - 1)
        if last:
            m.then_inc(tile_done.sem, 1)

    def complete(eng, q, b):
        eng.wait_ge(tile_done.sem, 4 * q + b + 1)

    def freed(q, b, instruction):
        instruction.then_inc(acc_free[b].sem, 1)
        return (acc_free[b].sem, q + 2)

    def rows(w, k):
        return w.rearrange("(k p) n -> p k n", k=k)

    w_pool_in = rows(h["pool_w_in"][0], KD)
    w_grp = h["pool_w_grp"][0]
    w_pool_out = rows(h["pool_w_out"][0], KI)
    w_hgrn_in = rows(h["hgrn_w_in"][0], KD)
    w_hgrn_out = rows(h["hgrn_w_out"][0], KI)
    w_in2 = rows(h["w_in_2"][0], KD)
    w_out2 = rows(h["w_out_2"][0], KD)
    w_up = rows(h["ffn_w_up_2"][0], KD)
    w_down = rows(h["ffn_w_down_2"][0], KF)
    w_ada = rows(h["ada_w_2"][0], KD)

    def pool_in(grp, gate):
        return w_pool_in[:, :, bass.ds(grp * 512 + gate * INNER, 512)]

    def pool_grp(grp):
        return w_grp[bass.ds(grp, 1)].rearrange("a (k p) n -> p (a k) n", k=4)

    def out_slab(w, n):
        return w[:, :, bass.ds(n * 256, 256)]

    def head_slab(i, j):
        n = 2 * i + j
        both = (3 - j) * INNER + i * 2 * P
        return [w_hgrn_in[:, :, bass.ds(c, wide)] for c, wide in
                ((n * P, P), (n * P + INNER, P), (both, 2 * P))]

    def up_slab(n):
        return [w_up[:, :, bass.ds(n * 256 + m * DFF, 256)] for m in range(2)]

    def down_slab(n):
        return w_down[:, :, bass.ds(n * P, P)]

    s_x, s_par, s_ctx, s_row, s_pad, s_bias, s_scr = (sig(n) for n in (
        "x_in", "parameters_in", "context_in", "rows_in", "padded_in", "bias_in", "scratch_out"))
    s_ada = [sig(f"ada_in{n}") for n in range(2)]

    rM.restart()
    x_tok = rM.new("x_tok", [2, D])
    par = [rM.new(f"par{n}", [P]) for n in range(3)]
    rR.restart()
    band = rR.new("band", [4, 384])
    iota_i = rM.new("iota_i", [16], I32)
    first = rM.new("first", [4, 16])
    mask_f = rM.new("mask_f", [7, 64])
    SQ = rM.new("SQ", [KD, TOK])

    sp.dma_start(x_tok[:, :, :], h["x"][0].rearrange("(a p) n -> p a n", a=2)).then_inc(s_x.sem, 16)
    place = {}
    n_par = 0
    for n, names in enumerate((
            ("norm_g", "pool_scale", "hgrn_lower_bounds", "hgrn_norm_g", "final_g", "c_2", "c_ctx_2",
             "norm1_g_2", "norm2_g_2", "final_norm_g_2"),
            ("ada_b_2", "cv_w_2", "cv_b_2", "cv_norm_g_2", "cv_norm_b_2"),
            ("ffn_conv_w_2", "ffn_conv_b_2"))):
        r = 0
        for name in names:
            src = h[name]
            s = src.shape
            flat = {1: "(r c) -> r c", 2: "a (r c) -> (a r) c", 3: "a b (r c) -> (a b r) c"}[len(s)]
            src = src.rearrange(flat, c=P)
            k = src.shape[0]
            sp.dma_start(par[n][r:r + k, :], src).then_inc(s_par.sem, 16)
            n_par += 1
            place[name] = (n, r, k)
            r += k

    def param(name, i=0, n=1):
        t, r, k = place[name]
        if isinstance(i, int):
            return table[t][:, r + i:r + i + n]
        return table[t][:, bass.ds(i + r, n)]

    one = g(lambda: pool.memset(ident[:, :], 0.0))
    ident_ok = g(lambda: pool.affine_select(out=ident[:, :], in_=ident[:, :], compare_op=ALU.not_equal, fill=1.0,
                                            base=0, pattern=[[-1, P]], channel_multiplier=1), one)
    ones_ok = v(lambda: dve.memset(ones[:, :], 1.0))
    v(lambda: dve.memset(block64[:, :], 0.0))
    z = v(lambda: dve.memset(sel8[:, :], 0.0))
    v(lambda: dve.memset(block64[0:64, 0:64], 1.0), z)
    v(lambda: dve.memset(block64[64:P, 64:P], 1.0))
    sel_ok = v(lambda: dve.memset(sel8[:, 7:8], 1.0))
    eps_ok = v(lambda: dve.memset(eps[:, :], EPS))
    for b in range(4):
        dve.sem_inc(acc_free[b].sem, 1)
    dve.sem_inc(lo_done.sem, 2)
    pool.sem_inc(lo_pool.sem, 2)

    m1 = g(lambda: pool.memset(mask_f[:, :, :], 1.0))
    for l in range(7):
        B = 1 << l
        mk = mask_f[:, l, :].rearrange("p (n b) -> p n b", b=B)
        t1 = g(lambda: pool.affine_select(out=mk, in_=mk, compare_op=ALU.is_ge, fill=0.0, base=0,
                                          pattern=[[-2 * B, 64 // B], [0, B]], channel_multiplier=1), m1)
        mask_ok = g(lambda: pool.affine_select(out=mk, in_=mk, compare_op=ALU.is_ge, fill=0.0, base=B - 1,
                                               pattern=[[2 * B, 64 // B], [0, B]], channel_multiplier=-1), t1)
    i1 = g(lambda: pool.iota(iota_i[:, :], pattern=[[1, 16]], base=1, channel_multiplier=0))
    for n in range(4):
        b1 = g(lambda: pool.memset(band[:, n, :], 1.0 / (2 << n)))
    for n in range(4):
        w = 2 << n
        for half, (c0, c1) in enumerate(((0, 256), (256, 384))):
            bb = band[:, n, c0:c1]
            b2 = g(lambda: pool.affine_select(out=bb, in_=bb, compare_op=ALU.is_ge, fill=0.0, base=0,
                                              pattern=[[1, c1 - c0]], channel_multiplier=-1), b1)
            b3 = g(lambda: pool.affine_select(out=bb, in_=bb, compare_op=ALU.is_ge, fill=0.0, base=w - 1,
                                              pattern=[[-1, c1 - c0]], channel_multiplier=1), b2)
    def roots(X, sq, ready, bank, *free):
        for k in range(KD):
            t = ready[k]
            if X is not None:
                t = a(lambda: act.activation(sq[:, k, :], X[:, k, :], ACT.Square, bias=0.0), t)
            wait(pe, t, *(free if k == 0 else ()))
            m = pe.matmul(misc[bank][:, 0:TOK], ones[:, :], sq[:, k, :], start=k == 0, stop=k == KD - 1)
        t = T.on(m)
        a(lambda: act.activation(eps[:, 1:2], eps[:, 0:1], ACT.Sqrt, bias=0.0), eps_ok)
        t = a(lambda: act.activation(rstd[:, 1, :], misc[bank][:, 0:TOK], ACT.Sqrt, bias=eps[:, 0:1], scale=1.0 / D), t)
        return v(lambda: dve.reciprocal(rstd[:, 0, :], rstd[:, 1, :]), t)

    def normed(X, xn, gain_of, ready):
        return [v(lambda: dve.scalar_tensor_tensor(out=xn[:, k, :], in0=X[:, k, :], scalar=gain_of(k),
                                                   in1=rstd[:, 0, :], op0=ALU.mult, op1=ALU.mult), ready)
                for k in range(KD)]

    def norm_in(X, xn, hi, lo, gain_of, shift_of, ready):
        rounded, done = [], []
        for k in range(KD + 2):
            if k < KD:
                t = v(lambda: dve.scalar_tensor_tensor(out=xn[:, k, :], in0=X[:, k, :], scalar=gain_of(k),
                                                       in1=rstd[:, 0, :], op0=ALU.mult, op1=ALU.mult), ready)
                shift = shift_of(k) if shift_of else 0.0
                rounded.append(a(lambda: act.activation(hi[:, k, :], xn[:, k, :], ACT.Identity, bias=shift), t))
            if k > 1:
                n = k - 2
                shift = shift_of(n) if shift_of else 0.0
                done.append(v(lambda: dve.scalar_tensor_tensor(out=lo[:, n, :], in0=xn[:, n, :], scalar=shift,
                                                               in1=hi[:, n, :].bitcast(F32), op0=ALU.add,
                                                               op1=ALU.subtract), rounded[n]))
        return done

    def turn_in(src, dst, arrived, frees):
        wait(pe, arrived, *frees)
        done = []
        for n, (half, kq) in enumerate(((0, 0), (1, 0), (0, 4), (1, 4))):
            for k in range(4):
                m = pe.transpose(misc[n][:, k * P:k * P + P],
                                 src[:, half, (kq + k) * P:(kq + k + 1) * P], ident[:, :])
            t = T.on(m)
            done.append(v(lambda: dve.tensor_copy(
                dst[:, kq:kq + 4, half * P:half * P + P],
                misc[n][:, :].rearrange("p (k t) -> p k t", k=4)), t))
        return [done[1 + 2 * (k // 4)] for k in range(KD)]

    x_ok = turn_in(x_tok, XT, (s_x.sem, 16), (ident_ok,))

    t = roots(XT, SQ, x_ok, 0, x_ok[-1])
    pe.wait_ge(s_par.sem, 16 * n_par)
    for n, wdt in enumerate((128, 116, 88)):
        m = pe.transpose(misc[3][:, n * P:n * P + wdt], par[n][0:wdt, :], ident[0:wdt, 0:wdt])
    par_t = T.on(m)
    for n, wdt in enumerate((128, 116, 88)):
        par_ok = v(lambda: dve.tensor_copy(table[n][:, :], misc[3][:, n * P:n * P + wdt]), par_t)

    wait(dve, par_ok)
    wait(act, par_ok)
    xn_ok = norm_in(XT, SQ, XH, XL, lambda k: param("norm_g", k), None, t)
    for n in range(4):
        f1 = v(lambda: dve.tensor_scalar(first[:, n, :], iota_i[:, :], float(2 << n), 0.5 ** (n + 1), ALU.min, ALU.mult),
               i1)
    f1 = v(lambda: dve.reciprocal(first[:, :, :], first[:, :, :]), f1)
    f1 = v(lambda: dve.tensor_tensor(band[:, :, 0:16], band[:, :, 0:16], first[:, :, :], ALU.mult), f1, b3)
    for c in (0, TOK):
        band_ok = v(lambda: dve.tensor_tensor(band[:, :, c:c + P], band[:, :, c:c + P],
                                              view(ident, 0, (0, 4), (1, P)), ALU.subtract), f1, ident_ok)
    v(lambda: dve.tensor_copy(mask_level[:, :, :], mask_f[:, :, :]), mask_ok)
    mask2_ok = v(lambda: dve.tensor_copy(mask_diag[:, :], ident[:, :]))

    ada_raw = [rR.new(f"ada_raw{n}", [4, 512]) for n in range(2)]
    ada_acc = rR.new("ada_acc", [3, 512])
    p_hi_at = rR.next
    p_hi = rR.new("p_hi", [4, TOK], F32R)
    p_lo = rR.new("p_lo", [4, TOK], F32R)
    v_tok = at(rM.start + (KF + KI) * TOK * 4, "v_tok", [2, 512])
    sg = at(rM.start + KI * TOK * 4, "sg", [4, TOK])
    rM.restart()
    MH = rM.new("MH", [KF, TOK], F32R)
    ML = rM.new("ML", [KF, TOK], F32R)

    def ada_load(eng, chunk, n, *after):
        wait(eng, *after)
        eng.dma_start(ada_raw[n][:, :, :], w_ada[:, 4 * n:4 * n + 4, bass.ds(chunk * 512, 512)])\
            .then_inc(s_ada[n].sem, 16)

    def ada(turn, accs, free):
        read, summed = [], {}
        for n in range(2):
            dve.wait_ge(s_ada[n].sem, 16 * turn + 16)
            for k in range(4 * n, 4 * n + 4):
                for m in accs:
                    w, o = ada_raw[n][:, k % 4, :], ada_acc[:, m, :]
                    s = silu_c[:, 8 * (m % 2) + k:8 * (m % 2) + k + 1]
                    if k == 0:
                        t = v(lambda: dve.tensor_scalar(o, w, s, None, ALU.mult), free)
                    else:
                        t = v(lambda: dve.scalar_tensor_tensor(out=o, in0=w, scalar=s, in1=o, op0=ALU.mult,
                                                               op1=ALU.add), summed[m])
                    summed[m] = t
            read.append(t)
        return read

    def ada_sum(accs, *after):
        wait(pe, *after)
        for m in accs:
            for n in range(4):
                ins = pe.matmul(misc[1][:, 4 * m + n:4 * m + n + 1], ada_acc[:, m, n * P:n * P + P],
                                ones[:, 0:1], start=True, stop=True)
        return T.on(ins)

    def ada_store(m, chunk, summed):
        tb, r, _ = place["ada_b_2"]
        d, bias = (mod, mod_ctx, mod)[m][:, bass.ds(chunk * 4, 4)], table[tb][:, bass.ds(chunk * 4 + r, 4)]
        return v(lambda: dve.tensor_tensor(d, misc[1][:, 4 * m:4 * m + 4], bias, ALU.add), summed)

    W8 = [weights(j, 8) for j in range(2)]
    W4 = [weights(j, 4, n=512) for j in range(2)]
    W16 = [weights(j, 16) for j in range(2)]
    W22 = [weights(j, KF, n=P) for j in range(2)]
    X = (XH, XL)

    split(0, 0, None)
    split(0, 1, None)

    r0 = param("hgrn_lower_bounds", 0, KI)
    r1 = param("hgrn_lower_bounds", KI, KI)
    t = v(lambda: dve.tensor_tensor(lb[:, 2, :], r0, r1, ALU.max), par_ok)
    v(lambda: dve.tensor_tensor(lb[:, 0, :], r0, lb[:, 2, :], ALU.subtract), t)
    t = v(lambda: dve.tensor_tensor(lb[:, 1, :], r1, lb[:, 2, :], ALU.subtract))
    t = a(lambda: act.activation(lb[:, 0:2, :], lb[:, 0:2, :], ACT.Exp, bias=0.0), t)
    t = v(lambda: dve.tensor_tensor(lb[:, 2, :], lb[:, 0, :], lb[:, 1, :], ALU.add), t)
    t = v(lambda: dve.reciprocal(lb[:, 2, :], lb[:, 2, :]), t)
    v(lambda: dve.tensor_tensor(lb[:, 3, :], lb[:, 0, :], lb[:, 2, :], ALU.mult), t)
    t = v(lambda: dve.tensor_tensor(lb[:, 1, :], lb[:, 1, :], lb[:, 2, :], ALU.mult), t)
    t = v(lambda: dve.tensor_tensor(lb[:, 0, :], lb[:, 3, :], lb[:, 1, :], ALU.add), t)
    t = v(lambda: dve.tensor_tensor(lb[:, 0, :], lb[:, 0, :], lb[:, 3, :], ALU.subtract), t)
    lb_ok = v(lambda: dve.tensor_scalar(lb[:, 1, :], lb[:, 0, :], -1.0, 1.0, ALU.mult, ALU.add), t)
    silu_ok = a(lambda: act.activation(silu_c[:, :], param("c_2", 0, 16), ACT.Silu, bias=0.0), par_ok)

    wait(pe, xn_ok[-1], band_ok)
    wait(dve, silu_ok)
    v(lambda: dve.memset(ada_acc[:, 2, :], 0.0))

    def pool_group(i, e):
        grp, q, turn = 2 * i + e, 6 * i + 3 * e, 4 * i + 2 * e
        for n, src in enumerate((pool_in(grp, 0), pool_in(grp, 1), pool_grp(grp))):
            u = 3 * e + n
            if n == 2:
                for b in range(2):
                    ada_load(sp, grp, b, (V.sem, latest(V)[1] - 4 * (1 - b)))
            load(3 * i + u // 2, u % 2, src)
        step = [(3 * i + (3 * e + n) // 2, (e + n) % 2) for n in range(3)]
        ahead = [(3 * i + (3 * e + n + 2) // 2, (e + n) % 2) for n in range(3)]

        slab_ready(*step[0])
        for b in range(4):
            project_tokens(q, b, W8[step[0][1]], (b // 2) * 256, 256, X, KD, b % 2)
        read = ada(turn, (0, 1), latest(T))
        wait(act, latest(T))
        for b in range(4):
            complete(act, q, b)
            f = (b // 2) * 256
            freed(q, b, act.activation(v_tok[:, b % 2, f:f + 256], acc[b][:, 0:256], ACT.Copy))
        split(*ahead[0], 4 * q + 4, 4 * 512)

        slab_ready(*step[1])
        pools = []
        for b in range(4):
            project(q + 1, b, W8[step[1][1]], b * P, X, KD)
            for f in ((0, 1), (2, 3), (), ())[b]:
                wait(pe, *((acc_free[n].sem, q + 2) for n in (2 * (f // 2), 2 * (f // 2) + 1)))
                o = misc[2 + f // 2][:, (f % 2) * TOK:(f % 2) * TOK + TOK]
                pe.matmul(o, v_tok[:, 0, f * P:f * P + P], band[:, bass.ds(grp, 1), 0:TOK],
                          start=True, stop=False)
                m = pe.matmul(o[:, P:TOK], v_tok[:, 1, f * P:f * P + P], band[:, bass.ds(grp, 1), TOK:384],
                              start=False, stop=True)
                if f % 2:
                    pools.append(T.on(m))
        for n in range(2):
            pt = misc[2 + n][:, :].rearrange("p (k t) -> p k t", k=2)
            t = a(lambda: act.activation(p_hi[:, 2 * n:2 * n + 2, :], pt, ACT.Copy), pools[n])
            ada_load(act, 4 + grp, n, read[n])
            p_ok = v(lambda: dve.tensor_tensor(p_lo[:, 2 * n:2 * n + 2, :], pt,
                                               p_hi[:, 2 * n:2 * n + 2, :].bitcast(F32), ALU.subtract), t)
        wait(act, p_ok)
        for b in range(4):
            complete(act, q + 1, b)
            freed(q + 1, b, act.activation(sg[:, b, :], acc[b][:, 0:TOK], ACT.Silu, bias=0.0))
        split(*ahead[1], 4 * q + 8)

        slab_ready(*step[2])
        wait(pe, p_ok)
        for b in range(4):
            project(q + 2, b, W4[step[2][1]], b * P, (p_hi, p_lo), 4)
        summed = ada_sum((0, 1, 2), read[1])
        rounded = []
        for b in range(5):
            if b < 4:
                wait(dve, (acc_free[b].sem, q + 3))
                complete(dve, q + 2, b)
                t = freed(q + 2, b, dve.scalar_tensor_tensor(
                    out=sg[:, b, :], in0=acc[b][:, 0:TOK], scalar=param("pool_scale", 4 * grp + b, 1),
                    in1=sg[:, b, :], op0=ALU.mult, op1=ALU.mult))
                rounded.append(a(lambda: act.activation(MH[:, bass.ds(4 * grp + b, 1), :], sg[:, b, :], ACT.Copy), t))
            if b > 0:
                n = bass.ds(4 * grp + b - 1, 1)
                m_ok = v(lambda: dve.tensor_tensor(ML[:, n, :], sg[:, b - 1, :], MH[:, n, :].bitcast(F32),
                                                   ALU.subtract), rounded[b - 1])
        ada_store(2, 3 + grp, summed)
        ada_store(0, grp, summed)
        summed = ada_store(1, grp, summed)
        split(*ahead[2], 4 * q + 12)
        ada(turn + 1, (2,), summed)

    with loop(2, V=66, A=12, T=6) as i:
        pool_group(i, 0)
        pool_group(i, 1)
    m_ok = (V.sem, latest(V)[1] - 8)
    pair, q = 6, 12

    def out_projection(pair, q, w, sq, before=None, after=None, ready=None, **per):
        first = latest(A)[1]
        with loop(2, **per) as i:
            for j in range(2):
                load(pair + i, j, out_slab(w, 2 * i + j))
                if before:
                    before(2 * i + j)
                slab_ready(pair + i, j)
                for n in range(2):
                    b = 2 * j + n
                    project(q + i, b, W16[j], n * P, (MH, ML), KI, ready if b == 0 else None)
                    complete(dve, q + i, b)
                    x = XT[:, bass.ds(4 * i + b, 1), :]
                    t = freed(q + i, b, dve.tensor_tensor(x, acc[b][:, 0:TOK], x, ALU.add))
                    a(lambda: act.activation(sq[:, bass.ds(4 * i + b, 1), :], x, ACT.Square, bias=0.0), t)
                split(pair + i + 1, j, 4 * (q + i) + 2 * j + 2)
                if after:
                    after(2 * i + j)
        return [(A.sem, first + 1 + k) for k in range(KD)]

    wait(pe, m_ok)

    def late_load(n):
        for b in range(2):
            ada_load(act, 8 + n, b, (V.sem, latest(V)[1] - 4 * (1 - b)))

    def late_sum(n):
        t = ada_store(2, 7 + n, ada_sum((2,), latest(V)))
        ada(8 + n, (2,), t)

    SQ2 = at(p_hi_at, "SQ2", [KD, TOK])
    squares = out_projection(pair, q, w_pool_out, SQ2, before=late_load, after=late_sum, V=18, A=4, T=2)
    last_chunk = latest(V)
    pair, q = pair + 2, q + 2

    t = roots(None, SQ2, squares, 0)
    xn_ok = norm_in(XT, SQ2, XH, XL, lambda k: param("norm_g", KD + k), None, t)[-1]
    ada_store(2, 11, ada_sum((2,), last_chunk))
    wait(pe, xn_ok)

    rM.restart()
    KQ = rM.new("KQ", [LEVELS * 2, TOK])
    QK = [rM.new(f"QK{j}", [2, TOK]) for j in range(2)]
    DD = [rM.new(f"DD{j}", [2, TOK]) for j in range(2)]
    AT = [rM.new(f"AT{j}", [3, P]) for j in range(2)]
    VT = rM.new("VT", [2, 2 * P])
    sigma = rM.new("sigma", [2, TOK])
    gsig = rM.new("gsig", [2, TOK])
    rR.restart()
    O = rR.new("O", [HEADS + 2, TOK])
    SG = rR.new("SG", [HEADS, TOK])

    zs = squares[-1]
    for t0 in (KQ, *QK, *AT, VT):
        zs = g(lambda: pool.memset(t0[:, :, :], 0.0), zs)
    wait(pe, zs)
    wait(act, zs)
    wait(dve, zs)

    def score_matmuls(j):
        kk, qq = QK[j][:, 0, :], QK[j][:, 1, :]
        for n in range(2):
            pe.matmul(misc[0][:, n * P:n * P + P], kk[:, n * P:n * P + P], qq[:, n * P:n * P + P],
                      start=True, stop=True)
        col = 2 * P
        for l in range(7):
            B = 1 << l
            for n in range(2):
                bank, c = divmod(col, 512)
                lhs = kk[:, n * P:n * P + P] if l == 0 else KQ[:, 2 * l, n * P:n * P + P]
                rhs = view(KQ, (2 * l + 1) * TOK + n * P + B, (2 * B, 64 // B), (1, B))
                o = misc[bank][:, c:c + 64].rearrange("p (n b) -> p n b", b=B)
                pe.matmul(o, lhs, rhs, start=True, stop=True)
                col += 64
        bank, c = divmod(col, 512)
        return T.on(pe.matmul(misc[bank][:, c:c + P], KQ[:, 14, 0:P], KQ[:, 15, P:TOK], start=True, stop=True))

    def score_copies(j):
        md = view(mask_diag, 0, (0, 2), (1, P))
        diagonal = misc[0][:, 0:2 * P].rearrange("p (n t) -> p n t", n=2)
        t = v(lambda: dve.copy_predicated(AT[j][:, 0:3:2, :], md, diagonal))
        col = 2 * P
        for l in range(7):
            B = 1 << l
            bank, c = divmod(col, 512)
            dims = [(2 * B, 64 // B), (1, B)]
            o = view(AT[j], B, (2 * P, 2), *dims)
            m = view(mask_level, l * 64, (0, 2), (B, 64 // B), (1, B))
            d = misc[bank][:, c:c + P].rearrange("p (n m b) -> p n m b", n=2, b=B)
            dve.drain()
            t = v(lambda: dve.copy_predicated(o, m, d))
            col += P
        bank, c = divmod(col, 512)
        return v(lambda: dve.tensor_copy(AT[j][:, 1, :], misc[bank][:, c:c + P]), t)

    def value_matmuls(j):
        o = misc[3][:, 0:TOK]
        c = slice(j * P, j * P + P)
        pe.matmul(o, VT[:, 0, c], AT[j][:, 0:2, :], start=True, stop=False)
        return T.on(pe.matmul(o[:, P:TOK], VT[:, 1, c], AT[j][:, 2, :], start=False, stop=True))

    def levels(j, ready):
        for l in range(LEVELS):
            B = 1 << l
            dims = [(2 * B, P // B), (TOK + B, 2), (1, B)]
            src, dec, o = view(QK[j], 0, *dims), view(DD[j], 0, *dims), view(KQ, l * 2 * TOK, *dims)
            made = v(lambda: dve.tensor_tensor(o, src, dec, ALU.mult), ready)
            if l < LEVELS - 1:
                other = view(DD[j], TOK + 2 * B - 1, (2 * B, P // B), (-B, 2), (0, B))
                ready = v(lambda: dve.tensor_tensor(dec, dec, other, ALU.mult))
        return made

    def head(i, j, q0, pair0):
        n, q, pair = 2 * i + j, q0 + 2 * i + j, pair0 + i
        load(pair, j, head_slab(i, j))
        before_v, before_a = latest(V), latest(A)
        o = view(ones, 0, (0, 2), (1, P))
        suffix = g(lambda: pool.tensor_tensor(DD[j][:, 0, :].rearrange("p (a t) -> p a t", a=2), o, o, ALU.mult),
                   before_v)

        slab_ready(pair, j)
        project(q, 0, W8[j], 0, X, KD)
        project(q, 1, W8[j], P, X, KD)
        wait(pe, before_v, before_a)
        if j == 0:
            wait(pe, *((acc_free[b].sem, q + 1) for b in (2, 3)))
        scored = score_matmuls(1 - j)
        o_done = value_matmuls(j)
        for b in (2, 3):
            if j == 0:
                project(q, b, W8[0], b * P, X, KD)
            else:
                project_tokens(q, b, W8[1], 2 * P, 2 * P, X, KD, b - 2)

        complete(act, q, 0)
        freed(q, 0, act.activation(QK[j][:, 1, :], acc[0][:, 0:TOK], ACT.Copy))
        complete(act, q, 1)
        wait(act, before_a)
        act.activation(sigma[:, 0, :], acc[1][:, 0:TOK], ACT.Sigmoid, bias=0.0, scale=-1.0)
        sig_ok = freed(q, 1, act.activation(sigma[:, 1, :], acc[1][:, 0:TOK], ACT.Sigmoid, bias=0.0))
        l0, l1 = lb[:, 0, bass.ds(n, 1)], lb[:, 1, bass.ds(n, 1)]
        wait(act, sig_ok)
        a(lambda: act.activation(QK[j][:, 0, :], sigma[:, 0, :], ACT.Copy, scale=l1))
        factors = a(lambda: act.activation(DD[j][:, 1, :], sigma[:, 1, :], ACT.Identity, bias=l0, scale=l1))
        a(lambda: act.activation(O[:, bass.ds(n, 1), :], misc[3][:, 0:TOK], ACT.Copy), o_done)
        g_ok = []
        for b in (2, 3):
            complete(act, q, b)
            if j == 0:
                g_ok.append(a(lambda: act.activation(gsig[:, b - 2, :], acc[b][:, 0:TOK], ACT.Sigmoid, bias=0.0)))
            else:
                freed(q, b, act.activation(VT[:, b - 2, :], acc[b][:, 0:TOK], ACT.Copy))

        wait(dve, factors, suffix, scored)
        levels(j, None)
        dve.drain()
        score_copies(1 - j)
        for b, ready in zip((2, 3), g_ok):
            wait(dve, ready)
            freed(q, b, dve.scalar_tensor_tensor(out=SG[:, bass.ds(n + b - 2, 1), :], in0=acc[b][:, 0:TOK],
                                                 scalar=param("hgrn_norm_g", n + b - 2, 1),
                                                 in1=gsig[:, b - 2, :], op0=ALU.mult, op1=ALU.mult))
        split(pair + 1, j, 4 * q + 4)

    VH = 2 * LEVELS - 1 + 9
    with loop(HEADS // 2, V=2 * VH, A=8, G=2, T=4) as i:
        head(i, 0, q, pair)
        head(i, 1, q, pair)
    pair, q = pair + HEADS // 2, q + HEADS

    OSQ = [at(rM.start + 36864, "OSQ0", [8, TOK]), at(rM.start + 8192, "OSQ1", [8, TOK])]
    L8 = at(rM.start + 16384, "L8", [8, P])

    def head_squares(c, heads):
        return {n: a(lambda: act.activation(OSQ[c][:, n, :], O[:, 2 + 8 * c + n, :], ACT.Square, bias=0.0))
                for n in heads}

    def head_sums(c, squared):
        wait(pe, (acc_free[c].sem, q + 1))
        for n in range(8):
            wait(pe, squared[n])
            m = pe.matmul(acc[c][0:8, 0:TOK], sel8[:, 7 - n:15 - n], OSQ[c][:, n, :], start=n == 0, stop=n == 7)
        return T.on(m)

    def head_roots(c, t):
        t = a(lambda: act.activation(rstd[0:8, c, :], acc[c][0:8, 0:TOK], ACT.Sqrt, bias=eps[0:8, 0:1],
                                     scale=1.0 / P), t)
        return v(lambda: dve.reciprocal(rstd[0:8, c, :], rstd[0:8, c, :]), t)

    wait(pe, latest(V), latest(A), *((acc_free[b].sem, q + 1) for b in (2, 3)))
    t = value_matmuls(0)
    scored = score_matmuls(1)
    o_read = a(lambda: act.activation(O[:, HEADS, :], misc[3][:, 0:TOK], ACT.Copy), t)
    wait(act, o_read)
    squared = head_squares(0, range(8))
    summed = head_sums(0, squared)
    t = g(lambda: pool.memset(L8[0:8, :, :], 0.0), scored)
    sel_rows = g(lambda: pool.affine_select(out=L8[0:8, :, :], in_=L8[0:8, :, :], compare_op=ALU.not_equal,
                                            fill=1.0, base=0, pattern=[[-1, 8], [0, P]], channel_multiplier=1), t)
    wait(dve, scored)
    t = score_copies(1)
    wait(pe, t, o_read)
    t = value_matmuls(1)

    def gate(n):
        return v(lambda: dve.tensor_tensor(SG[:, n:n + 2, :], SG[:, n:n + 2, :], O[:, n + 2:n + 4, :], ALU.mult))

    gated = {n: gate(n) for n in range(0, HEADS - 2, 2)}
    wait(act, scored)
    squared = head_squares(1, range(7))
    root = [head_roots(0, summed)]
    o_ok = a(lambda: act.activation(O[:, HEADS + 1, :], misc[3][:, 0:TOK], ACT.Copy), t)
    wait(act, o_ok)
    squared |= head_squares(1, (7,))
    root.append(head_roots(1, head_sums(1, squared)))

    rM.restart()
    MH = rM.new("MH_b", [KF, TOK], F32R)
    ML = rM.new("ML_b", [KF, TOK], F32R)
    wait(pe, sel_rows)
    wait(dve, o_ok)
    gated[HEADS - 2] = gate(HEADS - 2)
    read, rounded, m_ok = {}, {}, []
    for n in range(0, HEADS + 2, 2):
        if n < HEADS:
            b = (n // 2) % 2
            bank = misc[1 + b]
            wait(pe, root[n // 8], read.get(b))
            for k in range(2):
                m = pe.matmul(bank[:, k * TOK:k * TOK + TOK], L8[0:8, (n + k) % 8, :],
                              rstd[0:8, n // 8, :], start=True, stop=True)
            t = T.on(m)
            pv = bank[:, :].rearrange("p (k t) -> p k t", k=2)
            read[b] = t = v(lambda: dve.tensor_tensor(SG[:, n:n + 2, :], SG[:, n:n + 2, :], pv, ALU.mult), t, gated[n])
            rounded[n] = a(lambda: act.activation(MH[:, n:n + 2, :], SG[:, n:n + 2, :], ACT.Copy), t)
        if n > 0:
            e = slice(n - 2, n)
            m_ok += [v(lambda: dve.tensor_tensor(ML[:, e, :], SG[:, e, :], MH[:, e, :].bitcast(F32),
                                                 ALU.subtract), rounded[n - 2])] * 2
    SQ3 = at(rR.start + 16384, "SQ3", [KD, TOK])
    squares = out_projection(pair, q, w_hgrn_out, SQ3, ready=m_ok, A=4)
    pair, q = pair + 2, q + 2

    rM.restart()
    MIXH = rM.new("MIXH", [8, TOK], F32R)
    MIXL = rM.new("MIXL", [8, TOK], F32R)
    HCH = rM.new("HCH", [KD, TOK], F32R)
    HCL = rM.new("HCL", [KD, TOK], F32R)
    QT = rM.new("QT", [4, TOK])
    CP = rM.new("CP", [2, TOK + TAPS - 1])
    CA = rM.new("CA", [2, TOK])
    U = rM.new("U", [2, TOK])
    rR.restart()
    BIAS = rR.new("BIAS", [2, NA_HEADS, TOK])
    KT = rR.new("KT", [4, 2 * TOK])
    VV = rR.new("VV", [4, ATT])
    VG = rR.new("VG", [2, TOK])
    SR = rR.new("SR", [2, TOK])
    BS = rM.new("BS", [2, P])
    WS = rstd[:, :, :].rearrange("p a (b q) -> p (a b) q", b=2)
    c_tok = at(rM.start, "c_tok", [2, D])
    XC = at(rM.start + 8192, "XC", [KD, TOK])
    ws_in = at(rM.start + 32768, "ws_in", [4, P])
    pad = at(rM.start + 36864, "pad", [P])
    REL = 31
    rpb = at(rM.start + 36864 + 512, "rpb", [REL])
    scratch = nc.dram_tensor("rpb_padded", (NA_HEADS * 15, P), F32, kind="Internal").ap()

    def cols2(n, width=512):
        return w_in2[:, :, n:n + width]

    load(pair, 0, cols2(2048))
    load(pair, 1, cols2(1536))
    for b in range(4):
        for eng in (sp, pool, act, dve, pe):
            eng.wait_ge(acc_free[b].sem, q + 1)
    sp.dma_start(c_tok[:, :, :], h["ctx_2"][0].rearrange("(a p) n -> p a n", a=2)).then_inc(s_ctx.sem, 16)

    def spread(name, offset, n, parts):
        return bass.AP(h[name].tensor, offset, [[0, parts], [1, n]])

    n_rows = 0
    for k, name in enumerate(("sg_norm_g_2", "sg_norm_b_2")):
        sp.dma_start(SR[:, k, :], spread(name, 0, 256, P)).then_inc(s_row.sem, 16)
        n_rows += 16
    for n in range(4):
        sp.dma_start(BS[64 * (n % 2):64 * (n % 2) + 64, n // 2, :], spread("sg_b_2", n * P, P, 64))\
          .then_inc(s_row.sem, 16)
        n_rows += 16
    sp.dma_start(ws_in[:, :, :], h["sg_w_2"][0].rearrange("g p q -> p g q")).then_inc(s_row.sem, 16)
    n_rows += 16
    sp.dma_start(rpb[0:120, :], h["na_rpb_2"].rearrange("a h r c -> (a h r) c")).then_inc(s_pad.sem, 16)
    t = g(lambda: pool.memset(pad[:, :], 0.0))
    back = rpb[0:120, :]
    back = bass.AP(back.tensor, REL - 1, [list(back.ap[0]), [-1, REL]])
    t = g(lambda: pool.tensor_copy(pad[0:120, 48:48 + REL], back), t, (s_pad.sem, 16))
    wait(sp, t)
    sp.dma_start(scratch, pad[0:120, :]).then_inc(s_scr.sem, 16)
    sp.wait_ge(s_scr.sem, 16)
    n_bias = 0
    for r in range(4):
        for r2 in range(4):
            dst = BIAS[64 * (r % 2):64 * (r % 2) + 64, r // 2, :, (3 - r2) * GRID:(4 - r2) * GRID]
            src = bass.AP(scratch.tensor, (r2 - r + 7) * P, [[1, 64], [15 * P, NA_HEADS], [1, GRID]])
            sp.dma_start(dst, src).then_inc(s_bias.sem, 16)
            n_bias += 16
    pool.wait_ge(s_bias.sem, n_bias)
    for a0 in range(2):
        for r in range(2):
            part = BIAS[64 * r:64 * r + 64, a0, :, :].rearrange("p h (r c) -> p (h r) c", c=GRID)
            left, right = part[:, :, 16:64], part[:, :, 0:48]
            t = g(lambda: pool.affine_select(out=left, in_=left, compare_op=ALU.is_ge, fill=-1e30, base=55,
                                             pattern=[[0, 32], [-1, 48]], channel_multiplier=-1))
            bias_ok = g(lambda: pool.affine_select(out=right, in_=right, compare_op=ALU.is_ge, fill=-1e30,
                                                   base=-56, pattern=[[0, 32], [1, 48]],
                                                   channel_multiplier=1), t)

    wait(pool, bias_ok)

    for n, (gname, m0, s0) in enumerate((("norm1_g_2", mod, 8), ("norm1_g_2", mod_ctx, 8), ("norm2_g_2", mod, 32))):
        gain_ok = v(lambda: dve.scalar_tensor_tensor(out=gain[:, n, :], in0=m0[:, s0:s0 + 8], scalar=1.0,
                                                     in1=param(gname, 0, 8), op0=ALU.add, op1=ALU.mult))
    t = roots(None, SQ3, squares, 0)
    x_ok = normed(XT, XT, lambda k: param("final_g", k), t)
    t = roots(XT, SQ3, x_ok, 0, x_ok[0])
    wait(dve, gain_ok)
    xn_ok = norm_in(XT, SQ3, XH, XL, lambda k: gain[:, 0, k:k + 1], lambda k: mod[:, k:k + 1], t)
    HC = (HCH, HCL)

    for n, (c, j) in enumerate(((512, 0), (1024, 1), (0, 0))):
        load(pair + 1 + n // 2, j, cols2(c))
    load(pair + 2, 1, w_out2[:, :, 0:512])
    load(pair + 3, 0, w_out2[:, :, 512:1024])
    load(pair + 3, 1, up_slab(0))

    slab_ready(pair, 0)
    for b in range(4):
        project(q, b, W8[0], b * P, X, KD, xn_ok if b == 0 else None)
    cz = v(lambda: dve.memset(CP[:, :, :], 0.0), (s_scr.sem, 16))
    for f in range(2):
        complete(act, q, 2 + f)
        t = freed(q, 2 + f, act.activation(CA[:, f, :], acc[2 + f][:, 0:TOK], ACT.Sigmoid, bias=0.0))
        wait(dve, t, cz)
        complete(dve, q, f)
        gated = freed(q, f, dve.tensor_tensor(CP[:, f, 15:15 + TOK], acc[f][:, 0:TOK], CA[:, f, :], ALU.mult))
    split(pair + 1, 0, 4 * q + 4)
    q += 1
    chain = [gated, gated]

    xc_ok = turn_in(c_tok, XC, (s_ctx.sem, 16), ())

    def conv(k0, k1):
        for k in range(k0, k1):
            for f in range(2):
                w, x = param("cv_w_2", 2 * k + f), CP[:, f, k:k + TOK]
                if k == 0:
                    chain[f] = v(lambda: dve.tensor_scalar(CA[:, f, :], x, w, param("cv_b_2", f), ALU.mult,
                                                           ALU.add), (acc_free[f].sem, q + 1), chain[f])
                else:
                    chain[f] = v(lambda: dve.scalar_tensor_tensor(out=CA[:, f, :], in0=x, scalar=w, in1=CA[:, f, :],
                                                                  op0=ALU.mult, op1=ALU.add), chain[f])

    def context():
        t = roots(XC, SQ3, xc_ok, 0, xc_ok[-1])
        return norm_in(XC, SQ3, HCH, HCL, lambda k: gain[:, 1, k:k + 1], lambda k: mod_ctx[:, k:k + 1], t)[-1]

    slab_ready(pair, 1)
    for b in range(2):
        project(q, b, W8[1], b * P, X, KD)
    for b in range(2):
        project_tokens(q, 2 + b, W8[1], 256, 256, X, KD, b)
    for b in range(2):
        complete(act, q, b)
        u_ok = freed(q, b, act.activation(U[:, b, :], acc[b][:, 0:TOK], ACT.Gelu_apprx_tanh, bias=0.0))
    split(pair + 1, 1, 4 * q + 4)
    hc_ok = context()
    pe.wait_ge(s_row.sem, n_rows)
    dve.wait_ge(s_row.sem, n_rows)
    wait(pe, xc_ok[-1])
    for n in range(4):
        m = pe.transpose(misc[3][:, n * P:n * P + P], ws_in[:, n, :], ident[:, :])
    t = T.on(m)
    ws_ok = v(lambda: dve.tensor_copy(WS, misc[3][:, :].rearrange("p (g q) -> p g q", g=4)), t)
    conv(0, 8)
    for b in range(2):
        complete(act, q, 2 + b)
        t = freed(q, 2 + b, act.activation(VG[:, b, :], acc[2 + b][:, 0:TOK], ACT.Gelu_apprx_tanh, bias=0.0))
        t = v(lambda: dve.bn_stats(stats[:, b, 0:6], VG[:, b, :]), t)
        t = v(lambda: dve.bn_aggr(stats[:, b, 6:8], stats[:, b, 0:6]), t)
        t = v(lambda: dve.tensor_scalar(stats[:, b, 0:1], stats[:, b, 7:8], EPS, None, ALU.add), t)
        t = a(lambda: act.activation(stats[:, b, 1:2], stats[:, b, 0:1], ACT.Sqrt, bias=0.0), t)
        t = v(lambda: dve.reciprocal(stats[:, b, 2:3], stats[:, b, 1:2]), t)
        t = v(lambda: dve.tensor_scalar(VG[:, b, :], VG[:, b, :], stats[:, b, 6:7], stats[:, b, 2:3], ALU.subtract,
                                        ALU.mult), t)
        t = v(lambda: dve.tensor_tensor(VG[:, b, :], VG[:, b, :], SR[:, 0, :], ALU.mult), t)
        vg_ok = v(lambda: dve.tensor_tensor(VG[:, b, :], VG[:, b, :], SR[:, 1, :], ALU.add), t)
    q += 1

    slab_ready(pair + 1, 0)
    for who, xx in enumerate((X, HC)):
        if who:
            wait(pe, hc_ok)
        for b in range(4):
            project(q + who, b, W8[0], b * P, xx, KD)
            complete(act, q + who, b)
            k_ok = freed(q + who, b, act.activation(KT[:, b, who * TOK:who * TOK + TOK], acc[b][:, 0:TOK], ACT.Copy))
        if who == 0:
            wait(pe, vg_ok, ws_ok)
            for n in range(4):
                for half in range(2):
                    c = (n // 2) * TOK + half * P
                    m = pe.matmul(misc[0][64 * (n % 2):64 * (n % 2) + 64, c:c + P],
                                  VG[:, half, n * 64:n * 64 + 64], WS[:, n, :], start=True, stop=True)
            mixed = T.on(m)
    split(pair + 2, 0, 4 * q + 8)
    q += 2
    conv(8, 20)
    wait(dve, mixed, u_ok)
    mv = misc[0][:, :].rearrange("p (f a t) -> p f a t", f=2, a=2)
    uv = U[:, :, :].rearrange("p f (a t) -> p f a t", a=2)
    bsv = view(BS, 0, (P, 2), (0, 2), (1, P))
    t = v(lambda: dve.tensor_tensor(mv, mv, bsv, ALU.add))
    t = v(lambda: dve.tensor_tensor(uv, uv, mv, ALU.mult), t)
    t = a(lambda: act.activation(MIXH[:, 4:6, :], U[:, :, :], ACT.Copy), t)
    v(lambda: dve.tensor_tensor(MIXL[:, 4:6, :], U[:, :, :], MIXH[:, 4:6, :].bitcast(F32), ALU.subtract), t)

    slab_ready(pair + 1, 1)
    for b in range(4):
        project_tokens(q, b, W8[1], 0, 512, (X, HC)[b // 2], KD, b % 2)
        complete(act, q, b)
        v_ok = freed(q, b, act.activation(VV[:, b, :], acc[b][:, :], ACT.Copy))
    split(pair + 2, 1, 4 * q + 4)
    q += 1
    conv(20, TAPS)

    slab_ready(pair + 2, 0)
    for b in range(4):
        project(q, b, W8[0], b * P, X, KD)
        complete(act, q, b)
        q_ok = freed(q, b, act.activation(QT[:, b, :], acc[b][:, 0:TOK], ACT.Copy))
    split(pair + 3, 0, 4 * q + 4)
    q += 1

    caf = CA[:, :, :].rearrange("p f t -> p (f t)")
    rsf = rstd[:, :, :].rearrange("p f t -> p (f t)")

    def group_sum(src, *after):
        wait(pe, *after)
        return T.on(pe.matmul(acc[3][:, :], block64[:, :], src, start=True, stop=True))

    def group_norm():
        t = group_sum(caf, chain[0], chain[1], (acc_free[3].sem, q + 1))
        yield
        t = v(lambda: dve.scalar_tensor_tensor(out=caf, in0=acc[3][:, :], scalar=-1.0 / 64, in1=caf, op0=ALU.mult,
                                               op1=ALU.add), t)
        t = a(lambda: act.activation(rsf, caf, ACT.Square, bias=0.0), t)
        yield
        t = group_sum(rsf, t)
        yield
        t = a(lambda: act.activation(rsf, acc[3][:, :], ACT.Sqrt, bias=eps[:, 0:1], scale=1.0 / 64), t)
        t = v(lambda: dve.reciprocal(rsf, rsf), t)
        t = v(lambda: dve.tensor_tensor(caf, caf, rsf, ALU.mult), t)
        yield
        for f in range(2):
            t2 = v(lambda: dve.tensor_scalar(CA[:, f, :], CA[:, f, :], param("cv_norm_g_2", f),
                                             param("cv_norm_b_2", f), ALU.mult, ALU.add), t)
        t = a(lambda: act.activation(CA[:, :, :], CA[:, :, :], ACT.Silu, bias=0.0), t2)
        t = a(lambda: act.activation(MIXH[:, 6:8, :], CA[:, :, :], ACT.Copy), t)
        yield
        v(lambda: dve.tensor_tensor(MIXL[:, 6:8, :], CA[:, :, :], MIXH[:, 6:8, :].bitcast(F32), ALU.subtract), t)

    SS = [at(rM.start + 16384 + 2048 * n, f"SS{n}", [512]) for n in range(2)]
    EE = [at(rM.start + 20480 + 2048 * n, f"EE{n}", [512]) for n in range(2)]
    PT = [at(rM.start + 24576 + 4096 * n, f"PT{n}", [4, TOK]) for n in range(2)]
    wait(pe, q_ok, k_ok, v_ok)
    wait(dve, bias_ok, v_ok)
    scale = 0.125
    s_read, e_read, e_tok = [None, None], [None, None], [None, None]
    s_tok, p_tok, turned, pv_done = {}, {}, {}, {}

    def scores(n, half):
        r0 = 64 * (n % 2)
        wait(pe, s_read[half])
        s_tok[n, half] = T.on(pe.matmul(misc[half][:, :], QT[r0:r0 + 64, n // 2, half * P:half * P + P],
                                        KT[r0:r0 + 64, n // 2, :], start=True, stop=True))

    def softmax(n, half):
        S, E = SS[half], EE[half]
        bias = view(BIAS, (half * NA_HEADS + n) * TOK + TOK - 1, (-1, TOK))
        t = v(lambda: dve.scalar_tensor_tensor(out=S[:, 0:TOK], in0=misc[half][:, 0:TOK], scalar=scale,
                                               in1=bias, op0=ALU.mult, op1=ALU.add), s_tok[n, half])
        t = s_read[half] = v(lambda: dve.tensor_scalar(S[:, TOK:512], misc[half][:, TOK:512], scale, None, ALU.mult))
        t = v(lambda: dve.tensor_reduce(soft[:, half, 0:1], S[:, :], AX_X, ALU.max, negate=True), t)
        wait(act, e_read[half])
        e_tok[half] = a(lambda: act.activation(E[:, :], S[:, :], ACT.Exp, bias=soft[:, half, 0:1],
                                               accum_out=soft[:, half, 1:2]), t)

    def normalize(n, half):
        E = EE[half]
        t = v(lambda: dve.reciprocal(soft[:, half, 2:3], soft[:, half, 1:2]), e_tok[half])
        p_tok[n, half] = v(lambda: dve.tensor_scalar(E[:, :], E[:, :], soft[:, half, 2:3], None, ALU.mult), t)

    def turn(n, half):
        wait(pe, p_tok[n, half])
        if n > 0:
            wait(pe, turned[n - 1, half])
        for k in range(4):
            m = pe.transpose(misc[2 + half][:, k * P:k * P + P], EE[half][:, k * P:k * P + P], ident[:, :])
        e_read[half] = t = T.on(m)
        turned[n, half] = a(lambda: act.activation(
            PT[n % 2][:, :, half * P:half * P + P], misc[2 + half][:, :].rearrange("p (k t) -> p k t", k=4), ACT.Copy),
            t, pv_done.get(n - 2))

    def values(n):
        r0, b = 64 * (n % 2), n // 2
        wait(pe, turned[n, 0], turned[n, 1])
        if n % 2 == 0:
            pe.wait_ge(acc_free[b].sem, q + 1)
        for k in range(4):
            m = pe.matmul(acc[b][r0:r0 + 64, 0:TOK], VV[:, k, n * 64:n * 64 + 64], PT[n % 2][:, k, :],
                          start=k == 0, stop=k == 3)
        if n % 2 == 0:
            return T.on(m)
        m.then_inc(tile_done.sem, 1)
        return (tile_done.sem, 4 * q + b + 1)

    def finish(n):
        pv_done[n] = values(n)
        if n % 2:
            b = n // 2
            complete(act, q, b)
            t = a(lambda: act.activation(MIXH[:, b, :], acc[b][:, 0:TOK], ACT.Copy))
            wait(dve, t)
            return freed(q, b, dve.tensor_tensor(MIXL[:, b, :], acc[b][:, 0:TOK],
                                                 MIXH[:, b, :].bitcast(F32), ALU.subtract))

    steps = group_norm()
    scores(0, 0)
    scores(0, 1)
    for n in range(NA_HEADS):
        for half in range(2):
            softmax(n, half)
            if n + 1 < NA_HEADS:
                scores(n + 1, half)
        next(steps, None)
        for half in range(2):
            normalize(n, half)
            turn(n, half)
        if n > 0:
            finish(n - 1)
    mix_ok = finish(NA_HEADS - 1)
    q += 1

    x_ok, squares = [], []
    SQ4 = at(rR.start, "SQ4", [KD, TOK])
    wait(pe, mix_ok)
    for n in range(2):
        pr, j = pair + 2 + (n + 1) // 2, (n + 1) % 2
        slab_ready(pr, j)
        for b in range(4):
            project(q, b, W8[j], b * P, (MIXH, MIXL), KD)
            complete(dve, q, b)
            k = 4 * n + b
            x_ok.append(freed(q, b, dve.scalar_tensor_tensor(out=XT[:, k, :], in0=acc[b][:, 0:TOK],
                                                        scalar=mod[:, 16 + k:17 + k], in1=XT[:, k, :],
                                                        op0=ALU.mult, op1=ALU.add)))
            squares.append(a(lambda: act.activation(SQ4[:, k, :], XT[:, k, :], ACT.Square, bias=0.0), x_ok[-1]))
        if n == 0:
            split(pair + 3, 1, 4 * q + 4)
            load(pair + 4, 0, up_slab(1))
        else:
            split(pair + 4, 0, 4 * q + 4)
            load(pair + 4, 1, up_slab(2))
        q += 1

    GP = at(rR.start + 16384, "GP", [2, TOK + 2])
    GC = at(rR.start + 20480, "GC", [2, TOK])
    rM.restart()
    MH = rM.new("MH_c", [KF, TOK], F32R)
    ML = rM.new("ML_c", [KF, TOK], F32R)
    gz = v(lambda: dve.memset(GP[:, :, :], 0.0))
    t = roots(None, SQ4, squares, 0, mix_ok)
    xn_ok = norm_in(XT, SQ4, XH, XL, lambda k: gain[:, 2, k:k + 1], lambda k: mod[:, 24 + k:25 + k], t)
    wait(act, gz)

    def up(pr, j, n, q, ready=None):
        slab_ready(pr, j)
        before_v, before_a = latest(V), latest(A)
        for b in range(4):
            project(q, b, W8[j], b * P, X, KD, ready if b == 0 else None)
        conv = []
        for f in range(2):
            complete(act, q, f)
            wait(act, before_v)
            conv.append(freed(q, f, act.activation(GP[:, f, 1:1 + TOK], acc[f][:, 0:TOK], ACT.Copy)))
        wait(dve, before_a)
        for tap in range(3):
            for f in range(2):
                k = 2 * n + f
                w = param("ffn_conv_w_2", KF * tap + k, 1)
                if tap == 0:
                    conv[f] = v(lambda: dve.tensor_scalar(GC[:, f, :], GP[:, f, 0:TOK], w,
                                                          param("ffn_conv_b_2", k, 1), ALU.mult, ALU.add), conv[f])
                else:
                    conv[f] = v(lambda: dve.scalar_tensor_tensor(out=GC[:, f, :], in0=GP[:, f, tap:tap + TOK],
                                                                 scalar=w, in1=GC[:, f, :], op0=ALU.mult,
                                                                 op1=ALU.add), conv[f])
        gated = []
        for f in range(2):
            conv[f] = a(lambda: act.activation(GC[:, f, :], GC[:, f, :], ACT.Silu, bias=0.0), conv[f])
        for f in range(2):
            wait(dve, conv[f])
            complete(dve, q, 2 + f)
            gated.append(freed(q, 2 + f, dve.tensor_tensor(GC[:, f, :], GC[:, f, :], acc[2 + f][:, 0:TOK],
                                                           ALU.mult)))
        split(pr + 1, j, 4 * q + 4)
        both = bass.ds(2 * n, 2)
        t = a(lambda: act.activation(MH[:, both, :], GC[:, :, :], ACT.Copy), *gated)
        v(lambda: dve.tensor_tensor(ML[:, both, :], GC[:, :, :], MH[:, both, :].bitcast(F32), ALU.subtract), t)

    up(pair + 3, 1, 0, q, xn_ok)
    pair, q = pair + 4, q + 1
    with loop(5, V=14, A=6) as i:
        for j in range(2):
            up(pair + i, j, 1 + 2 * i + j, q + 2 * i + j)
    for i in range(3, 11):
        pr, j = pair + (i - 1) // 2, (i - 1) % 2
        load(pr, j, up_slab(i))
    m_all, m_most = latest(V), (V.sem, latest(V)[1] - 7)
    wait(pe, m_most)
    pair, q = pair + 5, q + 10
    tiles = 4 * q

    def down(i, j, ahead):
        n = 2 * i + j
        load(pair + i, j, down_slab(n))
        slab_ready(pair + i, j)
        pe.wait_ge(acc_free[j].sem, q + i + 1)
        (wh, wl) = W22[j]
        o = acc[j][:, 0:TOK]
        for k in range(KF):
            if k == KF - 2:
                wait(pe, m_all)
            pe.matmul(o, wh[:, k, :], MH[:, k, :], start=k == 0, stop=False)
            pe.matmul(o, wh[:, k, :], ML[:, k, :], start=False, stop=False)
            m = pe.matmul(o, wl[:, k, :], MH[:, k, :], start=False, stop=k == KF - 1)
        m.then_inc(tile_done.sem, 1)
        dve.wait_ge(tile_done.sem, tiles + n + 1)
        x = XT[:, bass.ds(n, 1), :]
        freed(q, j, dve.scalar_tensor_tensor(out=x, in0=acc[j][:, 0:TOK], scalar=mod[:, bass.ds(40 + n, 1)],
                                             in1=x, op0=ALU.mult, op1=ALU.add))
        if ahead:
            split(pair + i + 1, j, tiles + n + 1, KF * P)

    with loop(3) as i:
        down(i, 0, True)
        down(i, 1, True)
    down(3, 0, False)
    down(3, 1, False)

    x_ok = [(acc_free[k % 2].sem, q + 2 + k // 2) for k in range(KD)]
    OT = at(rR.start + 24576, "OT", [2, D])
    t = roots(XT, SQ4, x_ok, 0, latest(V))
    xn_ok = normed(XT, SQ4, lambda k: param("final_norm_g_2", k), t)
    s_out = sig("out_stored")
    wait(pe, xn_ok[-1])
    for half in range(2):
        for kq in range(2):
            n = 2 * half + kq
            for k in range(4):
                m = pe.transpose(misc[n][:, k * P:k * P + P], SQ4[:, 4 * kq + k, half * P:half * P + P], ident[:, :])
            t = T.on(m)
            t = v(lambda: dve.tensor_copy(OT[:, half, kq * 512:kq * 512 + 512], misc[n][:, :]), t)
        wait(sp, t)
        sp.dma_start(out[0, half * P:half * P + P, :], OT[:, half, :]).then_inc(s_out.sem, 16)
    sp.wait_ge(s_out.sem, 32)


_INS = ["x", "norm_g", "pool_w_in", "pool_w_grp", "pool_scale", "pool_w_out", "hgrn_w_in",
        "hgrn_lower_bounds", "hgrn_norm_g", "hgrn_w_out", "final_g", "c_2", "ctx_2", "c_ctx_2",
        "ada_w_2", "ada_b_2", "norm1_g_2", "w_in_2", "na_rpb_2", "sg_norm_g_2", "sg_norm_b_2",
        "sg_w_2", "sg_b_2", "cv_w_2", "cv_b_2", "cv_norm_g_2", "cv_norm_b_2", "w_out_2",
        "norm2_g_2", "ffn_w_up_2", "ffn_conv_w_2", "ffn_conv_b_2", "ffn_w_down_2",
        "final_norm_g_2"]


def kernel(**inputs):
    import numpy as _np
    import concourse.bacc as _bacc
    from concourse.bass_utils import run_bass_kernel_spmd as _run

    nc = _bacc.Bacc("TRN2", target_bir_lowering=False, num_devices=1)
    arrays, args = {}, {}
    for name in _INS:
        a = _np.ascontiguousarray(inputs[name])
        arrays[f"in_{name}_dram"] = a
        args[name] = nc.dram_tensor(f"in_{name}_dram", a.shape, mybir.dt.from_np(a.dtype),
                                    kind="ExternalInput").ap()
    out = nc.dram_tensor("out_0_dram", (1, TOK, D), F32, kind="ExternalOutput").ap()
    build(nc, args, out)
    r = _run(nc, [arrays], core_ids=[0])
    return r.results[0]["out_0_dram"]
```
